# Optimizing a Trainium2 kernel written in Bass

```python
import jax, jax.numpy as jnp
from jax import lax
import numpy as np
import math

D_MODEL = 1024
BATCH = 1
SEQ = 1024
DEPTH = 1

GRID_W = 64
CTX_LEN = 256
HEAD_DIM = 64
A_HEADS = 8
A_KV_HEADS = 2
A_WINDOW = 128
A_BLOCK = 128
B_HEADS = 8
NA_MAX_KH = 8
NA_KW = 16
NA_ROW_BLOCK = 2
A_WIDTH = A_HEADS * HEAD_DIM
A_KV_WIDTH = A_KV_HEADS * HEAD_DIM
B_WIDTH = B_HEADS * HEAD_DIM
MIX_WIDTH = A_WIDTH + B_WIDTH
IN_COLS = A_WIDTH + 2 * A_KV_WIDTH + 3 * B_WIDTH
FFN_HIDDEN = -(-8 * D_MODEL // (3 * 256)) * 256
N_MOD = 6
ROPE_BASE = 10000.0
EPS = 1e-6


def _rms_norm(x, g):
    xf = x.astype(jnp.float32)
    y = xf * lax.rsqrt(jnp.mean(xf * xf, axis=-1, keepdims=True) + EPS)
    return (y * g.astype(jnp.float32)).astype(x.dtype)

def _modulate(h, shift, scale):
    return h * (1 + scale) + shift

def _axial_rope(x, rows, cols):
    half = HEAD_DIM // 2
    quarter = half // 2
    inv_freq = 1.0 / (ROPE_BASE ** (jnp.arange(quarter, dtype=jnp.float32) / quarter))

    def rot(xh, pos):
        ang = pos.astype(jnp.float32)[:, None] * inv_freq[None, :]
        cos = jnp.cos(ang)[None, :, None, :]
        sin = jnp.sin(ang)[None, :, None, :]
        x1 = xh[..., :quarter].astype(jnp.float32)
        x2 = xh[..., quarter:].astype(jnp.float32)
        return jnp.concatenate([x1 * cos - x2 * sin, x1 * sin + x2 * cos], axis=-1)

    out = jnp.concatenate([rot(x[..., :half], rows), rot(x[..., half:], cols)], axis=-1)
    return out.astype(x.dtype)

def _in_proj(h, w_in):
    B, L, _ = h.shape
    p = h @ w_in
    offs = np.cumsum([A_WIDTH, A_KV_WIDTH, A_KV_WIDTH, B_WIDTH, B_WIDTH])
    q_a, k_a, v_a, q_b, k_b, v_b = jnp.split(p, offs, axis=-1)
    hd = lambda t, n: t.reshape(B, L, n, HEAD_DIM)
    return (hd(q_a, A_HEADS), hd(k_a, A_KV_HEADS), hd(v_a, A_KV_HEADS),
            hd(q_b, B_HEADS), hd(k_b, B_HEADS), hd(v_b, B_HEADS))

def _band_mask(S):
    nb = S // A_BLOCK
    span = A_BLOCK + 2 * A_WINDOW
    qpos = np.arange(nb)[:, None, None] * A_BLOCK + np.arange(A_BLOCK)[None, :, None]
    kpos = np.arange(nb)[:, None, None] * A_BLOCK - A_WINDOW + np.arange(span)[None, None, :]
    return (np.abs(kpos - qpos) <= A_WINDOW) & (kpos >= 0) & (kpos < S)

def _window_gqa_latent(q, k, v, k_ctx, v_ctx, sink):
    B, S = q.shape[:2]
    nb = S // A_BLOCK
    G = A_HEADS // A_KV_HEADS
    n_side = A_WINDOW // A_BLOCK
    scale = HEAD_DIM ** -0.5
    pad = ((0, 0), (A_WINDOW, A_WINDOW), (0, 0), (0, 0))
    kp = jnp.pad(k, pad).reshape(B, nb + 2 * n_side, A_BLOCK, A_KV_HEADS, HEAD_DIM)
    vp = jnp.pad(v, pad).reshape(B, nb + 2 * n_side, A_BLOCK, A_KV_HEADS, HEAD_DIM)
    kb = jnp.concatenate([kp[:, o:o + nb] for o in range(2 * n_side + 1)], axis=2)
    vb = jnp.concatenate([vp[:, o:o + nb] for o in range(2 * n_side + 1)], axis=2)
    span = kb.shape[2]
    qb = q.reshape(B, nb, A_BLOCK, A_KV_HEADS, G, HEAD_DIM)
    mask = jnp.asarray(_band_mask(S))[:, None, None]
    s_loc = jnp.einsum('bnqkgd,bnjkd->bnkgqj', qb, kb).astype(jnp.float32) * scale
    s_loc = jnp.where(mask, s_loc, -jnp.inf)
    s_ctx = jnp.einsum('bnqkgd,bjkd->bnkgqj', qb, k_ctx).astype(jnp.float32) * scale
    sink_col = jnp.broadcast_to(sink.astype(jnp.float32).reshape(1, 1, A_KV_HEADS, G, 1, 1),
                                s_loc.shape[:-1] + (1,))
    p = jax.nn.softmax(jnp.concatenate([s_loc, s_ctx, sink_col], axis=-1), axis=-1)
    L = k_ctx.shape[1]
    p_loc = p[..., :span].astype(v.dtype)
    p_ctx = p[..., span:span + L].astype(v.dtype)
    o = (jnp.einsum('bnkgqj,bnjkd->bnqkgd', p_loc, vb)
         + jnp.einsum('bnkgqj,bjkd->bnqkgd', p_ctx, v_ctx))
    return o.reshape(B, S, A_WIDTH)

def _na_pattern(rows):
    kh = min(NA_MAX_KH, rows)
    n_blk = rows // NA_ROW_BLOCK
    n_kr = min(NA_ROW_BLOCK + kh - 1, rows)
    r0 = np.arange(n_blk) * NA_ROW_BLOCK
    row_start = lambda r: np.clip(r - kh // 2, 0, rows - kh)
    k_start = np.minimum(row_start(r0), rows - n_kr)
    key_rows = k_start[:, None] + np.arange(n_kr)[None, :]
    qi = np.arange(NA_ROW_BLOCK * GRID_W)
    q_r = r0[:, None] + qi[None, :] // GRID_W
    q_c = qi % GRID_W
    kj = np.arange(n_kr * GRID_W)
    k_r = key_rows[:, kj // GRID_W]
    k_c = kj % GRID_W
    rs = row_start(q_r)
    cs = np.clip(q_c - NA_KW // 2, 0, GRID_W - NA_KW)
    row_ok = (k_r[:, None, :] >= rs[:, :, None]) & (k_r[:, None, :] < rs[:, :, None] + kh)
    col_ok = (k_c[None, :] >= cs[:, None]) & (k_c[None, :] < cs[:, None] + NA_KW)
    mask = row_ok & col_ok[None]
    dr = np.clip(k_r[:, None, :] - q_r[:, :, None] + NA_MAX_KH - 1, 0, 2 * NA_MAX_KH - 2)
    dc = np.broadcast_to(np.clip(k_c[None, :] - q_c[:, None] + NA_KW - 1, 0, 2 * NA_KW - 2)[None],
                         mask.shape)
    return key_rows, mask, dr, dc

def _neighbourhood_latent(q, k, v, k_ctx, v_ctx, rpb):
    B, S = q.shape[:2]
    rows = S // GRID_W
    key_rows, mask, dr, dc = _na_pattern(rows)
    n_blk, n_kr = key_rows.shape
    scale = HEAD_DIM ** -0.5
    idx = jnp.asarray(key_rows)
    kg = k.reshape(B, rows, GRID_W, B_HEADS, HEAD_DIM)[:, idx].reshape(
        B, n_blk, n_kr * GRID_W, B_HEADS, HEAD_DIM)
    vg = v.reshape(B, rows, GRID_W, B_HEADS, HEAD_DIM)[:, idx].reshape(
        B, n_blk, n_kr * GRID_W, B_HEADS, HEAD_DIM)
    qb = q.reshape(B, n_blk, NA_ROW_BLOCK * GRID_W, B_HEADS, HEAD_DIM)
    bias = jnp.transpose(rpb[:, jnp.asarray(dr), jnp.asarray(dc)], (1, 0, 2, 3)).astype(jnp.float32)
    s_loc = jnp.einsum('bnqhd,bnjhd->bnhqj', qb, kg).astype(jnp.float32) * scale + bias
    s_loc = jnp.where(jnp.asarray(mask)[:, None], s_loc, -jnp.inf)
    s_ctx = jnp.einsum('bnqhd,bjhd->bnhqj', qb, k_ctx).astype(jnp.float32) * scale
    p = jax.nn.softmax(jnp.concatenate([s_loc, s_ctx], axis=-1), axis=-1)
    kb_len = kg.shape[2]
    p_loc = p[..., :kb_len].astype(v.dtype)
    p_ctx = p[..., kb_len:].astype(v.dtype)
    o = (jnp.einsum('bnhqj,bnjhd->bnqhd', p_loc, vg)
         + jnp.einsum('bnhqj,bjhd->bnqhd', p_ctx, v_ctx))
    return o.reshape(B, S, B_WIDTH)

def _ctx_self_attention(q, k, v, n_kv, sink=None):
    B, L, H, _ = q.shape
    G = H // n_kv
    qg = q.reshape(B, L, n_kv, G, HEAD_DIM)
    s = jnp.einsum('blkgd,bjkd->bkglj', qg, k).astype(jnp.float32) * HEAD_DIM ** -0.5
    if sink is not None:
        sink_col = jnp.broadcast_to(sink.astype(jnp.float32).reshape(1, n_kv, G, 1, 1), s.shape[:-1] + (1,))
        s = jnp.concatenate([s, sink_col], axis=-1)
    p = jax.nn.softmax(s, axis=-1)[..., :L].astype(v.dtype)
    o = jnp.einsum('bkglj,bjkd->blkgd', p, v)
    return o.reshape(B, L, H * HEAD_DIM)

def _merge(o_a, o_b, g_a, g_b, w_out):
    return jnp.concatenate([_rms_norm(o_a, g_a), _rms_norm(o_b, g_b)], axis=-1) @ w_out

def _swiglu(h, w_gate, w_up, w_down):
    return (jax.nn.silu(h @ w_gate) * (h @ w_up)) @ w_down

def first_inputs(seed: int = 0) -> dict:
    key = jax.random.key(seed)
    ks = jax.random.split(key, 24)
    nrm = lambda k, shape: jax.random.normal(k, shape, dtype=jnp.float32)
    gain = lambda k, shape: 1.0 + 0.05 * nrm(k, shape)
    D = D_MODEL
    return {
        "x": nrm(ks[0], (BATCH, SEQ, D)),
        "c": nrm(ks[1], (BATCH, D)),
        "ctx": nrm(ks[2], (BATCH, CTX_LEN, D)),
        "c_ctx": nrm(ks[3], (D,)),
        "w_mod": nrm(ks[4], (DEPTH, D, N_MOD * D)) * (0.5 * D ** -0.5),
        "b_mod": 0.01 * nrm(ks[5], (DEPTH, N_MOD * D)),
        "norm1_g": gain(ks[6], (DEPTH, D)),
        "w_in": nrm(ks[7], (DEPTH, D, IN_COLS)) * D ** -0.5,
        "qn_a": gain(ks[8], (DEPTH, HEAD_DIM)),
        "kn_a": gain(ks[9], (DEPTH, HEAD_DIM)),
        "sink_a": 0.5 * nrm(ks[10], (DEPTH, A_HEADS)),
        "qn_b": gain(ks[11], (DEPTH, HEAD_DIM)),
        "kn_b": gain(ks[12], (DEPTH, HEAD_DIM)),
        "rpb_b": 0.1 * nrm(ks[13], (DEPTH, B_HEADS, 2 * NA_MAX_KH - 1, 2 * NA_KW - 1)),
        "on_a": gain(ks[14], (DEPTH, A_WIDTH)),
        "on_b": gain(ks[15], (DEPTH, B_WIDTH)),
        "w_out": nrm(ks[16], (DEPTH, MIX_WIDTH, D)) * MIX_WIDTH ** -0.5,
        "norm2_g": gain(ks[17], (DEPTH, D)),
        "w_gate": nrm(ks[18], (DEPTH, D, FFN_HIDDEN)) * D ** -0.5,
        "w_up": nrm(ks[19], (DEPTH, D, FFN_HIDDEN)) * D ** -0.5,
        "w_down": nrm(ks[20], (DEPTH, FFN_HIDDEN, D)) * FFN_HIDDEN ** -0.5,
    }

def first_block(x, c, ctx, c_ctx, w_mod, b_mod, norm1_g, w_in, qn_a, kn_a, sink_a, qn_b, kn_b,
              rpb_b, on_a, on_b, w_out, norm2_g, w_gate, w_up, w_down):
    S = x.shape[1]
    t = jnp.arange(S)
    row_pos = t // GRID_W
    col_pos = t % GRID_W
    for l in range(DEPTH):
        mod = (jax.nn.silu(c) @ w_mod[l] + b_mod[l])[:, None, :]
        mod_c = (jax.nn.silu(c_ctx) @ w_mod[l] + b_mod[l])[None, None, :]
        sh1, sc1, g1, sh2, sc2, g2 = jnp.split(mod, N_MOD, axis=-1)
        csh1, csc1, cg1, csh2, csc2, cg2 = jnp.split(mod_c, N_MOD, axis=-1)

        h = _modulate(_rms_norm(x, norm1_g[l]), sh1, sc1)
        hc = _modulate(_rms_norm(ctx, norm1_g[l]), csh1, csc1)
        q_a, k_a, v_a, q_b, k_b, v_b = _in_proj(h, w_in[l])
        q_ac, k_ac, v_ac, q_bc, k_bc, v_bc = _in_proj(hc, w_in[l])

        q_a = _axial_rope(_rms_norm(q_a, qn_a[l]), row_pos, col_pos)
        k_a = _axial_rope(_rms_norm(k_a, kn_a[l]), row_pos, col_pos)
        q_ac, k_ac = _rms_norm(q_ac, qn_a[l]), _rms_norm(k_ac, kn_a[l])
        q_b, k_b = _rms_norm(q_b, qn_b[l]), _rms_norm(k_b, kn_b[l])
        q_bc, k_bc = _rms_norm(q_bc, qn_b[l]), _rms_norm(k_bc, kn_b[l])

        o_a = _window_gqa_latent(q_a, k_a, v_a, k_ac, v_ac, sink_a[l])
        o_b = _neighbourhood_latent(q_b, k_b, v_b, k_bc, v_bc, rpb_b[l])
        x_new = x + g1 * _merge(o_a, o_b, on_a[l], on_b[l], w_out[l])
        h2 = _modulate(_rms_norm(x_new, norm2_g[l]), sh2, sc2)
        x_new = x_new + g2 * _swiglu(h2, w_gate[l], w_up[l], w_down[l])

        if l < DEPTH - 1:
            o_ac = _ctx_self_attention(q_ac, k_ac, v_ac, A_KV_HEADS, sink_a[l])
            o_bc = _ctx_self_attention(q_bc, k_bc, v_bc, B_HEADS)
            ctx = ctx + cg1 * _merge(o_ac, o_bc, on_a[l], on_b[l], w_out[l])
            hc2 = _modulate(_rms_norm(ctx, norm2_g[l]), csh2, csc2)
            ctx = ctx + cg2 * _swiglu(hc2, w_gate[l], w_up[l], w_down[l])
        x = x_new
    return x


CHUNK = 64
N_MIXERS = 4
GLA_HEADS = 4
GLA_DK = (D_MODEL // 2) // GLA_HEADS
GLA_DV = D_MODEL // GLA_HEADS
GLA_GATE_RANK = 16
GLA_TAU = 16.0
GLA_IN = 2 * GLA_HEADS * GLA_DK + 2 * GLA_HEADS * GLA_DV + GLA_GATE_RANK
POOL_WINDOWS = (2, 4, 8, 16)
POOL_GROUPS = len(POOL_WINDOWS)
POOL_GW = D_MODEL // POOL_GROUPS
SSD_DINNER = 2 * D_MODEL
SSD_HEADDIM = 64
SSD_HEADS = SSD_DINNER // SSD_HEADDIM
SSD_GROUPS = 4
SSD_HPG = SSD_HEADS // SSD_GROUPS
SSD_STATE = 128
SSD_CONV = 4
SSD_CONV_DIM = SSD_DINNER + 2 * SSD_GROUPS * SSD_STATE
SSD_IN = SSD_DINNER + SSD_CONV_DIM + SSD_HEADS
SB_HEADS = 16
SB_HEADDIM = D_MODEL // SB_HEADS
SB_QBLOCK = 128
FFN_DIM = 2816
FFN_CONV = 3


def rms_normalize(x):
    xf = x.astype(jnp.float32)
    y = xf * lax.rsqrt(jnp.mean(xf * xf, axis=-1, keepdims=True) + EPS)
    return y.astype(x.dtype)

def rmsnorm(x, w):
    return rms_normalize(x) * w

def causal_dwconv(u, w, b):
    K = w.shape[0]
    L = u.shape[1]
    up = jnp.pad(u, ((0, 0), (K - 1, 0), (0, 0)))
    out = up[:, K - 1:K - 1 + L] * w[K - 1] + b
    for k in range(K - 1):
        out = out + up[:, k:k + L] * w[k]
    return out

def to_chunks(a):
    b_, l_ = a.shape[:2]
    return jnp.moveaxis(a.reshape(b_, l_ // CHUNK, CHUNK, *a.shape[2:]), 1, 0)

def from_chunks(a):
    a = jnp.moveaxis(a, 0, 1)
    return a.reshape(a.shape[0], a.shape[1] * a.shape[2], *a.shape[3:])

def gla_mixer(h, w_in, w_gate2, b_gate, norm_w, w_out):
    b_, l_, _ = h.shape
    hk, hv = GLA_HEADS * GLA_DK, GLA_HEADS * GLA_DV
    proj = h @ w_in
    q, k, v, r, glr = jnp.split(proj, [hk, 2 * hk, 2 * hk + hv, 2 * hk + 2 * hv], axis=-1)
    q = q.reshape(b_, l_, GLA_HEADS, GLA_DK).astype(jnp.float32) * (GLA_DK ** -0.5)
    k = k.reshape(b_, l_, GLA_HEADS, GLA_DK).astype(jnp.float32)
    v = v.reshape(b_, l_, GLA_HEADS, GLA_DV).astype(jnp.float32)
    log_a = jax.nn.log_sigmoid((glr @ w_gate2 + b_gate).astype(jnp.float32)) / GLA_TAU
    log_a = log_a.reshape(b_, l_, GLA_HEADS, GLA_DK)
    qc, kc, vc, lac = to_chunks(q), to_chunks(k), to_chunks(v), to_chunks(log_a)
    g = jnp.cumsum(lac, axis=2)
    g_end = g[:, :, -1]
    k_dec = kc * jnp.exp(g_end[:, :, None] - g)

    def body(state, inp):
        q_c, kd_c, v_c, ge_c = inp
        state = state * jnp.exp(ge_c)[..., None] + jnp.einsum('bshk,bshv->bhkv', kd_c, v_c)
        o = jnp.einsum('bqhk,bhkv->bqhv', q_c, state)
        return state, o

    s0 = jnp.zeros((b_, GLA_HEADS, GLA_DK, GLA_DV), jnp.float32)
    _, o = lax.scan(body, s0, (qc, k_dec, vc, g_end))
    o = rms_normalize(from_chunks(o)).reshape(b_, l_, hv) * norm_w
    o = o.astype(h.dtype) * jax.nn.silu(r)
    return o @ w_out

def pool_mixer(h, w_grp, b_grp, scale):
    b_, l_, d_ = h.shape
    hf = h.astype(jnp.float32)
    cs = jnp.concatenate([jnp.zeros((b_, 1, d_), jnp.float32), jnp.cumsum(hf, axis=1)], axis=1)
    t1 = jnp.arange(1, l_ + 1, dtype=jnp.float32)
    outs = []
    for gi, win in enumerate(POOL_WINDOWS):
        sl = slice(gi * POOL_GW, (gi + 1) * POOL_GW)
        c = cs[..., sl]
        lower = jnp.concatenate([jnp.zeros((b_, win - 1, POOL_GW), jnp.float32), c[:, :l_ + 1 - win]], axis=1)
        mean = (c[:, 1:] - lower) / jnp.minimum(t1, float(win))[None, :, None]
        dlt = (mean - hf[..., sl]).astype(h.dtype)
        outs.append(dlt @ w_grp[gi] + b_grp[gi])
    return jnp.concatenate(outs, axis=-1) * scale

def ssd_mixer(h, w_in, conv_w, conv_b, dt_bias, a_log, d_skip, norm_w, w_out):
    b_, l_, _ = h.shape
    G, HG, P, N = SSD_GROUPS, SSD_HPG, SSD_HEADDIM, SSD_STATE
    proj = h @ w_in
    z, xbc, dt = jnp.split(proj, [SSD_DINNER, SSD_DINNER + SSD_CONV_DIM], axis=-1)
    xbc = jax.nn.silu(causal_dwconv(xbc, conv_w, conv_b))
    xs, bm, cm = jnp.split(xbc, [SSD_DINNER, SSD_DINNER + G * N], axis=-1)
    xs = xs.reshape(b_, l_, G, HG, P)
    bm = bm.reshape(b_, l_, G, N)
    cm = cm.reshape(b_, l_, G, N)
    dt = jax.nn.softplus((dt + dt_bias).astype(jnp.float32)).reshape(b_, l_, G, HG)
    a_h = -jnp.exp(a_log.astype(jnp.float32)).reshape(G, HG)
    causal = jnp.tril(jnp.ones((CHUNK, CHUNK), bool))

    def body(state, inp):
        x_c, b_c, c_c, dt_c = inp
        acs = jnp.cumsum(dt_c * a_h, axis=1)
        seg = acs[:, :, None] - acs[:, None, :]
        lmat = jnp.exp(jnp.where(causal[None, :, :, None, None], seg, -jnp.inf))
        xdt = x_c * dt_c[..., None]
        cb = jnp.einsum('btgn,bsgn->btsg', c_c, b_c)
        y = jnp.einsum('btsg,btsgh,bsghp->btghp', cb, lmat, xdt)
        y = y + jnp.einsum('btgn,bghpn,btgh->btghp', c_c, state, jnp.exp(acs))
        decay_end = jnp.exp(acs[:, -1:] - acs)
        state = state * jnp.exp(acs[:, -1])[..., None, None] + jnp.einsum('bsgn,bsgh,bsghp->bghpn', b_c, decay_end, xdt)
        return state, y

    s0 = jnp.zeros((b_, G, HG, P, N), jnp.float32)
    _, ys = lax.scan(body, s0, (to_chunks(xs), to_chunks(bm), to_chunks(cm), to_chunks(dt)))
    y = from_chunks(ys) + d_skip.reshape(G, HG)[..., None] * xs
    y = y.reshape(b_, l_, SSD_DINNER) * jax.nn.silu(z)
    y = rms_normalize(y.reshape(b_, l_, G, SSD_DINNER // G)).reshape(b_, l_, SSD_DINNER) * norm_w
    return y.astype(h.dtype) @ w_out

def sb_mixer(h, w_qkv, w_out):
    b_, l_, _ = h.shape
    q, k, v = jnp.split(h @ w_qkv, 3, axis=-1)
    q = q.reshape(b_, l_, SB_HEADS, SB_HEADDIM).transpose(0, 2, 1, 3) * (SB_HEADDIM ** -0.5)
    k = k.reshape(b_, l_, SB_HEADS, SB_HEADDIM).transpose(0, 2, 1, 3)
    v = v.reshape(b_, l_, SB_HEADS, SB_HEADDIM).transpose(0, 2, 1, 3)
    nb = l_ // SB_QBLOCK
    qb = jnp.moveaxis(q.reshape(b_, SB_HEADS, nb, SB_QBLOCK, SB_HEADDIM), 2, 0)
    starts = jnp.arange(nb, dtype=jnp.int32) * SB_QBLOCK
    key_pos = jnp.arange(l_, dtype=jnp.int32)

    def block(inp):
        q_i, start = inp
        zt = jnp.einsum('bhqd,bhkd->bhqk', q_i, k).astype(jnp.float32)
        qpos = start + jnp.arange(SB_QBLOCK, dtype=jnp.int32)
        mask = key_pos[None, :] < qpos[:, None]
        log_1mb = jnp.where(mask, jax.nn.log_sigmoid(-zt), 0.0)
        rc = lax.cumsum(log_1mb, axis=3, reverse=True)
        surv = jnp.concatenate([rc[..., 1:], jnp.zeros_like(rc[..., :1])], axis=-1)
        att = jnp.where(mask, jnp.exp(jax.nn.log_sigmoid(zt) + surv), 0.0)
        return jnp.einsum('bhqk,bhkd->bhqd', att.astype(v.dtype), v)

    o = lax.map(block, (qb, starts))
    o = jnp.moveaxis(o, 0, 2).reshape(b_, SB_HEADS, l_, SB_HEADDIM)
    o = o.transpose(0, 2, 1, 3).reshape(b_, l_, D_MODEL)
    return o @ w_out

def conv_ffn(h, w_up, conv_w, conv_b, w_down):
    u = causal_dwconv(h @ w_up, conv_w, conv_b)
    g, val = jnp.split(u, 2, axis=-1)
    return (jax.nn.silu(g) * val) @ w_down

def second_inputs(seed: int = 0) -> dict:
    key = jax.random.key(seed)
    ks = list(jax.random.split(key, 40))
    f32 = jnp.float32

    def nrm(i, shape, scale):
        return jax.random.normal(ks[i], shape, f32) * scale

    n_a = len(range(0, DEPTH, N_MIXERS))
    n_b = len(range(1, DEPTH, N_MIXERS))
    n_c = len(range(2, DEPTH, N_MIXERS))
    n_d = len(range(3, DEPTH, N_MIXERS))
    dt0 = jnp.exp(jax.random.uniform(ks[20], (n_c, SSD_HEADS), f32) * (math.log(0.1) - math.log(0.001)) + math.log(0.001))
    return {
        'x': nrm(0, (BATCH, SEQ, D_MODEL), 1.0),
        'mix_norm_w': 1.0 + nrm(1, (DEPTH, D_MODEL), 0.02),
        'ffn_norm_w': 1.0 + nrm(2, (DEPTH, D_MODEL), 0.02),
        'final_norm_w': 1.0 + nrm(3, (D_MODEL,), 0.02),
        'gla_w_in': nrm(4, (n_a, D_MODEL, GLA_IN), D_MODEL ** -0.5),
        'gla_w_gate2': nrm(5, (n_a, GLA_GATE_RANK, GLA_HEADS * GLA_DK), GLA_GATE_RANK ** -0.5),
        'gla_b_gate': nrm(6, (n_a, GLA_HEADS * GLA_DK), 0.1),
        'gla_norm_w': 1.0 + nrm(7, (n_a, GLA_HEADS * GLA_DV), 0.02),
        'gla_w_out': nrm(8, (n_a, GLA_HEADS * GLA_DV, D_MODEL), (GLA_HEADS * GLA_DV) ** -0.5),
        'pool_w': nrm(9, (n_b, POOL_GROUPS, POOL_GW, POOL_GW), POOL_GW ** -0.5),
        'pool_b': nrm(10, (n_b, POOL_GROUPS, POOL_GW), 0.02),
        'pool_scale': 1.0 + nrm(11, (n_b, D_MODEL), 0.02),
        'ssd_w_in': nrm(12, (n_c, D_MODEL, SSD_IN), D_MODEL ** -0.5),
        'ssd_conv_w': nrm(13, (n_c, SSD_CONV, SSD_CONV_DIM), SSD_CONV ** -0.5),
        'ssd_conv_b': nrm(14, (n_c, SSD_CONV_DIM), 0.02),
        'ssd_dt_bias': dt0 + jnp.log(-jnp.expm1(-dt0)),
        'ssd_a_log': jnp.log(jax.random.uniform(ks[15], (n_c, SSD_HEADS), f32, 1.0, 16.0)),
        'ssd_d': 1.0 + nrm(16, (n_c, SSD_HEADS), 0.02),
        'ssd_norm_w': 1.0 + nrm(17, (n_c, SSD_DINNER), 0.02),
        'ssd_w_out': nrm(18, (n_c, SSD_DINNER, D_MODEL), SSD_DINNER ** -0.5),
        'sb_w_qkv': nrm(19, (n_d, D_MODEL, 3 * D_MODEL), D_MODEL ** -0.5),
        'sb_w_out': nrm(21, (n_d, D_MODEL, D_MODEL), D_MODEL ** -0.5),
        'ffn_w_up': nrm(22, (DEPTH, D_MODEL, 2 * FFN_DIM), D_MODEL ** -0.5),
        'ffn_conv_w': nrm(23, (DEPTH, FFN_CONV, 2 * FFN_DIM), FFN_CONV ** -0.5),
        'ffn_conv_b': nrm(24, (DEPTH, 2 * FFN_DIM), 0.02),
        'ffn_w_down': nrm(25, (DEPTH, FFN_DIM, D_MODEL), FFN_DIM ** -0.5),
    }

def second_block(x, mix_norm_w, ffn_norm_w, final_norm_w,
              gla_w_in, gla_w_gate2, gla_b_gate, gla_norm_w, gla_w_out,
              pool_w, pool_b, pool_scale,
              ssd_w_in, ssd_conv_w, ssd_conv_b, ssd_dt_bias, ssd_a_log, ssd_d, ssd_norm_w, ssd_w_out,
              sb_w_qkv, sb_w_out,
              ffn_w_up, ffn_conv_w, ffn_conv_b, ffn_w_down):
    for i in range(DEPTH):
        m, j = i % N_MIXERS, i // N_MIXERS
        h = rmsnorm(x, mix_norm_w[i])
        if m == 0:
            y = gla_mixer(h, gla_w_in[j], gla_w_gate2[j], gla_b_gate[j], gla_norm_w[j], gla_w_out[j])
        elif m == 1:
            y = pool_mixer(h, pool_w[j], pool_b[j], pool_scale[j])
        elif m == 2:
            y = ssd_mixer(h, ssd_w_in[j], ssd_conv_w[j], ssd_conv_b[j], ssd_dt_bias[j], ssd_a_log[j],
                          ssd_d[j], ssd_norm_w[j], ssd_w_out[j])
        else:
            y = sb_mixer(h, sb_w_qkv[j], sb_w_out[j])
        x = x + y.astype(x.dtype)
        h = rmsnorm(x, ffn_norm_w[i])
        x = x + conv_ffn(h, ffn_w_up[i], ffn_conv_w[i], ffn_conv_b[i], ffn_w_down[i]).astype(x.dtype)
    return rmsnorm(x, final_norm_w)


def setup_inputs(seed=0):
    out = dict(first_inputs(seed))
    for name, value in second_inputs(seed + 1).items():
        if name != "x":
            out[name + "_2"] = value
    return out


def reference(
    x, c, ctx, c_ctx, w_mod, b_mod, norm1_g, w_in, qn_a, kn_a, sink_a, qn_b, kn_b, rpb_b, on_a,
    on_b, w_out, norm2_g, w_gate, w_up, w_down, mix_norm_w_2, ffn_norm_w_2, final_norm_w_2,
    gla_w_in_2, gla_w_gate2_2, gla_b_gate_2, gla_norm_w_2, gla_w_out_2, pool_w_2, pool_b_2,
    pool_scale_2, ssd_w_in_2, ssd_conv_w_2, ssd_conv_b_2, ssd_dt_bias_2, ssd_a_log_2, ssd_d_2,
    ssd_norm_w_2, ssd_w_out_2, sb_w_qkv_2, sb_w_out_2, ffn_w_up_2, ffn_conv_w_2, ffn_conv_b_2,
    ffn_w_down_2,
):
    x = first_block(
        x, c, ctx, c_ctx, w_mod, b_mod, norm1_g, w_in, qn_a, kn_a, sink_a, qn_b, kn_b, rpb_b,
        on_a, on_b, w_out, norm2_g, w_gate, w_up, w_down,
    )
    return second_block(
        x, mix_norm_w_2, ffn_norm_w_2, final_norm_w_2, gla_w_in_2, gla_w_gate2_2, gla_b_gate_2,
        gla_norm_w_2, gla_w_out_2, pool_w_2, pool_b_2, pool_scale_2, ssd_w_in_2, ssd_conv_w_2,
        ssd_conv_b_2, ssd_dt_bias_2, ssd_a_log_2, ssd_d_2, ssd_norm_w_2, ssd_w_out_2,
        sb_w_qkv_2, sb_w_out_2, ffn_w_up_2, ffn_conv_w_2, ffn_conv_b_2, ffn_w_down_2,
    )


_drawn_inputs = setup_inputs


def setup_inputs(seed=0):
    import zlib

    import numpy as np

    out = dict(_drawn_inputs(seed))
    spreads = {}
    factors = {'norm1_g': 3.813,
     'qn_a': 8.0,
     'kn_a': 8.0,
     'sink_a': 8.0,
     'qn_b': 8.0,
     'kn_b': 8.0,
     'rpb_b': 8.0,
     'on_a': 3.027,
     'on_b': 3.03,
     'ffn_norm_w_2': 4.519,
     'final_norm_w_2': 2.851,
     'gla_norm_w_2': 5.305,
     'ffn_conv_b_2': 4.504}
    for name, (base, spread) in spreads.items():
        noise = np.random.default_rng([zlib.crc32(name.encode()), seed]).standard_normal(out[name].shape)
        drawn = base * np.exp(spread * noise) if base else spread * noise
        out[name] = __import__('jax').numpy.asarray(drawn.astype(out[name].dtype))
    for name, factor in factors.items():
        out[name] = (out[name] * factor).astype(out[name].dtype)
    return out
```

```python
from contextlib import ExitStack

import numpy as np

import concourse.bass as bass
from concourse import mybir

F = mybir.dt.float32
R = mybir.dt.float32r
BF = mybir.dt.bfloat16
ALU = mybir.AluOpType
ACT = mybir.ActivationFunctionType
AX = mybir.AxisListType.X
KB = 1024
BIG = 1.0e30

C_ID, C_ONE, C_BLK, C_PERM, C_SUF, C_DV, C_ML, C_MR = [128 * i for i in range(8)]
C_IND = 1024
C_EPS = 1026
C_N = 1032
V_BMOD, V_N1, V_QA, V_KA, V_QB, V_KB, V_ONA, V_ONB = 0, 48, 56, 57, 58, 59, 60, 64
V_N2, V_MIX, V_FFN, V_FIN, V_GLN, V_CW, V_CB = 68, 76, 84, 92, 100, 108, 240
V_N = 288
M_MOD, M_CMOD, M_G1, M_GC, M_QA, M_QB, M_G2, M_RAW = 0, 48, 64, 72, 80, 81, 82, 96
M_N = 144

DNG = [5, 5, 4, 4, 4]
NH = 22


def slab_plan():
    plan = [("mod", m) for m in range(16)]
    plan += [("in", m) for m in range(18)]
    plan += [("out", m) for m in range(8)]

    def ffn(gu, dn):
        out, h = [], 0
        order = ffn_order()
        for kind, a in order:
            if kind == "gu":
                out += [(gu + "g", a), (gu + "u", a)]
            else:
                out += [(dn, a * 8 + m) for m in range(8)]
        return out

    plan += ffn("f1", "d1")
    plan += [("gl", 0)] + [("gk", m) for m in range(4)] + [("gv", m) for m in range(8)]
    plan += [("gq", m) for m in range(4)] + [("gr", m) for m in range(8)]
    plan += [("go", m) for m in range(8)]
    plan += ffn("f2", "d2")
    return plan


def ffn_order():
    order, done, start = [], 0, 0
    for g, n in enumerate(DNG):
        while done < min(start + n + 1, NH):
            order.append(("gu", done))
            done += 1
        order.append(("dn", g))
        start += n
    return order


def activation(*a, **k):
    return lambda e: e.activation(*a, **k)

def matmul(*a, **k):
    return lambda e: e.matmul(*a, **k)

def memset(*a, **k):
    return lambda e: e.memset(*a, **k)

def reciprocal(*a, **k):
    return lambda e: e.reciprocal(*a, **k)

def scalar_tensor_tensor(*a, **k):
    return lambda e: e.scalar_tensor_tensor(*a, **k)

def tensor_copy(*a, **k):
    return lambda e: e.tensor_copy(*a, **k)

def tensor_reduce(*a, **k):
    return lambda e: e.tensor_reduce(*a, **k)

def tensor_scalar(*a, **k):
    return lambda e: e.tensor_scalar(*a, **k)

def tensor_tensor(*a, **k):
    return lambda e: e.tensor_tensor(*a, **k)

def tensor_tensor_reduce(*a, **k):
    return lambda e: e.tensor_tensor_reduce(*a, **k)

def transpose(*a, **k):
    return lambda e: e.transpose(*a, **k)


def build(nc, T, out):
    B0 = 16512
    names = {}

    def at(name, off, shape, dt):
        return nc.alloc_sbuf_tensor_at(name, shape, dt, offset=off)

    o = B0
    cst = at("cst", o, [128, C_N], F); o += C_N * 4
    vec = at("vec", o, [128, V_N], F); o += V_N * 4
    mv = at("mv", o, [128, M_N], F); o += M_N * 4
    idb = at("idb", o, [128, 128], BF); o += 256
    mlb = at("mlb", o, [128, 128], BF); o += 256
    mrb = at("mrb", o, [128, 128], BF); o += 256
    snk = at("snk", o, [128, 16], F); o += 64
    csl = at("csl", o, [128, 16], F); o += 64
    nmx = at("nmx", o, [128, 32], F); o += 128
    den = at("den", o, [128, 32], F); o += 128
    rdn = at("rdn", o, [128, 32], F); o += 128
    oss = at("oss", o, [128, 16], F); o += 64
    ors = at("ors", o, [128, 16], F); o += 64
    ege = at("ege", o, [128, 4, 16], F); o += 256
    one1 = at("one1", o, [128, 128], F); o += 512
    o = (o + 31) // 32 * 32
    raw = at("raw", o, [128, 3, 1024], F); o += 12 * KB
    wh = at("wh", o, [128, 2, 8, 128], R); o += 8 * KB
    wl = at("wl", o, [128, 2, 8, 128], R); o += 8 * KB
    AH = o
    hh = at("hh", o, [128, 8, 1024], R); o += 32 * KB
    hl = at("hl", o, [128, 8, 1024], R); o += 32 * KB
    U = o

    with ExitStack() as ctx:
        sem = lambda n: ctx.enter_context(nc.semaphore(n))
        S = [ctx.enter_context(nc.psum_tensor(f"S{i}", [128, 1024], F)) for i in range(3)]
        M = [ctx.enter_context(nc.psum_tensor(f"M{i}", [128, 512], F)) for i in range(2)]

        class Queue:

            def __init__(self, name):
                self.name, self.sem, self.n, self.items, self.seen = name, sem("s_" + name), 0, [], {}

            def wait(self, *toks):
                for s, v in toks:
                    if self.seen.get(s.name, 0) < v:
                        self.seen[s.name] = v
                        self.items.append(lambda e, s=s, v=v: e.wait_ge(s, v))

            def run(self, f, *toks):
                self.wait(*toks)
                self.items.append(f)

            def op(self, f, *toks):
                self.wait(*toks)
                self.n += 1
                self.items.append(lambda e: f(e).then_inc(self.sem, 1))
                return (self.sem, self.n)

        pe, act, dve, pool, sp = (Queue(n) for n in ("pe", "act", "dve", "pool", "sp"))

        def load(s, n, dst, src, *toks):
            sp.run(lambda e: e.dma_start(dst, src).then_inc(s, 16), *toks)
            return (s, 16 * n)

        class Ring:

            def __init__(self, n):
                self.n, self.i, self.readers = n, 0, [()] * n

            def take(self):
                k = self.i % self.n
                self.i += 1
                return k, self.readers[k]

        slots = Ring(3)
        mslot = Ring(2)

        plan = slab_plan()
        s_raw = [sem(f"s_raw{i}") for i in range(3)]
        raw_free, w_free = {}, {}
        loaded, split = {}, {}
        cur = {"load": 0, "split": 0, "w": 0}
        extra = []

        def src_of(kind, m):
            if kind == "raw":
                return T["w_modT"][m], 1024
            if kind == "mod":
                return T["w_mod0"][m], 1024
            if kind in ("d1", "d2"):
                g = m // 8
                k0, k = sum(DNG[:g]), DNG[g]
                return T["w_" + kind][m % 8][:, 128 * k0:128 * (k0 + k)], 128 * k
            return T["w_" + kind][m], 1024

        def load_slab():
            i = cur["load"]
            if i >= len(plan):
                return
            cur["load"] += 1
            src, n = src_of(*plan[i])
            j = i % 3
            loaded[i] = load(s_raw[j], i // 3 + 1, raw[:, j, 0:n], src, *(raw_free[i - 3] if i >= 3 else ()))

        def split_slab():
            i = cur["split"]
            if i >= len(plan):
                return
            cur["split"] += 1
            if plan[i][0] in ("mod", "raw"):
                return
            n, j, k = src_of(*plan[i])[1], i % 3, cur["w"] % 2
            free = w_free.get(cur["w"] - 2, ())
            cur["w"] += 1
            h = wh[:, k, :, :].rearrange("p a b -> p (a b)")[:, 0:n]
            l = wl[:, k, :, :].rearrange("p a b -> p (a b)")[:, 0:n]
            r = raw[:, j, 0:n]
            a = act.op(activation(h, r, ACT.Copy), loaded[i], *free)
            b = pool.op(tensor_tensor(l, r, h.bitcast(F), ALU.subtract), a, loaded[i], *free)
            raw_free[i] = (a, b)
            split[i] = (k, cur["w"] - 1, (a, b))
            load_slab()

        at_slab = {"i": 0}

        def next_slab(kind):
            i = at_slab["i"]
            at_slab["i"] += 1
            assert plan[i][0] == kind, (plan[i], kind)
            while cur["split"] < min(i + 2, len(plan)):
                split_slab()
            return split[i]

        def gemm(kind, kt, mm, hi, lo, toks, width=1024, ctx_act=None):
            k_, w_i, wt = next_slab(kind)
            j, free = slots.take()
            pe.wait(*wt)
            pe.wait(*free)
            if ctx_act is not None:
                jc, cfree = mslot.take()
                pe.wait(*cfree)
            for k in range(kt):
                pe.wait(*toks[k])
                wk, vk = wh[:, k_, k, 0:mm], wl[:, k_, k, 0:mm]
                for n, (w, x) in enumerate(((wk, hi), (wk, lo), (vk, hi))):
                    st, en = k == 0 and n == 0, k == kt - 1 and n == 2
                    for c in range(0, width, 512):
                        last = (matmul(
                            S[j][0:mm, c:c + 512], w, x[:, k, c:c + 512], start=st, stop=en))
                        if en and c == width - 512 and ctx_act is None:
                            tok = pe.op(last)
                        else:
                            pe.run(last)
                    if ctx_act is not None:
                        cx = ctx_act[0] if n != 1 else ctx_act[1]
                        f = (matmul(
                            M[jc][0:mm, 0:256], w, cx[:, k, :], start=st, stop=en))
                        if en:
                            tok = pe.op(f)
                        else:
                            pe.run(f)
            w_free[w_i] = (tok,)
            if ctx_act is not None:
                return j, jc, tok
            return j, tok

        s_c = sem("s_c")
        load(s_c, 1, cst[:, :], T["cst"])
        load(s_c, 2, vec[:, :], T["vec"])
        load(s_c, 3, csl[:, :], T["cc"])
        t_c = load(s_c, 4, snk[0:1, 0:8], T["sink"])
        ID = cst[:, C_ID:C_ID + 128]
        EPS = cst[:, C_EPS:C_EPS + 1]

        hch = at("hch", U, [128, 8, 256], R)
        hcl = at("hcl", U + 8 * KB, [128, 8, 256], R)
        P_QB, P_KA, P_KB, P_V = U, U + 16 * KB, U + 21 * KB, U + 41 * KB
        P_QA, P_CS = U + 66 * KB, U + 82 * KB
        P_SQ, P_RS, P_RP, P_VT = U + 90 * KB, U + 95 * KB, U + 100 * KB, U + 100 * KB
        qb = at("qb", P_QB, [128, 4, 1024], F)
        ka = at("ka", P_KA, [128, 1280], F)
        kb = at("kb", P_KB, [128, 4, 1280], F)
        vv = at("vv", P_V, [128, 10, 640], F)
        qa = at("qa", P_QA, [128, 4, 1024], F)
        cs = at("cs", P_CS, [128, 2, 1024], F)
        sq = at("sq", P_SQ, [128, 1280], F)
        rs = at("rs", P_RS, [128, 1280], F)
        rp = at("rp", P_RP, [128, 1024], F)
        vt = at("vt", P_VT, [128, 1280], F)
        xw = at("xw", P_V, [128, 8, 1280], F)
        xq = at("xq", P_KA, [128, 3, 1280], F)

        s_xw = [sem(f"s_xw{i}") for i in range(8)]
        t_xw = []
        for k in range(8):
            t_xw.append(load(s_xw[k], 1, xw[:, k, :], T["xT"][k]))
            if k in (1, 3, 5):
                load_slab()
        t_cs = load(sem("s_cs"), 1, cs[:, :, :], T["cs"])

        t_sil = act.op(activation(csl[:, :], csl[:, :], ACT.Silu), t_c)
        t_idb = act.op(activation(idb[:, :], ID, ACT.Copy))
        act.op(activation(mlb[:, :], cst[:, C_ML:C_ML + 128], ACT.Copy))
        t_msk = act.op(activation(mrb[:, :], cst[:, C_MR:C_MR + 128], ACT.Copy))
        t_snk = act.op(activation(snk[0:1, 8:16], snk[0:1, 0:8], ACT.Copy, scale=-1.0))
        dve.op(tensor_scalar(mv[:, M_QA:M_QA + 1], vec[:, V_QA:V_QA + 1], -0.125, None, ALU.mult), t_c)
        t_qg = dve.op(tensor_scalar(mv[:, M_QB:M_QB + 1], vec[:, V_QB:V_QB + 1], -0.125, None, ALU.mult))
        t_one = dve.op(memset(one1[:, :], 1.0))

        xqr = Ring(3)
        j, _ = slots.take()
        jc, _ = mslot.take()
        for k in range(8):
            a, free = xqr.take()
            t = act.op(activation(xq[:, a, :], xw[:, k, :], ACT.Square), t_xw[k], *free)
            pe.wait(t, t_c)
            for c, d in ((0, S[j][:, 0:512]), (512, S[j][:, 512:1024]), (1024, M[jc][:, 0:256])):
                f = (matmul(
                    d, cst[:, C_ONE:C_ONE + 128], xq[:, a, c:c + min(512, 1280 - c)], start=k == 0, stop=k == 7))
                if c == 1024:
                    t_ms = pe.op(f)
                else:
                    pe.run(f)
            xqr.readers[a] = (t_ms,)
        act.op(activation(rs[:, 0:1024], S[j][:, :], ACT.Ln, bias=EPS), t_ms)
        t = act.op(activation(rs[:, 1024:1280], M[jc][:, 0:256], ACT.Ln, bias=EPS))
        slots.readers[j] = mslot.readers[jc] = (t,)
        t_rs = act.op(activation(rs[:, :], rs[:, :], ACT.Exp, scale=-0.5), t)
        t_xr = []
        for k in range(8):
            eng = pool if k % 2 else dve
            t_xr.append(eng.op(tensor_tensor(xw[:, k, :], xw[:, k, :], rs[:, :], ALU.mult), t_rs, t_xw[k]))

        jm, mfree = mslot.take()
        pe.wait(t_sil, *mfree)
        for m in range(16):
            while cur["split"] <= m:
                split_slab()
            for k in range(8):
                f = (matmul(
                    M[jm][:, 2 * m:2 * m + 2], raw[:, m % 3, 128 * k:128 * k + 128], csl[:, 2 * k:2 * k + 2],
                    start=k == 0, stop=k == 7))
                pe.wait(loaded[m])
                if k == 7:
                    t = pe.op(f)
                else:
                    pe.run(f)
            raw_free[m] = (t,)
            load_slab()
        at_slab["i"] = 16
        mp = M[jm][:, 0:32].rearrange("p (m c) -> p c m", c=2)
        t1 = dve.op(tensor_tensor(mv[:, M_MOD:M_MOD + 16], mp[:, 0, :], vec[:, V_BMOD:V_BMOD + 16], ALU.add), t)
        t2 = dve.op(tensor_tensor(mv[:, M_CMOD:M_CMOD + 16], mp[:, 1, :], vec[:, V_BMOD:V_BMOD + 16], ALU.add))
        mslot.readers[jm] = (t1, t2)
        t1 = dve.op(scalar_tensor_tensor(mv[:, M_G1:M_G1 + 8], mv[:, M_MOD + 8:M_MOD + 16], 1.0,
                                                     vec[:, V_N1:V_N1 + 8], ALU.add, ALU.mult), t2)
        t_g = dve.op(scalar_tensor_tensor(mv[:, M_GC:M_GC + 8], mv[:, M_CMOD + 8:M_CMOD + 16], 1.0,
                                                      vec[:, V_N1:V_N1 + 8], ALU.add, ALU.mult), t1)
        t_h = []
        for k in range(8):
            xk = xw[:, k, :]
            ta = act.op(activation(xk[:, 0:1024], xk[:, 0:1024], ACT.Identity,
                        bias=mv[:, M_MOD + k:M_MOD + k + 1], scale=mv[:, M_G1 + k:M_G1 + k + 1]), t_g, t_xr[k])
            tb = act.op(activation(xk[:, 1024:1280], xk[:, 1024:1280], ACT.Identity,
                        bias=mv[:, M_CMOD + k:M_CMOD + k + 1], scale=mv[:, M_GC + k:M_GC + k + 1]))
            dve.op(tensor_copy(hh[:, k, :], xk[:, 0:1024]), tb)
            tc_ = dve.op(tensor_copy(hch[:, k, :], xk[:, 1024:1280]))
            td = pool.op(tensor_tensor(hl[:, k, :], xk[:, 0:1024], hh[:, k, :].bitcast(F), ALU.subtract), tc_, tb)
            te = dve.op(tensor_tensor(hcl[:, k, :], xk[:, 1024:1280], hch[:, k, :].bitcast(F), ALU.subtract), tc_)
            t_h.append((te, td))

        units = [("k", ka[:, :], vec[:, V_KA:V_KA + 1], True)]
        units += [("k", kb[:, m, :], vec[:, V_KB:V_KB + 1], False) for m in range(4)]
        units += [("v", m, None, False) for m in range(5)]
        units += [("q", qa[:, m, :], mv[:, M_QA:M_QA + 1], True) for m in range(4)]
        units += [("q", qb[:, m, :], mv[:, M_QB:M_QB + 1], False) for m in range(4)]
        t_ready = {}
        free_sq, free_vt, free_rp = [()], [()], [()]
        st = {}

        def stage0(u):
            kind, dst, g, rope = units[u]
            cx = kind != "q"
            if cx:
                j, jc, t = gemm("in", 8, 128, hh, hl, t_h, ctx_act=(hch, hcl))
            else:
                j, t = gemm("in", 8, 128, hh, hl, t_h)
                jc = None
            w = 1280 if cx else 1024
            if kind == "v":
                d = (sq if dst % 2 else vt)[:, :]
                dve.wait(*free_vt[0], *free_rp[0], *free_sq[0])
            else:
                d = dst
            if u == len(units) - 4:
                st["ctx_done"] = t
            tt = dve.op(tensor_copy(d[:, 0:1024], S[j][:, :]), t)
            slots.readers[j] = (tt,)
            if cx:
                tt = dve.op(tensor_copy(d[:, 1024:1280], M[jc][:, 0:256]))
                mslot.readers[jc] = (tt,)
            st[u] = tt

        def stage1(u):
            kind, dst, g, rope = units[u]
            j, free = slots.take()
            cx = kind != "q"
            if cx:
                jc, cfree = mslot.take()
                pe.wait(*cfree)
            pe.wait(*free)
            if kind == "v":
                pe.wait(st[u])
                src = sq if dst % 2 else vt
                for i in range(10):
                    d = S[j][:, 128 * i:128 * i + 128] if i < 8 else M[jc][:, 128 * (i - 8):128 * (i - 7)]
                    f = transpose(d, src[:, 128 * i:128 * i + 128], ID)
                    if i == 9:
                        t = pe.op(f)
                    else:
                        pe.run(f)
                if dst % 2:
                    free_sq[0] = (t,)
                else:
                    free_vt[0] = (t,)
                c = 128 * dst
                act.op(activation(vv[:, 0:8, c:c + 128], S[j][:, :].rearrange("p (a b) -> p a b", b=128), ACT.Copy), t)
                tt = act.op(activation(vv[:, 8:10, c:c + 128], M[jc][:, 0:256].rearrange("p (a b) -> p a b", b=128), ACT.Copy))
                slots.readers[j] = mslot.readers[jc] = (tt,)
                t_ready[u] = (tt,)
                return
            w = 1280 if cx else 1024
            t = act.op(activation(sq[:, 0:w], dst[:, 0:w], ACT.Square), st[u], *free_sq[0])
            pe.wait(t)
            blk = cst[:, C_BLK:C_BLK + 128]
            pe.run(matmul(S[j][:, 0:512], blk, sq[:, 0:512], start=True, stop=True))
            f = matmul(S[j][:, 512:1024], blk, sq[:, 512:1024], start=True, stop=True)
            if cx:
                pe.run(f)
                t = pe.op(matmul(M[jc][:, 0:256], blk, sq[:, 1024:1280], start=True, stop=True))
            else:
                t = pe.op(f)
            free_sq[0] = (t,)
            w = 1280 if cx else 1024
            tt = act.op(activation(rs[:, 0:1024], S[j][:, :], ACT.Ln, bias=EPS), t, *st.get("rs_free", ()))
            slots.readers[j] = (tt,)
            if cx:
                tt = act.op(activation(rs[:, 1024:1280], M[jc][:, 0:256], ACT.Ln, bias=EPS))
                mslot.readers[jc] = (tt,)
            tt = act.op(activation(rs[:, 0:w], rs[:, 0:w], ACT.Exp, scale=-0.5), tt)
            tt = dve.op(scalar_tensor_tensor(dst[:, 0:w], dst[:, 0:w], g, rs[:, 0:w], ALU.mult, ALU.mult), tt, t_qg, st[u])
            st["rs_free"] = (tt,)
            st[u, "n"] = tt
            t_ready[u] = (tt,)

        def stage2(u):
            kind, dst, g, rope = units[u]
            if not rope:
                return
            j, free = slots.take()
            pe.wait(st[u, "n"], *free)
            pm = cst[:, C_PERM:C_PERM + 128]
            pe.run(matmul(S[j][:, 0:512], pm, dst[:, 0:512], start=True, stop=True))
            t = pe.op(matmul(S[j][:, 512:1024], pm, dst[:, 512:1024], start=True, stop=True))
            ta = dve.op(tensor_tensor(rp[:, :], S[j][:, :], cs[:, 1, :], ALU.mult), t, t_cs, *free_rp[0], *free_vt[0])
            slots.readers[j] = (ta,)
            tb = pool.op(tensor_tensor(dst[:, 0:1024], dst[:, 0:1024], cs[:, 0, :], ALU.mult), t, t_cs, st[u, "n"])
            tb = pool.op(tensor_tensor(dst[:, 0:1024], dst[:, 0:1024], rp[:, :], ALU.add), ta, tb)
            free_rp[0] = (tb,)
            t_ready[u] = (tb,)

        nu = len(units)
        for s in range(nu + 2):
            if s < nu:
                stage0(s)
            if 1 <= s <= nu:
                stage1(s - 1)
            if s >= 2:
                stage2(s - 2)

        P_HL = AH + 32 * KB
        pp = at("pp", P_HL, [128, 2, 840], F)
        pt = at("pt", P_HL + 7 * KB, [128, 2, 7, 128], F)
        bt = at("bt", P_HL + 15 * KB, [128, 2, 1472], F)
        cb = at("cb", AH, [128, 1024], F)
        mr = at("mr", AH + 4 * KB, [128, 2, 1024], F)
        oa = at("oa", P_CS, [128, 8, 512], F)
        ob = at("ob", P_QA, [128, 8, 512], F)
        t_cb = load(sem("s_cb"), 1, cb[:, :], T["c_row"].to_broadcast([128, 1024]), st[nu - 1])
        t_cbs = act.op(activation(cb[:, :], cb[:, :], ACT.Silu), t_cb)
        s_mr = [sem("s_mr0"), sem("s_mr1")]
        mr_free = {}
        t_mods = []

        def mod_col(n):
            def ld(n):
                return load(s_mr[n % 2], n // 2 + 1, mr[:, n % 2, :], T["w_modT"][n], st[nu - 1], *mr_free.get(n - 2, ()))
            if n == 0:
                st["mr", 0], st["mr", 1] = ld(0), ld(1)
            t = dve.op(tensor_tensor_reduce(mr[:, n % 2, :], mr[:, n % 2, :], cb[:, :], 1.0, 0.0,
                       ALU.mult, ALU.add, mv[:, M_RAW + 16 + n:M_RAW + 17 + n]), st["mr", n], t_cbs)
            mr_free[n] = (t,)
            t_mods.append(t)
            if n + 2 < 32:
                st["mr", n + 2] = ld(n + 2)

        s_bt = [sem("s_bt0"), sem("s_bt1")]
        bt_free = {}
        t_bt = {}

        def bias_table(h):
            t = load(s_bt[h % 2], h // 2 + 1, bt[:, h % 2, :], T["bias"][h], st[nu - 1], *bt_free.get(h - 2, ()))
            t_bt[h] = t

        def bias_neg(h):
            t_bt[h] = act.op(activation(bt[:, h % 2, :], bt[:, h % 2, :], ACT.Copy, scale=-1.0), t_bt[h])

        items = []
        for h in range(8):
            for b in range(8):
                lo_ = max(b - 1, 0)
                hi_ = min(b + 1, 7)
                items.append(("a", h, b, 128 * lo_, 128 * (hi_ - lo_ + 1)))
        start = [0, 0, 0, 128, 256, 384, 512, 512]
        size = [512, 512, 576, 576, 576, 576, 512, 512]
        bcol = [6 * 64, 4 * 64, 896, 896, 896, 896, 2 * 64, 0]
        for h in range(8):
            for b in range(8):
                items.append(("b", h, b, start[b], size[b]))

        srd, ptr = Ring(2), Ring(3)
        srd.readers = [slots.readers[0], slots.readers[1]]
        banks = [S[2][:, 0:512], S[2][:, 512:1024], M[0][:, :]]
        ptr.readers = [slots.readers[2], slots.readers[2], mslot.readers[0]]
        o_free = [mslot.readers[1]]
        pring, ptring = Ring(2), Ring(2)
        av_last = {}
        it = {}

        def qk(i):
            kind, h, b, k0, L = items[i]
            s_, free = srd.take()
            D = S[s_]
            if kind == "a":
                p0 = 64 * (h // 4)
                q = qa[p0:p0 + 64, h % 4, 128 * b:128 * b + 128]
                kk = ka[p0:p0 + 64, :]
                pe.wait(*t_ready[0], *t_ready[10 + h % 4], t_msk, t_snk, t_one)
            else:
                p0 = 64 * (h % 2)
                q = qb[p0:p0 + 64, h // 2, 128 * b:128 * b + 128]
                kk = kb[p0:p0 + 64, h // 2, :]
                pe.wait(*t_ready[1 + h // 2], *t_ready[14 + h // 2])
            pe.wait(*free)
            n1 = min(256, L)
            pe.run(matmul(D[:, 0:256], q, kk[:, 1024:1280], start=True, stop=True))
            left = kind == "a" and b > 0
            f = matmul(D[:, 256:256 + n1], q, kk[:, k0:k0 + n1], start=True,
                                   stop=not (left or (kind == "a" and b == 0)))
            pe.run(f)
            if left:
                pe.run(matmul(D[:, 256:384], idb[:, :], mlb[:, :], start=False, stop=True))
            elif kind == "a":
                pe.run(matmul(D[:, 384:512], idb[:, :], mrb[:, :], start=False, stop=True))
            if L > 256:
                f = matmul(D[:, 512:256 + L], q, kk[:, k0 + 256:k0 + L], start=True, stop=kind == "b")
                if kind == "b":
                    t = pe.op(f)
                else:
                    pe.run(f)
                    pe.run(matmul(D[:, 512:640], idb[:, :], mrb[:, :], start=False, stop=True))
            w = 256 + L
            if kind == "a":
                t = pe.op(matmul(D[:, w:w + 1], one1[0:1, :], snk[0:1, 8 + h:9 + h], start=True, stop=True))
                w += 1
            col = b + 8 * (h % 2) + 16 * (kind == "b")
            nm = nmx[:, col:col + 1]
            if kind == "a":
                t = dve.op(tensor_reduce(nm, D[:, 0:w], AX, ALU.min), t, *it.get("nm", {}).get(col, ()))
            else:
                bc = bcol[b]
                t = dve.op(tensor_reduce(nm, D[:, 0:256], AX, ALU.min), t, *it.get("nm", {}).get(col, ()))
                t = dve.op(tensor_tensor_reduce(D[:, 256:w], D[:, 256:w], bt[:, h % 2, bc:bc + L], 1.0, nm,
                           ALU.add, ALU.min, nm), t, t_bt[h])
                bt_free[h] = (t,)
            pk, pfree = pring.take()
            t = act.op(activation(pp[:, pk, 0:w], D[:, 0:w], ACT.Exp, bias=nm, scale=-1.0,
                       accum_out=den[:, col:col + 1]), t, *pfree, *it.get("den", {}).get(col, ()))
            it.setdefault("nm", {})[col] = (t,)
            srd.readers[s_] = (t,)
            it[i] = (pk, t)

        def tr(i):
            kind, h, b, k0, L = items[i]
            pk, t = it[i]
            pe.wait(t)
            n = (256 + L + 127) // 128
            tk, tfree = ptring.take()
            toks = []
            for half in range(2):
                tiles = list(range(4 * half, min(4 * half + 4, n)))
                if not tiles:
                    continue
                bk, free = ptr.take()
                pe.wait(*free)
                full = [x for x in tiles if 128 * x + 128 <= 256 + L]
                for x in tiles:
                    kw = min(128, 256 + L - 128 * x)
                    f = (transpose(
                        banks[bk][0:kw, 128 * (x - 4 * half):128 * (x - 4 * half) + 128], pp[:, pk, 128 * x:128 * x + kw], ID))
                    if x == tiles[-1]:
                        tp = pe.op(f)
                    else:
                        pe.run(f)
                pring.readers[pk] = (tp,)
                m = len(full)
                if m:
                    src = banks[bk][:, 0:128 * m]
                    dst = pt[:, tk, 4 * half:4 * half + m, :].rearrange("p a b -> p (a b)")
                    if half == 0:
                        te = act.op(activation(dst, src, ACT.Copy), tp, *tfree)
                    else:
                        te = dve.op(tensor_copy(dst, src), tp, *tfree)
                    toks.append(te)
                if m < len(tiles):
                    te = dve.op(tensor_copy(pt[0:64, tk, 4 * half + m, :],
                                banks[bk][0:64, 128 * m:128 * m + 128]), tp, *tfree)
                    toks.append(te)
                ptr.readers[bk] = (te,)
            it[i, "t"] = (tk, toks, n)

        def av(i):
            kind, h, b, k0, L = items[i]
            tk, toks, n = it[i, "t"]
            pe.wait(*toks)
            if b == 0:
                pe.wait(*o_free[0])
                if kind == "a":
                    pe.wait(*t_ready[5])
                else:
                    pe.wait(*t_ready[6 + h // 2])
            vc = 64 * (h // 4) if kind == "a" else 128 + 64 * h
            tiles = [8, 9] + [k0 // 128 + x for x in range(n - 2)]
            for x, v in enumerate(tiles):
                kw = min(128, 256 + L - 128 * x)
                f = (matmul(M[1][:, 64 * b:64 * b + 64], pt[0:kw, tk, x, :],
                     vv[0:kw, v, vc:vc + 64], start=x == 0, stop=x == n - 1))
                if x == n - 1:
                    t = pe.op(f)
                else:
                    pe.run(f)
            ptring.readers[tk] = (t,)
            if b == 7:
                c = 8 * (h % 2) + 16 * (kind == "b")
                dst = (oa if kind == "a" else ob)[:, :, 64 * h:64 * h + 64]
                r = dve.op(reciprocal(rdn[:, c:c + 8], den[:, c:c + 8]), it[i][1], *it.get(("rd", c), ()))
                it.setdefault("den", {}).update({c + x: (r,) for x in range(8)})
                t = dve.op(tensor_tensor(dst, M[1][:, :].rearrange("p (a b) -> p a b", b=64),
                           rdn[:, c:c + 8].unsqueeze(2).to_broadcast([128, 8, 64]), ALU.mult), t, r)
                it["rd", c] = (t,)
                o_free[0] = (t,)
                it[kind, "o"] = t

        bias_table(0)
        bias_table(1)
        NI = len(items)
        mods = 0
        for i in range(NI + 2):
            if i < NI:
                if items[i][0] == "b" and items[i][2] == 0:
                    bias_neg(items[i][1])
                qk(i)
                if items[i][0] == "b" and items[i][2] == 7 and items[i][1] + 2 < 8:
                    bias_table(items[i][1] + 2)
            if i >= 2:
                av(i - 2)
            if 1 <= i <= NI:
                tr(i - 1)
            if i % 4 == 2 and mods < 32:
                mod_col(mods)
                mods += 1
        t = dve.op(tensor_tensor(mv[:, M_MOD + 16:M_MOD + 48], mv[:, M_RAW + 16:M_RAW + 48],
                   vec[:, V_BMOD + 16:V_BMOD + 48], ALU.add), t_mods[-1])
        t_mod = dve.op(scalar_tensor_tensor(mv[:, M_G2:M_G2 + 8], mv[:, M_MOD + 32:M_MOD + 40], 1.0,
                       vec[:, V_N2:V_N2 + 8], ALU.add, ALU.mult), t)

        xt = at("xt", U, [128, 8, 1024], F)
        x2 = at("x2", U + 32 * KB, [128, 1024], F)
        sqt = at("sqt", U + 36 * KB, [128, 2, 1024], F)
        rs2 = at("rs2", U + 44 * KB, [128, 1024], F)
        tt_ = at("tt_", U + 48 * KB, [128, 3, 1024], F)
        s_xt = [sem(f"s_xt{i}") for i in range(8)]
        att_done = (it["b", "o"], (pe.sem, pe.n))
        t_xt = [(load(s_xt[k], 1, xt[:, k, :], T["xT"][k][:, 0:1024], *att_done),) for k in range(8)]
        osq = at("osq", U + 32 * KB, [128, 512], F)
        slots.readers = [srd.readers[0], srd.readers[1], ptr.readers[0] + ptr.readers[1]]
        mslot.readers = [ptr.readers[2], o_free[0]]

        for n, buf in enumerate((oa, ob)):
            for b in range(8):
                c = 8 * n + b
                t = act.op(activation(osq[:, :], buf[:, b, :], ACT.Square,
                           accum_out=oss[:, c:c + 1]), it["ab"[n], "o"], *att_done, (act.sem, act.n))
        t = act.op(activation(ors[:, :], oss[:, :], ACT.Ln, bias=EPS, scale=1.0 / 512), t)
        t_or = act.op(activation(ors[:, :], ors[:, :], ACT.Exp, scale=-0.5), t)
        t_on = []
        for n, buf in enumerate((oa, ob)):
            for b in range(8):
                eng = dve if b % 2 else pool
                t_on.append(eng.op(tensor_scalar(buf[:, b, :], buf[:, b, :],
                            ors[:, 8 * n + b:8 * n + b + 1], None, ALU.mult), t_or))
        t_h = [[] for _ in range(8)]
        for n, buf in enumerate((oa, ob)):
            for f_ in range(4):
                j, free = slots.take()
                pe.wait(*free)
                for b in range(8):
                    pe.wait(t_on[8 * n + b])
                    f = transpose(S[j][:, 128 * b:128 * b + 128],
                                                                        buf[:, b, 128 * f_:128 * f_ + 128], ID)
                    if b == 7:
                        t = pe.op(f)
                    else:
                        pe.run(f)
                k = 4 * n + f_
                g = vec[:, V_ONA + k:V_ONA + k + 1]
                ta = act.op(activation(hh[:, k, :], S[j][:, :], ACT.Copy, scale=g), t, *att_done)
                tb = dve.op(scalar_tensor_tensor(hl[:, k, :], S[j][:, :], g,
                            hh[:, k, :].bitcast(F), ALU.mult, ALU.subtract), ta, *att_done)
                slots.readers[j] = (ta, tb)
                t_h[k] = (ta, tb)

        sqr = Ring(2)
        x2s = {"tok": (), "free": ()}

        def square(k, tok, X):
            a, free = sqr.take()
            t = act.op(activation(sqt[:, a, :], X[:, k, :], ACT.Square), *tok, *free, *x2s.get("ovl", ()))
            if k == 0:
                t = pool.op(tensor_copy(x2[:, :], sqt[:, a, :]), t, *x2s["free"])
            else:
                t = pool.op(tensor_tensor(x2[:, :], x2[:, :], sqt[:, a, :], ALU.add), t, *x2s["tok"])
            sqr.readers[a] = (t,)
            x2s["tok"] = (t,)

        def rstd():
            j, free = slots.take()
            pe.wait(*free, *x2s["tok"])
            one = cst[:, C_ONE:C_ONE + 128]
            pe.run(matmul(S[j][:, 0:512], one, x2[:, 0:512], start=True, stop=True))
            t = pe.op(matmul(S[j][:, 512:1024], one, x2[:, 512:1024], start=True, stop=True))
            x2s["free"] = (t,)
            t = act.op(activation(rs2[:, :], S[j][:, :], ACT.Ln, bias=EPS), t)
            slots.readers[j] = (t,)
            return act.op(activation(rs2[:, :], rs2[:, :], ACT.Exp, scale=-0.5), t)

        ttr = Ring(3)

        def normed(G, SH, toks):
            t_rs = rstd()
            out_ = []
            for k in range(8):
                a, free = ttr.take()
                y = tt_[:, a, :]
                g = G[:, k:k + 1]
                t = pool.op(tensor_tensor(y, xt[:, k, :], rs2[:, :], ALU.mult), t_rs, *toks[k], *free)
                if SH is None:
                    t = act.op(activation(y, y, ACT.Copy, scale=g), t)
                else:
                    s = SH[:, k:k + 1]
                    t = act.op(activation(y, y, ACT.Identity, scale=g, bias=s), t)
                ta = dve.op(tensor_copy(hh[:, k, :], y), t)
                tb = dve.op(tensor_tensor(hl[:, k, :], y, hh[:, k, :].bitcast(F), ALU.subtract), ta)
                ttr.readers[a] = (tb,)
                out_.append((ta, tb))
            return out_

        def residual(k, j, t, gate, sq_last):
            f = (scalar_tensor_tensor(xt[:, k, :], S[j][:, :], gate, xt[:, k, :], ALU.mult, ALU.add)) \
                if gate is not None else (tensor_tensor(xt[:, k, :], S[j][:, :], xt[:, k, :], ALU.add))
            t = dve.op(f, t, t_mod, *t_xt[k])
            slots.readers[j] = (t,)
            t_xt[k] = (t,)
            if sq_last:
                square(k, (t,), xt)

        x2s["ovl"] = tuple(t_on)
        sqr.readers = [(t_or,)] * 2
        for m in range(8):
            j, t = gemm("out", 8, 128, hh, hl, t_h)
            residual(m, j, t, mv[:, M_MOD + 16 + m:M_MOD + 17 + m], True)

        fh = at("fh", U + 60 * KB, [128, 6, 1024], R)
        fl = at("fl", U + 84 * KB, [128, 6, 1024], R)
        sg = at("sg", U + 44 * KB, [128, 2, 1024], F)
        pr = at("pr", U + 52 * KB, [128, 2, 1024], F)
        hid_free = {}
        hid = {}

        def emit_hidden(j_, y, ty, r, ring_k):
            q = j_ % 6
            ta = dve.op(tensor_copy(fh[:, q, :], y), ty, *hid_free.get(j_ - 6, ()))
            tb = pool.op(tensor_tensor(fl[:, q, :], y, fh[:, q, :].bitcast(F), ALU.subtract), ty, ta)
            hid[j_] = (ta, tb)
            return tb

        def down(kind, g, gate, final):
            k0, n = sum(DNG[:g]), DNG[g]
            for m in range(8):
                k_, w_i, wt = next_slab(kind)
                j, free = slots.take()
                pe.wait(*wt, *free)
                for k in range(n):
                    q = (k0 + k) % 6
                    pe.wait(*hid[k0 + k])
                    for i_, (w, x) in enumerate(((wh, fh), (wh, fl), (wl, fh))):
                        stt, en = k == 0 and i_ == 0, k == n - 1 and i_ == 2
                        for c in (0, 512):
                            f = (matmul(
                                S[j][:, c:c + 512], w[:, k_, k, :], x[:, q, c:c + 512], start=stt, stop=en))
                            if en and c:
                                t = pe.op(f)
                            else:
                                pe.run(f)
                w_free[w_i] = (t,)
                gt = gate[:, m:m + 1] if gate is not None else None
                residual(m, j, t, gt, final)
            for k in range(n):
                hid_free[k0 + k] = (t,)

        t_h = normed(mv[:, M_G2:M_G2 + 8], mv[:, M_MOD + 24:M_MOD + 32], t_xt)
        sgr, prr = Ring(2), Ring(2)
        sgr.readers = prr.readers = None
        sgr.readers, prr.readers = [t_h[-1]] * 2, [t_h[-1]] * 2
        x2s["ovl"] = ()
        for kind, a in ffn_order():
            if kind == "gu":
                jg, tg = gemm("f1g", 8, 128, hh, hl, t_h)
                s_, free = sgr.take()
                p_, pfree = prr.take()
                t = act.op(activation(sg[:, s_, :], S[jg][:, :], ACT.Silu), tg, *free)
                slots.readers[jg] = (t,)
                ju, tu = gemm("f1u", 8, 128, hh, hl, t_h)
                t = dve.op(tensor_tensor(pr[:, p_, :], sg[:, s_, :], S[ju][:, :], ALU.mult), t, tu, *pfree)
                slots.readers[ju] = (t,)
                sgr.readers[s_] = (t,)
                tb = emit_hidden(a, pr[:, p_, :], t, None, None)
                prr.readers[p_] = (tb,)
            else:
                down("d1", a, mv[:, M_MOD + 40:M_MOD + 48], a == len(DNG) - 1)

        ttr.readers = [prr.readers[0] + prr.readers[1] + sgr.readers[0] + sgr.readers[1]] * 3
        s_sp = sem("s_spill")
        for k in range(8):
            t_sp = load(s_sp, k + 1, T["spill"][k], xt[:, k, :], *t_xt[k])
        act.wait(*ttr.readers[0])
        t_h = normed(vec[:, V_MIX:V_MIX + 8], None, t_xt)
        vo = at("vo", U, [128, 4, 8, 256], F)
        gq = at("gq", U + 32 * KB, [128, 4, 1024], F)
        gd = at("gd", U + 48 * KB, [128, 8, 512], F)
        gst = at("gst", U + 64 * KB, [128, 8, 256], F)
        gt2 = at("gt2", U + 72 * KB, [128, 2, 1024], F)
        gsq = at("gsq", U + 80 * KB, [128, 1024], F)
        grs = at("grs", U + 84 * KB, [128, 1024], F)
        gz = at("gz", U + 88 * KB, [128, 2, 512], F)
        ge = at("ge", U + 92 * KB, [128, 2, 512], F)
        glr = at("glr", U + 96 * KB, [32, 1024], F)
        wg2 = at("wg2", U + 100 * KB, [32, 512], F)
        ffn_done = tuple(hid_free[21])
        t_w2 = load(sem("s_w2"), 1, wg2[0:17, :], T["w_gate2"], *ffn_done)
        t_gl1 = dve.op(memset(glr[:, :], 1.0), *ffn_done)
        j, t = gemm("gl", 8, 16, hh, hl, t_h)
        t_glr = dve.op(tensor_copy(glr[0:16, :], S[j][0:16, :]), t, t_gl1)
        slots.readers[j] = (t_glr,)
        jg, free = mslot.take()
        gring = Ring(2)
        t_dec = []
        ge_free = mslot.readers[jg]
        jd, dfree = slots.take()
        dring = Ring(2)
        dring.readers = [dfree, dfree]
        jz, zfree = slots.take()
        zring = Ring(2)
        zring.readers = [zfree, zfree]
        pe.wait(*free)
        for i in range(8):
            z, zf = zring.take()
            Z = S[jz][:, 512 * z:512 * z + 512]
            t = pe.op(matmul(Z, glr[0:17, 128 * i:128 * i + 128], wg2[0:17, :], start=True, stop=True),
                      t_glr, t_w2, *zf)
            a, gf = gring.take()
            ta = act.op(activation(ge[:, a, :], Z, ACT.Abs), t, *gf, *ffn_done)
            ta = act.op(activation(ge[:, a, :], ge[:, a, :], ACT.Exp, scale=-1.0), ta)
            ta = act.op(activation(ge[:, a, :], ge[:, a, :], ACT.Ln, bias=1.0), ta)
            tb = dve.op(scalar_tensor_tensor(gz[:, a, :], Z, 0.0, ge[:, a, :], ALU.min, ALU.subtract),
                        ta, t, *ffn_done)
            zring.readers[z] = (tb,)
            d, df = dring.take()
            Dm = S[jd][:, 512 * d:512 * d + 512]
            t = pe.op(matmul(Dm, cst[:, C_SUF:C_SUF + 128], gz[:, a, :], start=True, stop=True), tb, *df)
            for h in range(4):
                f = (matmul(M[jg][:, 16 * h + 2 * i:16 * h + 2 * i + 2], gz[:, a, 128 * h:128 * h + 128],
                     cst[:, C_IND:C_IND + 2], start=True, stop=True))
                if h == 3:
                    tg = pe.op(f)
                else:
                    pe.run(f)
            gring.readers[a] = (tg,)
            td = act.op(activation(gd[:, i, :], Dm, ACT.Exp), t, *t_h[-1])
            dring.readers[d] = (td,)
            t_dec.append(td)
        t_ege = act.op(activation(ege[:, :, :].rearrange("p a b -> p (a b)"), M[jg][:, 0:64], ACT.Exp), tg)
        mslot.readers[jg] = (t_ege,)
        slots.readers[jd] = dring.readers[0] + dring.readers[1]
        slots.readers[jz] = zring.readers[0] + zring.readers[1]

        g2r = Ring(2)
        pend = []
        t_kd, t_v = {}, {}

        def g_fin(u):
            kind, m, a, t = u
            j, free = slots.take()
            pe.wait(t, *free)
            for i in range(8):
                f = transpose(S[j][:, 128 * i:128 * i + 128], gt2[:, a, 128 * i:128 * i + 128], ID)
                if i == 7:
                    t = pe.op(f)
                else:
                    pe.run(f)
            g2r.readers[a] = (t,)
            P3 = S[j][:, :].rearrange("p (a b) -> p a b", b=128)
            if kind == "gk":
                d = gd[:, :, 128 * m:128 * m + 128]
                t = dve.op(tensor_tensor(d, P3, d, ALU.mult), t, t_dec[-1])
                t_kd[m] = t
            else:
                h, c = m // 2, 128 * (m % 2)
                t = act.op(activation(vo[:, h, :, c:c + 128], P3, ACT.Copy), t, t_sp, *t_h[-1])
                t_v[m] = t
            slots.readers[j] = (t,)

        for n in range(12):
            kind, m = ("gk", n) if n < 4 else ("gv", n - 4)
            j, t = gemm(kind, 8, 128, hh, hl, t_h)
            a, free = g2r.take()
            t = dve.op(tensor_copy(gt2[:, a, :], S[j][:, :]), t, *free, *ffn_done)
            slots.readers[j] = (t,)
            pend.append((kind, m, a, t))
            if len(pend) > 1:
                g_fin(pend.pop(0))
        t_q = []
        for m in range(4):
            j, t = gemm("gq", 8, 128, hh, hl, t_h)
            t = act.op(activation(gq[:, m, :], S[j][:, :], ACT.Copy, scale=float(128 ** -0.5)), t, *t_h[-1])
            slots.readers[j] = (t,)
            t_q.append(t)
            if pend:
                g_fin(pend.pop(0))

        kvb = [S[2][:, 0:256], S[2][:, 512:768], M[0][:, 0:256], M[1][:, 0:256]]
        kvr = Ring(4)
        kvr.readers = [slots.readers[2], slots.readers[2], mslot.readers[0], mslot.readers[1]]
        o_rd = [slots.readers[0], slots.readers[1]]
        stv = Ring(8)
        prev = None
        t_gn = {}
        norms = []
        free_gsq = [()]
        free_grs = [()]

        def kv(h, c):
            b, free = kvr.take()
            pe.wait(*free, t_kd[h], t_v[2 * h], t_v[2 * h + 1])
            p0, i = 64 * (c % 2), c // 2
            t = pe.op(matmul(kvb[b], gd[p0:p0 + 64, i, 128 * h:128 * h + 128], vo[p0:p0 + 64, h, i, :],
                                         start=True, stop=True))
            s, sfree = stv.take()
            if c == 0:
                t = dve.op(tensor_copy(gst[:, s, :], kvb[b]), t, *sfree, *ffn_done)
            else:
                q = (s - 1) % 8
                t = dve.op(scalar_tensor_tensor(gst[:, s, :], gst[:, q, :], ege[:, h, c:c + 1], kvb[b],
                           ALU.mult, ALU.add), t, t_ege, *sfree, st["gs"])
            st["gs"] = t
            kvr.readers[b] = (t,)
            return s, t

        def oo(h, c, s, t):
            pe.wait(t, t_q[h], *o_rd[0], *o_rd[1])
            for d in range(2):
                f = (matmul(S[d][:, 64 * c:64 * c + 64], gst[:, s, 128 * d:128 * d + 128],
                     gq[:, h, 64 * c:64 * c + 64], start=True, stop=True))
                if d:
                    t = pe.op(f)
                else:
                    pe.run(f)
            stv.readers[s] = (t,)
            return t

        def head_out(h, t):
            O = vo[:, h, :, :].rearrange("p a b -> p (a b)")
            ta = act.op(activation(O[:, 0:1024], S[0][:, :], ACT.Copy), t)
            tb = dve.op(tensor_copy(O[:, 1024:2048], S[1][:, :]), t)
            o_rd[0], o_rd[1] = (ta,), (tb,)
            t_gn[h] = (ta, tb)

        lag = []
        for h in range(4):
            for c in range(16):
                s, t = kv(h, c)
                lag.append((h, c, s, t))
                if len(lag) > 2:
                    x = lag.pop(0)
                    t = oo(*x)
                    if x[1] == 15:
                        head_out(x[0], t)
        while lag:
            x = lag.pop(0)
            t = oo(*x)
        head_out(3, t)
        slots.readers = [o_rd[0], o_rd[1], kvr.readers[0] + kvr.readers[1]]
        mslot.readers = [kvr.readers[2], kvr.readers[3]]

        def head_norm(h):
            O = vo[:, h, :, :].rearrange("p a b -> p (a b)")
            j, free = slots.take()
            pe.wait(*free)
            for d in range(2):
                t = act.op(activation(gsq[:, :], O[:, 1024 * d:1024 * d + 1024], ACT.Square),
                           *t_gn[h], *free_gsq[0], *ffn_done)
                pe.wait(t)
                for c in (0, 512):
                    f = (matmul(S[j][:, c:c + 512], cst[:, C_DV:C_DV + 128], gsq[:, c:c + 512],
                         start=d == 0, stop=d == 1))
                    if c:
                        t = pe.op(f)
                    else:
                        pe.run(f)
                free_gsq[0] = (t,)
            t = act.op(activation(grs[:, :], S[j][:, :], ACT.Ln, bias=EPS), t, *free_grs[0])
            slots.readers[j] = (t,)
            t = act.op(activation(grs[:, :], grs[:, :], ACT.Exp, scale=-0.5), t)
            for d in range(2):
                Od = O[:, 1024 * d:1024 * d + 1024]
                g = vec[:, V_GLN + 2 * h + d:V_GLN + 2 * h + d + 1]
                tn = dve.op(scalar_tensor_tensor(Od, Od, g, grs[:, :], ALU.mult, ALU.mult), t, *t_gn[h])
                st["gn", 2 * h + d] = tn
            free_grs[0] = (tn,)

        t_o = []
        for m in range(8):
            j, t = gemm("gr", 8, 128, hh, hl, t_h)
            a, free = g2r.take()
            t = act.op(activation(gt2[:, a, :], S[j][:, :], ACT.Silu), t, *free)
            slots.readers[j] = (t,)
            if m % 2 == 0:
                head_norm(m // 2)
            Od = vo[:, m // 2, :, :].rearrange("p a b -> p (a b)")[:, 1024 * (m % 2):1024 * (m % 2) + 1024]
            t = dve.op(tensor_tensor(Od, Od, gt2[:, a, :], ALU.mult), t, st["gn", m])
            g2r.readers[a] = (t,)
            t_o.append((Od, t))
        r_done = (pe.sem, pe.n)
        t_h = []
        for m in range(8):
            Od, t = t_o[m]
            ta = dve.op(tensor_copy(hh[:, m, :], Od), t, r_done)
            tb = pool.op(tensor_tensor(hl[:, m, :], Od, hh[:, m, :].bitcast(F), ALU.subtract), t, ta, r_done)
            t_h.append((ta, tb))
        t_xt = []
        for k in range(8):
            t_xt.append((load(s_xt[k], 2, xt[:, k, :], T["spill"][k], *t_h[k], *t_h[-1], t_sp),))
        x2s["ovl"] = t_h[-1]
        x2s["free"] += t_h[-1]
        for m in range(8):
            j, t = gemm("go", 8, 128, hh, hl, t_h)
            residual(m, j, t, None, True)
        ttr.readers = [t_h[-1]] * 3
        t_h = normed(vec[:, V_FFN:V_FFN + 8], None, t_xt)

        ub = at("ub", U + 40 * KB, [128, 2, 1026], F)
        tg_ = at("tg_", U + 49 * KB, [128, 1, 1024], F)
        tv_ = at("tv_", U + 53 * KB, [128, 1, 1024], F)
        t = tuple(x2s["free"]) + t_h[-1]
        sqr = Ring(1)
        sqr.readers = [x2s["tok"]]
        t_z = [dve.op(memset(ub[:, i, 0:2], 0.0), *t, *x2s["tok"]) for i in range(2)]
        ubr = Ring(2)
        ubr.readers = [(t_z[1],), (t_z[1],)]
        tring = {0: t_h[-1], 1: t_h[-1]}
        hid_free = {}

        def conv(j, t, buf, which, n):
            a, free = ubr.take()
            x = buf[:, 0, :]
            t0 = act.op(activation(ub[:, a, 2:1026], S[j][:, :], ACT.Copy), t, *free)
            w = [vec[:, V_CW + 44 * i + n:V_CW + 44 * i + n + 1] for i in range(3)]
            t1 = act.op(activation(x, S[j][:, :], ACT.Identity, scale=w[2], bias=vec[:, V_CB + n:V_CB + n + 1]),
                        *tring[which])
            slots.readers[j] = (t1,)
            t2 = dve.op(scalar_tensor_tensor(x, ub[:, a, 1:1025], w[1], x, ALU.mult, ALU.add), t0, t1)
            t3 = dve.op(scalar_tensor_tensor(x, ub[:, a, 0:1024], w[0], x, ALU.mult, ALU.add), t2)
            ubr.readers[a] = (t3,)
            return t3

        for kind, a in ffn_order():
            if kind == "gu":
                jg, tg = gemm("f2g", 8, 128, hh, hl, t_h)
                t = conv(jg, tg, tg_, 0, a)
                ts = act.op(activation(tg_[:, 0, :], tg_[:, 0, :], ACT.Silu), t)
                ju, tu = gemm("f2u", 8, 128, hh, hl, t_h)
                t = conv(ju, tu, tv_, 1, 22 + a)
                t = dve.op(tensor_tensor(tv_[:, 0, :], tv_[:, 0, :], tg_[:, 0, :], ALU.mult), t, ts)
                tring[0] = (t,)
                tb = emit_hidden(a, tv_[:, 0, :], t, None, None)
                tring[1] = (tb,)
            else:
                down("d2", a, None, a == len(DNG) - 1)

        fo = at("fo", U + 60 * KB, [128, 8, 1024], F)
        rs3 = at("rs3", U + 92 * KB, [128, 1024], F)
        j, free = slots.take()
        pe.wait(*free, *x2s["tok"])
        one = cst[:, C_ONE:C_ONE + 128]
        pe.run(matmul(S[j][:, 0:512], one, x2[:, 0:512], start=True, stop=True))
        t = pe.op(matmul(S[j][:, 512:1024], one, x2[:, 512:1024], start=True, stop=True))
        t = act.op(activation(rs3[:, :], S[j][:, :], ACT.Ln, bias=EPS), t)
        t = act.op(activation(rs3[:, :], rs3[:, :], ACT.Exp, scale=-0.5), t)
        s_out = sem("s_out")
        for k in range(8):
            ta = dve.op(scalar_tensor_tensor(fo[:, k, :], xt[:, k, :], vec[:, V_FIN + k:V_FIN + k + 1],
                        rs3[:, :], ALU.mult, ALU.mult), t, *t_xt[k])
            t_out = load(s_out, k + 1, out[k], fo[:, k, :], ta)
        sp.wait(t_out)
        assert at_slab["i"] == len(plan), (at_slab, len(plan))

        block = ctx.enter_context(nc.Block())

        @block.tensor
        def _(e):
            for f in pe.items:
                f(e)

        @block.scalar
        def _(e):
            for f in act.items:
                f(e)

        @block.vector
        def _(e):
            for f in dve.items:
                f(e)

        @block.gpsimd
        def _(e):
            for f in pool.items:
                f(e)

        @block.sync
        def _(e):
            for f in sp.items:
                f(e)


def constants():
    f = np.float32
    c = np.zeros((128, C_N), f)
    i = np.arange(128)
    c[:, C_ID:C_ID + 128] = np.eye(128, dtype=f)
    c[:, C_ONE:C_ONE + 128] = 1.0 / 1024
    c[:, C_BLK:C_BLK + 128] = (i[:, None] // 64 == i[None] // 64) / 64.0
    c[:, C_PERM:C_PERM + 128] = i[:, None] == (i[None] ^ 16)
    c[:, C_SUF:C_SUF + 128] = ((i[:, None] > i[None]) & (i[:, None] // 64 == i[None] // 64)) / 16.0
    c[:, C_DV:C_DV + 128] = 1.0 / 256
    c[:, C_ML:C_ML + 128] = np.where(i[None] < i[:, None], BIG, 0)
    c[:, C_MR:C_MR + 128] = np.where(i[None] > i[:, None], BIG, 0)
    c[:, C_IND:C_IND + 2] = (i[:, None] // 64 == np.arange(2)[None]) / 16.0
    c[:, C_EPS] = 1e-6
    inv = (f(1.0) / (f(10000.0) ** (np.arange(16, dtype=f) / f(16)))).astype(f)
    t = np.arange(1024)
    d = i % 64
    pos = np.where((d < 32)[:, None], t[None] // 64, t[None] % 64).astype(f)
    ang = (pos * inv[d % 16][:, None]).astype(f)
    sign = np.where(d % 32 < 16, -1.0, 1.0).astype(f)
    cs = np.stack([np.cos(ang), np.sin(ang) * sign[:, None]], 1).astype(f)
    return c, np.ascontiguousarray(cs)


def bias_index():
    dr = np.zeros((128, 23, 64), int)
    dc = np.zeros((128, 23, 64), int)
    ok = np.zeros((128, 23, 64), bool)
    q = np.arange(128)
    qr, qc = q // 64, q % 64
    kc = np.arange(64)
    c0 = np.clip(qc - 8, 0, 48)
    col_ok = (kc[None] >= c0[:, None]) & (kc[None] < c0[:, None] + 16)
    es = list(range(1, 15)) + list(range(3, 12))
    for s, e in enumerate(es):
        dr[:, s, :] = np.clip(e - qr, 0, 14)[:, None]
        dc[:, s, :] = np.clip(kc[None] - qc[:, None] + 15, 0, 30)
        row = np.ones(128, bool)
        if s >= 14 and e == 3:
            row = qr == 0
        if s >= 14 and e == 11:
            row = qr == 1
        ok[:, s, :] = col_ok & row[:, None]
    return dr.reshape(128, -1), dc.reshape(128, -1), ok.reshape(128, -1)


def cols(v):
    return np.ascontiguousarray(v).reshape(-1, 128).T


def slabs(w):
    k, m = w.shape
    return np.ascontiguousarray(w.reshape(k // 128, 128, m // 128, 128).transpose(2, 1, 0, 3)).reshape(m // 128, 128, k)


def layout(i):
    f = np.float32
    A = {}
    cst, cs = constants()
    A["cst"], A["cs"] = cst, cs
    v = np.zeros((128, V_N), f)
    v[:, V_BMOD:V_BMOD + 48] = cols(i["b_mod"][0])
    v[:, V_N1:V_N1 + 8] = cols(i["norm1_g"][0])
    for c, n in ((V_QA, "qn_a"), (V_KA, "kn_a"), (V_QB, "qn_b"), (V_KB, "kn_b")):
        v[:, c] = np.concatenate([i[n][0], i[n][0]])
    v[:, V_ONA:V_ONA + 4] = cols(i["on_a"][0])
    v[:, V_ONB:V_ONB + 4] = cols(i["on_b"][0])
    v[:, V_N2:V_N2 + 8] = cols(i["norm2_g"][0])
    v[:, V_MIX:V_MIX + 8] = cols(i["mix_norm_w_2"][0])
    v[:, V_FFN:V_FFN + 8] = cols(i["ffn_norm_w_2"][0])
    v[:, V_FIN:V_FIN + 8] = cols(i["final_norm_w_2"])
    v[:, V_GLN:V_GLN + 8] = cols(i["gla_norm_w_2"][0])
    for t in range(3):
        v[:, V_CW + 44 * t:V_CW + 44 * t + 44] = cols(i["ffn_conv_w_2"][0, t])
    v[:, V_CB:V_CB + 44] = cols(i["ffn_conv_b_2"][0])
    A["vec"] = v
    cc = np.stack([cols(i["c"][0]), cols(i["c_ctx"])], 2)
    A["cc"] = np.ascontiguousarray(cc).reshape(128, 16)
    A["c_row"] = np.ascontiguousarray(i["c"])
    A["sink"] = np.ascontiguousarray(i["sink_a"])
    x = np.concatenate([i["x"][0], i["ctx"][0]], 0)
    A["xT"] = np.ascontiguousarray(x.T).reshape(8, 128, 1280)
    w = i["w_mod"][0]
    A["w_mod0"] = slabs(w[:, :2048])
    A["w_modT"] = np.ascontiguousarray(w[:, 2048:].T).reshape(32, 128, 1024)
    w = i["w_in"][0]
    qa, ka, va, qb, kb, vb = np.split(w, np.cumsum([512, 128, 128, 512, 512]), axis=1)
    order = np.concatenate([np.concatenate([np.arange(64) + 64 * j, np.arange(64) + 64 * (j + 4)]) for j in range(4)])
    A["w_in"] = slabs(np.concatenate([ka, kb, va, vb, qa[:, order], qb], 1))
    A["w_out"] = slabs(i["w_out"][0])
    A["w_f1g"] = slabs(i["w_gate"][0])
    A["w_f1u"] = slabs(i["w_up"][0])
    A["w_d1"] = slabs(i["w_down"][0])
    dr, dc, ok = bias_index()
    A["bias"] = np.where(ok[None], i["rpb_b"][0][:, dr, dc], f(-BIG)).astype(f)
    g = i["gla_w_in_2"][0]
    q, k, vv, r, gl = np.split(g, np.cumsum([512, 512, 1024, 1024]), axis=1)
    A["w_gq"], A["w_gk"], A["w_gv"], A["w_gr"] = slabs(q), slabs(k), slabs(vv), slabs(r)
    glp = np.zeros((1024, 128), f)
    glp[:, :16] = gl
    A["w_gl"] = slabs(glp)
    A["w_gate2"] = np.concatenate([i["gla_w_gate2_2"][0], i["gla_b_gate_2"]], 0)
    A["w_go"] = slabs(i["gla_w_out_2"][0])
    u = i["ffn_w_up_2"][0]
    A["w_f2g"], A["w_f2u"] = slabs(u[:, :2816]), slabs(u[:, 2816:])
    A["w_d2"] = slabs(i["ffn_w_down_2"][0])
    return A


def kernel(**inputs):
    import concourse.bacc as _bacc
    from concourse.bass_utils import run_bass_kernel_spmd as _run

    arrays = layout({k: np.asarray(v) for k, v in inputs.items()})
    nc = _bacc.Bacc("TRN2", target_bir_lowering=False, num_devices=1)
    T = {}
    for name, a in arrays.items():
        T[name] = nc.dram_tensor(f"in_{name}", a.shape, mybir.dt.from_np(a.dtype), kind="ExternalInput").ap()
    T["spill"] = nc.dram_tensor("spill", (8, 128, 1024), F).ap()
    out = nc.dram_tensor("out_0", (8, 128, 1024), F, kind="ExternalOutput").ap()
    build(nc, T, out)
    r = _run(nc, [{f"in_{n}": a for n, a in arrays.items()}], core_ids=[0])
    got = r.results[0]["out_0"]
    return np.ascontiguousarray(got.reshape(1024, 1024).T).reshape(1, 1024, 1024)
```

```python
from contextlib import ExitStack

import numpy as np

import concourse.bass as bass
from concourse import mybir

F = mybir.dt.float32
R = mybir.dt.float32r
BF = mybir.dt.bfloat16
ALU = mybir.AluOpType
ACT = mybir.ActivationFunctionType
AX = mybir.AxisListType.X
KB = 1024
BIG = 1.0e30

C_ID, C_ONE, C_BLK, C_PERM, C_SUF, C_DV, C_ML, C_MR = [128 * i for i in range(8)]
C_IND = 1024
C_EPS = 1026
C_N = 1032
V_BMOD, V_N1, V_QA, V_KA, V_QB, V_KB, V_ONA, V_ONB = 0, 48, 56, 57, 58, 59, 60, 64
V_N2, V_MIX, V_FFN, V_FIN, V_GLN, V_CW, V_CB = 68, 76, 84, 92, 100, 108, 240
V_N = 288
M_MOD, M_CMOD, M_G1, M_GC, M_QA, M_QB, M_G2, M_RAW = 0, 48, 64, 72, 80, 81, 82, 96
M_N = 144

DNG = [5, 5, 4, 4, 4]
NH = 22


def slab_plan():
    plan = [("mod", m) for m in range(16)]
    plan += [("in", m) for m in range(18)]
    plan += [("out", m) for m in range(8)]

    def ffn(gu, dn):
        out, h = [], 0
        order = ffn_order()
        for kind, a in order:
            if kind == "gu":
                out += [(gu + "g", a), (gu + "u", a)]
            else:
                out += [(dn, a * 8 + m) for m in range(8)]
        return out

    plan += ffn("f1", "d1")
    plan += [("gl", 0)] + [("gk", m) for m in range(4)] + [("gv", m) for m in range(8)]
    plan += [("gq", m) for m in range(4)] + [("gr", m) for m in range(8)]
    plan += [("go", m) for m in range(8)]
    plan += ffn("f2", "d2")
    return plan


def ffn_order():
    order, done, start = [], 0, 0
    for g, n in enumerate(DNG):
        while done < min(start + n + 1, NH):
            order.append(("gu", done))
            done += 1
        order.append(("dn", g))
        start += n
    return order


def activation(*a, **k):
    return lambda e: e.activation(*a, **k)

def matmul(*a, **k):
    return lambda e: e.matmul(*a, **k)

def memset(*a, **k):
    return lambda e: e.memset(*a, **k)

def reciprocal(*a, **k):
    return lambda e: e.reciprocal(*a, **k)

def scalar_tensor_tensor(*a, **k):
    return lambda e: e.scalar_tensor_tensor(*a, **k)

def tensor_copy(*a, **k):
    return lambda e: e.tensor_copy(*a, **k)

def tensor_reduce(*a, **k):
    return lambda e: e.tensor_reduce(*a, **k)

def tensor_scalar(*a, **k):
    return lambda e: e.tensor_scalar(*a, **k)

def tensor_tensor(*a, **k):
    return lambda e: e.tensor_tensor(*a, **k)

def tensor_tensor_reduce(*a, **k):
    return lambda e: e.tensor_tensor_reduce(*a, **k)

def transpose(*a, **k):
    return lambda e: e.transpose(*a, **k)


def build(nc, T, out):
    B0 = 16512
    names = {}

    def at(name, off, shape, dt):
        return nc.alloc_sbuf_tensor_at(name, shape, dt, offset=off)

    o = B0
    cst = at("cst", o, [128, C_N], F); o += C_N * 4
    vec = at("vec", o, [128, V_N], F); o += V_N * 4
    mv = at("mv", o, [128, M_N], F); o += M_N * 4
    idb = at("idb", o, [128, 128], BF); o += 256
    mlb = at("mlb", o, [128, 128], BF); o += 256
    mrb = at("mrb", o, [128, 128], BF); o += 256
    snk = at("snk", o, [128, 16], F); o += 64
    csl = at("csl", o, [128, 16], F); o += 64
    nmx = at("nmx", o, [128, 32], F); o += 128
    den = at("den", o, [128, 32], F); o += 128
    rdn = at("rdn", o, [128, 32], F); o += 128
    oss = at("oss", o, [128, 16], F); o += 64
    ors = at("ors", o, [128, 16], F); o += 64
    ege = at("ege", o, [128, 4, 16], F); o += 256
    dsn = at("dsn", o, [128, 32], F); o += 128
    o = (o + 31) // 32 * 32
    A_RAW, A_W = o, o + 12 * KB
    raw = at("raw", o, [128, 3, 1024], F); o += 12 * KB
    wh = at("wh", o, [128, 2, 8, 128], R); o += 8 * KB
    wl = at("wl", o, [128, 2, 8, 128], R); o += 8 * KB
    AH = o
    hh = at("hh", o, [128, 8, 1024], R); o += 32 * KB
    hl = at("hl", o, [128, 8, 1024], R); o += 32 * KB
    U = o

    with ExitStack() as ctx:
        sem = lambda n: ctx.enter_context(nc.semaphore(n))
        S = [ctx.enter_context(nc.psum_tensor(f"S{i}", [128, 1024], F)) for i in range(3)]
        M = [ctx.enter_context(nc.psum_tensor(f"M{i}", [128, 512], F)) for i in range(2)]

        class Queue:

            def __init__(self, name):
                self.name, self.sem, self.n, self.items, self.seen = name, sem("s_" + name), 0, [], {}

            def wait(self, *toks):
                for s, v in toks:
                    if self.seen.get(s.name, 0) < v:
                        self.seen[s.name] = v
                        self.items.append(lambda e, s=s, v=v: e.wait_ge(s, v))

            def run(self, f, *toks):
                self.wait(*toks)
                self.items.append(f)

            def op(self, f, *toks):
                self.wait(*toks)
                self.n += 1
                self.items.append(lambda e: f(e).then_inc(self.sem, 1))
                return (self.sem, self.n)

        pe, act, dve, pool, sp = (Queue(n) for n in ("pe", "act", "dve", "pool", "sp"))

        def load(s, n, dst, src, *toks):
            sp.run(lambda e: e.dma_start(dst, src).then_inc(s, 16), *toks)
            return (s, 16 * n)

        class Ring:

            def __init__(self, n):
                self.n, self.i, self.readers = n, 0, [()] * n

            def take(self):
                k = self.i % self.n
                self.i += 1
                return k, self.readers[k]

        slots = Ring(3)
        mslot = Ring(2)

        plan = slab_plan()
        s_raw = [sem(f"s_raw{i}") for i in range(3)]
        raw_free, w_free = {}, {}
        loaded, split = {}, {}
        cur = {"load": 0, "split": 0, "w": 0}
        raw_gate, w_gate = [], []

        def src_of(kind, m):
            if kind == "raw":
                return T["w_modT"][m], 1024
            if kind == "mod":
                return T["w_mod0"][m], 1024
            if kind in ("d1", "d2"):
                g = m // 8
                k0, k = sum(DNG[:g]), DNG[g]
                return T["w_" + kind][m % 8][:, 128 * k0:128 * (k0 + k)], 128 * k
            return T["w_" + kind][m], 1024

        def load_slab():
            i = cur["load"]
            if i >= (len(plan) if raw_gate else 34):
                return
            cur["load"] += 1
            src, n = src_of(*plan[i])
            j = i % 3
            loaded[i] = load(s_raw[j], i // 3 + 1, raw[:, j, 0:n], src, *(raw_free[i - 3] if i >= 3 else ()), *raw_gate)

        def split_slab():
            i = cur["split"]
            if i >= len(plan):
                return
            cur["split"] += 1
            if plan[i][0] in ("mod", "raw"):
                return
            n, j, k = src_of(*plan[i])[1], i % 3, cur["w"] % 2
            free = w_free.get(cur["w"] - 2, ()) + tuple(w_gate)
            cur["w"] += 1
            h = wh[:, k, :, :].rearrange("p a b -> p (a b)")[:, 0:n]
            l = wl[:, k, :, :].rearrange("p a b -> p (a b)")[:, 0:n]
            r = raw[:, j, 0:n]
            a = act.op(activation(h, r, ACT.Copy), loaded[i], *free)
            b = pool.op(tensor_tensor(l, r, h.bitcast(F), ALU.subtract), a, loaded[i], *free)
            raw_free[i] = (a, b)
            split[i] = (k, cur["w"] - 1, (a, b))
            load_slab()

        at_slab = {"i": 0, "hold": 34}

        def next_slab(kind):
            i = at_slab["i"]
            at_slab["i"] += 1
            assert plan[i][0] == kind, (plan[i], kind)
            if i >= at_slab["hold"]:
                at_slab["hold"] = len(plan)
            while cur["split"] < min(i + 2, at_slab["hold"]):
                split_slab()
            return split[i]

        def gemm(kind, kt, mm, hi, lo, toks, width=1024, ctx_act=None):
            k_, w_i, wt = next_slab(kind)
            j, free = slots.take()
            pe.wait(*wt)
            pe.wait(*free)
            if ctx_act is not None:
                jc, cfree = mslot.take()
                pe.wait(*cfree)
            for k in range(kt):
                pe.wait(*toks[k])
                wk, vk = wh[:, k_, k, 0:mm], wl[:, k_, k, 0:mm]
                for n, (w, x) in enumerate(((wk, hi), (wk, lo), (vk, hi))):
                    st, en = k == 0 and n == 0, k == kt - 1 and n == 2
                    for c in range(0, width, 512):
                        last = (matmul(
                            S[j][0:mm, c:c + 512], w, x[:, k, c:c + 512], start=st, stop=en))
                        if en and c == width - 512 and ctx_act is None:
                            tok = pe.op(last)
                        else:
                            pe.run(last)
                    if ctx_act is not None:
                        cx = ctx_act[0] if n != 1 else ctx_act[1]
                        f = (matmul(
                            M[jc][0:mm, 0:256], w, cx[:, k, :], start=st, stop=en))
                        if en:
                            tok = pe.op(f)
                        else:
                            pe.run(f)
            w_free[w_i] = (tok,)
            if ctx_act is not None:
                return j, jc, tok
            return j, tok

        s_c = sem("s_c")
        load(s_c, 1, cst[:, :], T["cst"])
        load(s_c, 2, vec[:, :], T["vec"])
        t_c = load(s_c, 3, csl[:, :], T["cc"])
        ID = cst[:, C_ID:C_ID + 128]
        EPS = cst[:, C_EPS:C_EPS + 1]

        hch = at("hch", U, [128, 8, 256], R)
        hcl = at("hcl", U + 8 * KB, [128, 8, 256], R)
        P_QB, P_KA, P_KB, P_V = U, U + 16 * KB, U + 21 * KB, U + 41 * KB
        P_QA, P_CS = U + 66 * KB, U + 82 * KB
        P_SQ, P_RS, P_RP, P_VT = U + 90 * KB, U + 95 * KB, U + 100 * KB, U + 100 * KB
        qb = at("qb", P_QB, [128, 4, 1024], F)
        ka = at("ka", P_KA, [128, 1280], F)
        kb = at("kb", P_KB, [128, 4, 1280], F)
        vv = at("vv", P_V, [128, 10, 640], F)
        qa = at("qa", P_QA, [128, 4, 1024], F)
        cs = at("cs", P_CS, [128, 2, 1024], F)
        sq = at("sq", P_SQ, [128, 1280], F)
        rs = at("rs", P_RS, [128, 1280], F)
        rp = at("rp", P_RP, [128, 1024], F)
        vt = at("vt", P_VT, [128, 1280], F)
        xw = at("xw", P_V, [128, 8, 1280], F)
        xq = at("xq", P_KA, [128, 3, 1280], F)

        s_xw = [sem(f"s_xw{i}") for i in range(8)]
        t_xw = []
        for k in range(8):
            t_xw.append(load(s_xw[k], 1, xw[:, k, :], T["xT"][k]))
            if k in (1, 3, 5):
                load_slab()
        t_cs = load(sem("s_cs"), 1, cs[:, :, :], T["cs"])

        t_sil = act.op(activation(csl[:, :], csl[:, :], ACT.Silu), t_c)
        t_idb = act.op(activation(idb[:, :], ID, ACT.Copy))
        act.op(activation(mlb[:, :], cst[:, C_ML:C_ML + 128], ACT.Copy))
        t_msk = act.op(activation(mrb[:, :], cst[:, C_MR:C_MR + 128], ACT.Copy))
        dve.op(tensor_scalar(mv[:, M_QA:M_QA + 1], vec[:, V_QA:V_QA + 1], -0.125, None, ALU.mult), t_c)
        t_qg = dve.op(tensor_scalar(mv[:, M_QB:M_QB + 1], vec[:, V_QB:V_QB + 1], -0.125, None, ALU.mult))

        xqr = Ring(3)
        j, _ = slots.take()
        jc, _ = mslot.take()
        for k in range(8):
            a, free = xqr.take()
            t = act.op(activation(xq[:, a, :], xw[:, k, :], ACT.Square), t_xw[k], *free)
            pe.wait(t, t_c)
            for c, d in ((0, S[j][:, 0:512]), (512, S[j][:, 512:1024]), (1024, M[jc][:, 0:256])):
                f = (matmul(
                    d, cst[:, C_ONE:C_ONE + 128], xq[:, a, c:c + min(512, 1280 - c)], start=k == 0, stop=k == 7))
                if c == 1024:
                    t_ms = pe.op(f)
                else:
                    pe.run(f)
            xqr.readers[a] = (t_ms,)
        act.op(activation(rs[:, 0:1024], S[j][:, :], ACT.Ln, bias=EPS), t_ms)
        t = act.op(activation(rs[:, 1024:1280], M[jc][:, 0:256], ACT.Ln, bias=EPS))
        slots.readers[j] = mslot.readers[jc] = (t,)
        t_rs = act.op(activation(rs[:, :], rs[:, :], ACT.Exp, scale=-0.5), t)
        t_xr = []
        for k in range(8):
            eng = pool if k % 2 else dve
            t_xr.append(eng.op(tensor_tensor(xw[:, k, :], xw[:, k, :], rs[:, :], ALU.mult), t_rs, t_xw[k]))

        jm, mfree = mslot.take()
        pe.wait(t_sil, *mfree)
        for m in range(16):
            while cur["split"] <= m:
                split_slab()
            for k in range(8):
                f = (matmul(
                    M[jm][:, 2 * m:2 * m + 2], raw[:, m % 3, 128 * k:128 * k + 128], csl[:, 2 * k:2 * k + 2],
                    start=k == 0, stop=k == 7))
                pe.wait(loaded[m])
                if k == 7:
                    t = pe.op(f)
                else:
                    pe.run(f)
            raw_free[m] = (t,)
            load_slab()
        at_slab["i"] = 16
        mp = M[jm][:, 0:32].rearrange("p (m c) -> p c m", c=2)
        t1 = dve.op(tensor_tensor(mv[:, M_MOD:M_MOD + 16], mp[:, 0, :], vec[:, V_BMOD:V_BMOD + 16], ALU.add), t)
        t2 = dve.op(tensor_tensor(mv[:, M_CMOD:M_CMOD + 16], mp[:, 1, :], vec[:, V_BMOD:V_BMOD + 16], ALU.add))
        mslot.readers[jm] = (t1, t2)
        t1 = dve.op(scalar_tensor_tensor(mv[:, M_G1:M_G1 + 8], mv[:, M_MOD + 8:M_MOD + 16], 1.0,
                                                     vec[:, V_N1:V_N1 + 8], ALU.add, ALU.mult), t2)
        t_g = dve.op(scalar_tensor_tensor(mv[:, M_GC:M_GC + 8], mv[:, M_CMOD + 8:M_CMOD + 16], 1.0,
                                                      vec[:, V_N1:V_N1 + 8], ALU.add, ALU.mult), t1)
        t_h = []
        for k in range(8):
            xk = xw[:, k, :]
            ta = act.op(activation(xk[:, 0:1024], xk[:, 0:1024], ACT.Identity,
                        bias=mv[:, M_MOD + k:M_MOD + k + 1], scale=mv[:, M_G1 + k:M_G1 + k + 1]), t_g, t_xr[k])
            tb = act.op(activation(xk[:, 1024:1280], xk[:, 1024:1280], ACT.Identity,
                        bias=mv[:, M_CMOD + k:M_CMOD + k + 1], scale=mv[:, M_GC + k:M_GC + k + 1]))
            dve.op(tensor_copy(hh[:, k, :], xk[:, 0:1024]), tb)
            tc_ = dve.op(tensor_copy(hch[:, k, :], xk[:, 1024:1280]))
            td = pool.op(tensor_tensor(hl[:, k, :], xk[:, 0:1024], hh[:, k, :].bitcast(F), ALU.subtract), tc_, tb)
            te = dve.op(tensor_tensor(hcl[:, k, :], xk[:, 1024:1280], hch[:, k, :].bitcast(F), ALU.subtract), tc_)
            t_h.append((te, td))

        units = [("k", ka[:, :], vec[:, V_KA:V_KA + 1], True)]
        units += [("k", kb[:, m, :], vec[:, V_KB:V_KB + 1], False) for m in range(4)]
        units += [("v", m, None, False) for m in range(5)]
        units += [("q", qa[:, m, :], mv[:, M_QA:M_QA + 1], True) for m in range(4)]
        units += [("q", qb[:, m, :], mv[:, M_QB:M_QB + 1], False) for m in range(4)]
        t_ready = {}
        free_sq, free_vt, free_rp = [()], [()], [()]
        st = {}

        def stage0(u):
            kind, dst, g, rope = units[u]
            cx = kind != "q"
            if cx:
                j, jc, t = gemm("in", 8, 128, hh, hl, t_h, ctx_act=(hch, hcl))
            else:
                j, t = gemm("in", 8, 128, hh, hl, t_h)
                jc = None
            w = 1280 if cx else 1024
            if kind == "v":
                d = (sq if dst % 2 else vt)[:, :]
                dve.wait(*free_vt[0], *free_rp[0], *free_sq[0])
            else:
                d = dst
            if u == len(units) - 4:
                st["ctx_done"] = t
            tt = dve.op(tensor_copy(d[:, 0:1024], S[j][:, :]), t)
            slots.readers[j] = (tt,)
            if cx:
                tt = dve.op(tensor_copy(d[:, 1024:1280], M[jc][:, 0:256]))
                mslot.readers[jc] = (tt,)
            st[u] = tt

        def stage1(u):
            kind, dst, g, rope = units[u]
            j, free = slots.take()
            cx = kind != "q"
            if cx:
                jc, cfree = mslot.take()
                pe.wait(*cfree)
            pe.wait(*free)
            if kind == "v":
                pe.wait(st[u])
                src = sq if dst % 2 else vt
                for i in range(10):
                    d = S[j][:, 128 * i:128 * i + 128] if i < 8 else M[jc][:, 128 * (i - 8):128 * (i - 7)]
                    f = transpose(d, src[:, 128 * i:128 * i + 128], ID)
                    if i == 9:
                        t = pe.op(f)
                    else:
                        pe.run(f)
                if dst % 2:
                    free_sq[0] = (t,)
                else:
                    free_vt[0] = (t,)
                c = 128 * dst
                act.op(activation(vv[:, 0:8, c:c + 128], S[j][:, :].rearrange("p (a b) -> p a b", b=128), ACT.Copy), t)
                tt = act.op(activation(vv[:, 8:10, c:c + 128], M[jc][:, 0:256].rearrange("p (a b) -> p a b", b=128), ACT.Copy))
                slots.readers[j] = mslot.readers[jc] = (tt,)
                t_ready[u] = (tt,)
                return
            w = 1280 if cx else 1024
            t = act.op(activation(sq[:, 0:w], dst[:, 0:w], ACT.Square), st[u], *free_sq[0])
            pe.wait(t)
            blk = cst[:, C_BLK:C_BLK + 128]
            pe.run(matmul(S[j][:, 0:512], blk, sq[:, 0:512], start=True, stop=True))
            f = matmul(S[j][:, 512:1024], blk, sq[:, 512:1024], start=True, stop=True)
            if cx:
                pe.run(f)
                t = pe.op(matmul(M[jc][:, 0:256], blk, sq[:, 1024:1280], start=True, stop=True))
            else:
                t = pe.op(f)
            free_sq[0] = (t,)
            w = 1280 if cx else 1024
            tt = act.op(activation(rs[:, 0:1024], S[j][:, :], ACT.Ln, bias=EPS), t, *st.get("rs_free", ()))
            slots.readers[j] = (tt,)
            if cx:
                tt = act.op(activation(rs[:, 1024:1280], M[jc][:, 0:256], ACT.Ln, bias=EPS))
                mslot.readers[jc] = (tt,)
            tt = act.op(activation(rs[:, 0:w], rs[:, 0:w], ACT.Exp, scale=-0.5), tt)
            tt = dve.op(scalar_tensor_tensor(dst[:, 0:w], dst[:, 0:w], g, rs[:, 0:w], ALU.mult, ALU.mult), tt, t_qg, st[u])
            st["rs_free"] = (tt,)
            st[u, "n"] = tt
            t_ready[u] = (tt,)

        def stage2(u):
            kind, dst, g, rope = units[u]
            if not rope:
                return
            j, free = slots.take()
            pe.wait(st[u, "n"], *free)
            pm = cst[:, C_PERM:C_PERM + 128]
            pe.run(matmul(S[j][:, 0:512], pm, dst[:, 0:512], start=True, stop=True))
            t = pe.op(matmul(S[j][:, 512:1024], pm, dst[:, 512:1024], start=True, stop=True))
            ta = dve.op(tensor_tensor(rp[:, :], S[j][:, :], cs[:, 1, :], ALU.mult), t, t_cs, *free_rp[0], *free_vt[0])
            slots.readers[j] = (ta,)
            tb = pool.op(tensor_tensor(dst[:, 0:1024], dst[:, 0:1024], cs[:, 0, :], ALU.mult), t, t_cs, st[u, "n"])
            tb = pool.op(tensor_tensor(dst[:, 0:1024], dst[:, 0:1024], rp[:, :], ALU.add), ta, tb)
            free_rp[0] = (tb,)
            t_ready[u] = (tb,)

        nu = len(units)
        for s in range(nu + 2):
            if s < nu:
                stage0(s)
            if 1 <= s <= nu:
                stage1(s - 1)
            if s >= 2:
                stage2(s - 2)

        pp = at("pp", AH, [128, 3, 896], F)
        pth = at("pth", AH + 11 * KB, [128, 2, 7, 128], R)
        ptl = at("ptl", AH + 18 * KB, [128, 2, 7, 128], R)
        qs = at("qs", AH + 25 * KB, [128, 2, 1024], R)
        qx = at("qx", AH + 33 * KB, [128, 1024], R)
        kh = at("kh", AH + 41 * KB, [128, 2, 1280], R)
        kl = at("kl", AH + 51 * KB, [128, 2, 1280], R)
        ohl = at("ohl", AH + 61 * KB, [128, 2, 4, 64], F)
        vh = at("vh", U + 98 * KB, [128, 2, 10, 128], R)
        bt = at("bt", A_RAW, [128, 2, 1472], F)
        cb = at("cb", A_W, [128, 1024], F)
        mr = at("mr", A_W + 4 * KB, [128, 3, 1024], F)
        oa = at("oa", P_CS, [128, 8, 512], F)
        ob = at("ob", P_QA, [128, 8, 512], F)
        p1 = (st[nu - 1], *st["rs_free"], *free_sq[0], *free_vt[0], *free_rp[0])
        t_cb = load(sem("s_cb"), 1, cb[:, :], T["c_row"].to_broadcast([128, 1024]), *p1)
        t_sk = load(sem("s_sk"), 1, snk[:, 0:8], T["sink"].to_broadcast([128, 8]))
        t_cbs = act.op(activation(cb[:, :], cb[:, :], ACT.Silu), t_cb)
        t_snk = act.op(activation(snk[:, 8:16], snk[:, 0:8], ACT.Copy, scale=-1.0), t_sk)
        s_mr = [sem(f"s_mr{i}") for i in range(3)]
        mr_free, t_mods = {}, []

        def mod_load(n):
            if n < 32:
                st["mr", n] = load(s_mr[n % 3], n // 3 + 1, mr[:, n % 3, :], T["w_modT"][n], *p1,
                                   *mr_free.get(n - 3, ()))

        def mod_col(n, half):
            r, c = slice(512 * half, 512 * half + 512), mv[:, M_RAW + 16 + n:M_RAW + 17 + n]
            t = dve.op(tensor_tensor_reduce(mr[:, n % 3, r], mr[:, n % 3, r], cb[:, r], 1.0, c if half else 0.0,
                       ALU.mult, ALU.add, c), st["mr", n], t_cbs)
            if half:
                mr_free[n] = (t,)
                t_mods.append(t)
                mod_load(n + 3)

        s_bt = [sem("s_bt0"), sem("s_bt1")]
        bt_free, t_bt = {}, {}

        def bias_table(h):
            t_bt[h] = load(s_bt[h % 2], h // 2 + 1, bt[:, h % 2, :], T["bias"][h], *p1, *bt_free.get(h - 2, ()))

        def bias_neg(h):
            t_bt[h] = act.op(activation(bt[:, h % 2, :], bt[:, h % 2, :], ACT.Copy, scale=-1.0), t_bt[h])

        heads = []
        for p in range(4):
            heads += [("a", p, p), ("a", p + 4, p)]
        for p in range(4):
            heads += [("b", 2 * p, p + 4), ("b", 2 * p + 1, p + 4)]
        start = [0, 0, 0, 128, 256, 384, 512, 512]
        size = [512, 512, 576, 576, 576, 576, 512, 512]
        bcol = [6 * 64, 4 * 64, 896, 896, 896, 896, 2 * 64, 0]
        items = []
        for n, (kind, h, p) in enumerate(heads):
            for b in range(8):
                if kind == "a":
                    b0, b1 = max(b - 1, 0), min(b + 1, 7)
                    items.append((n, kind, h, p, b, 128 * b0, 128 * (b1 - b0 + 1)))
                else:
                    items.append((n, kind, h, p, b, start[b], size[b]))

        srd, ptr, pring, ptring = Ring(2), Ring(2), Ring(3), Ring(2)
        srd.readers = [slots.readers[0], slots.readers[1]]
        banks = [S[2][:, 0:512], S[2][:, 512:1024]]
        ptr.readers = [slots.readers[2], slots.readers[2]]
        o_free = [mslot.readers[0], mslot.readers[1]]
        it = {}
        q_rd, v_rd, t_qk, t_vh = {}, {}, {}, {}

        s_hd = [sem("s_hd0"), sem("s_hd1")]
        n_hd = [0, 0]

        def halves(n):
            return slice(64 * (n % 2), 64 * (n % 2) + 64), slice(64 - 64 * (n % 2), 128 - 64 * (n % 2))

        def prep_head(n):
            kind, h, p = heads[n]
            z = n % 2
            own, other = halves(n)
            src, u = (qa[:, p, :], 10 + p) if p < 4 else (qb[:, p - 4, :], 10 + p)
            free = q_rd.get(z, ())
            first = n < 2
            ta = act.op(activation(qs[own, z, :], src[own, :], ACT.Copy), *t_ready[u], *p1, *free)
            lo = dve if first else pool
            tb = lo.op(tensor_tensor(qx[own, :], src[own, :], qs[own, z, :].bitcast(F), ALU.subtract),
                       ta, *t_ready[u], *p1, *free, (pool.sem, pool.n))
            n_hd[z] += 1
            t = load(s_hd[z], n_hd[z], qs[other, z, :].bitcast(F), qx[own, :].bitcast(F), tb)
            if n < 2 or kind == "b":
                k, u = (ka[:, :], 0) if kind == "a" else (kb[:, p - 4, :], p - 3)
                ta = act.op(activation(kh[own, z, :], k[own, :], ACT.Copy), *t_ready[u], *p1, *free)
                tb = lo.op(tensor_tensor(kl[own, z, :], k[own, :], kh[own, z, :].bitcast(F), ALU.subtract),
                           ta, *t_ready[u], *p1, *free, (pool.sem, pool.n))
                load(s_hd[z], n_hd[z] + 1, kh[other, z, :].bitcast(F), kh[own, z, :].bitcast(F), ta)
                n_hd[z] += 2
                t = load(s_hd[z], n_hd[z], kl[other, z, :].bitcast(F), kl[own, z, :].bitcast(F), tb)
            t_qk[n] = (t, tb)
            if not first:
                pool.wait(tb)

        def keep_warm(n):
            bk, free = ptr.take()
            pe.wait(t_msk, *free)
            for _ in range(n):
                t = pe.op(matmul(banks[bk], idb[:, :], mlb[:, :].unsqueeze(1).to_broadcast([128, 4, 128]), start=True, stop=True))
            ptr.readers[bk] = (t,)

        def prep_v(n):
            z = n % 2
            c = 64 * n if n < 2 else 128 + 64 * (n - 8)
            u = 5 if n < 2 else 6 + (n - 8) // 2
            free = v_rd.get(z, ())
            v = vv[:, :, c:c + 64]
            h_, l_ = vh[:, z, :, 0:64], vh[:, z, :, 64:128]
            ta = act.op(activation(h_, v, ACT.Copy), *t_ready[u], *p1, *free)
            tb = pool.op(tensor_tensor(l_, v, h_.bitcast(F), ALU.subtract), ta, *t_ready[u], *p1, *free)
            t_vh[z, n >= 8] = (ta, tb)

        def qk(i):
            n, kind, h, p, b, k0, L = items[i]
            s_, free = srd.take()
            D = S[s_]
            z = n % 2
            Q = qs[:, z, 128 * b:128 * b + 128]
            pe.wait(*t_qk[n], t_msk, *free)
            w = 256 + L
            parts = [(0, 256, 1024, None)]
            n1 = min(256, L)
            if kind == "a":
                m = (256, mlb) if b > 0 else (384, mrb)
                parts.append((256, 256 + n1, k0, m))
                if L > 256:
                    parts.append((512, w, k0 + 256, (512, mrb)))
            else:
                parts += [(256, 512, k0, None), (512, w, k0 + 256, None)]
            for c0, c1, kc, m in parts:
                for x, K in enumerate((kh, kl)):
                    f = matmul(D[:, c0:c1], Q, K[:, z, kc:kc + c1 - c0], start=x == 0, stop=x == 1 and m is None)
                    if c1 == w and x == 1 and m is None:
                        t = pe.op(f)
                    else:
                        pe.run(f)
                if m is not None:
                    f = matmul(D[:, m[0]:m[0] + 128], idb[:, :], m[1][:, :], start=False, stop=True)
                    if c1 == w:
                        t = pe.op(f)
                    else:
                        pe.run(f)
            q_rd[z] = (t,)
            col = b + 8 * (n % 4)
            nm = nmx[:, col:col + 1]
            old = it.get(("col", col), ())
            if kind == "a":
                t = dve.op(tensor_reduce(nm, D[:, 0:w], AX, ALU.min), t, *old)
                t = dve.op(tensor_scalar(nm, nm, snk[:, 8 + h:9 + h], None, ALU.min), t, t_snk)
            else:
                bc = bcol[b]
                t = dve.op(tensor_reduce(nm, D[:, 0:256], AX, ALU.min), t, *old)
                t = dve.op(tensor_tensor_reduce(D[:, 256:w], D[:, 256:w], bt[:, h % 2, bc:bc + L], 1.0, nm,
                           ALU.add, ALU.min, nm), t, t_bt[h])
                bt_free[h] = (t,)
            it[i] = (s_, w, t, col, old)

        def ex(i):
            s_, w, t, col, old = it[i]
            D, nm = S[s_], nmx[:, col:col + 1]
            pk, pfree = pring.take()
            t = act.op(activation(pp[:, pk, 0:w], D[:, 0:w], ACT.Exp, bias=nm, scale=-1.0,
                       accum_out=den[:, col:col + 1]), t, *pfree, *old)
            srd.readers[s_] = (t,)
            it[i] = (pk, t)

        def tr(i):
            n, kind, h, p, b, k0, L = items[i]
            pk, t = it[i]
            pe.wait(t)
            nt = (256 + L + 127) // 128
            tk, tfree = ptring.take()
            toks = []
            for half in range(2):
                tiles = list(range(4 * half, min(4 * half + 4, nt)))
                if not tiles:
                    continue
                bk, free = ptr.take()
                pe.wait(*free)
                for x in tiles:
                    f = transpose(banks[bk][:, 128 * (x - 4 * half):128 * (x - 4 * half) + 128],
                                  pp[:, pk, 128 * x:128 * x + 128], ID)
                    if x == tiles[-1]:
                        tp = pe.op(f)
                    else:
                        pe.run(f)
                pring.readers[pk] = (tp,)
                src = banks[bk][:, 0:128 * len(tiles)]
                H, Lo = (y[:, tk, 4 * half:4 * half + len(tiles), :].rearrange("p a b -> p (a b)") for y in (pth, ptl))
                ta = act.op(activation(H, src, ACT.Copy), tp, *tfree)
                tb = dve.op(tensor_tensor(Lo, src, H.bitcast(F), ALU.subtract), tp, ta, *tfree)
                toks += [ta, tb]
                ptr.readers[bk] = (ta, tb)
            it[i, "t"] = (tk, toks, nt)

        def av(i):
            n, kind, h, p, b, k0, L = items[i]
            tk, toks, nt = it[i, "t"]
            ok = b // 4
            pe.wait(*toks)
            if b % 4 == 0:
                pe.wait(*o_free[ok], *t_vh[n % 2, kind == "b"])
            tiles = [8, 9] + [k0 // 128 + x for x in range(nt - 2)]
            O = M[ok][:, 128 * (b % 4):128 * (b % 4) + 128]
            for x, v in enumerate(tiles):
                V = vh[:, n % 2, v, :]
                pe.run(matmul(O, pth[:, tk, x, :], V, start=x == 0, stop=False))
                f = matmul(O, ptl[:, tk, x, :], V, start=False, stop=x == nt - 1)
                if x == nt - 1:
                    t = pe.op(f)
                else:
                    pe.run(f)
            ptring.readers[tk] = (t,)
            v_rd[n % 2] = (t,)
            if b % 4 == 3:
                c = 8 * (n % 4) + 4 * ok
                dst = (oa if kind == "a" else ob)[:, 4 * ok:4 * ok + 4, 64 * h:64 * h + 64]
                dc = den[:, c:c + 4]
                if kind == "a":
                    te = act.op(activation(dsn[:, c:c + 4], nmx[:, c:c + 4], ACT.Exp, bias=snk[:, h:h + 1]), it[i][1], t_sk)
                    te = dve.op(tensor_tensor(dc, dc, dsn[:, c:c + 4], ALU.add), te)
                else:
                    te = it[i][1]
                r = dve.op(reciprocal(rdn[:, c:c + 4], dc), te)
                R4 = rdn[:, c:c + 4].unsqueeze(2).to_broadcast([128, 4, 64])
                O4 = M[ok][:, :].rearrange("p (a b) -> p a b", b=128)
                ta = dve.op(tensor_tensor(dst, O4[:, :, 0:64], R4, ALU.mult), t, r, *p1)
                tb = dve.op(tensor_tensor(ohl[:, ok, :, :], O4[:, :, 64:128], R4, ALU.mult), *it.get(("ohl", ok), ()))
                o_free[ok] = (tb,)
                tb = pool.op(tensor_tensor(dst, dst, ohl[:, ok, :, :], ALU.add), ta, tb)
                it["ohl", ok] = (tb,)
                for x in range(4):
                    it["col", c + x] = (r,)
                it[kind, "o"] = tb

        t_pz = dve.op(memset(pp[:, :, 832:896], 0.0), *p1)
        pe.wait(t_pz)
        bias_table(0)
        bias_table(1)
        for n in range(3):
            mod_load(n)
        prep_head(0)
        prep_head(1)
        prep_v(0)
        prep_v(1)
        NI = len(items)
        keep_warm(60)
        for i in range(NI + 2):
            if i < NI:
                n, kind, h, p, b = items[i][:5]
                if kind == "b" and b == 0:
                    bias_neg(h)
                qk(i)
                if b == 7 and kind == "b" and h + 2 < 8:
                    bias_table(h + 2)
                if b == 1 and 1 <= n < 15:
                    prep_head(n + 1)
                if b == 4 and 7 <= n < 15:
                    prep_v(n + 1)
            if 1 <= i < 4:
                keep_warm(8)
            if 1 <= i <= NI:
                tr(i - 1)
            if i < NI:
                ex(i)
            if i >= 2:
                av(i - 2)
            if i % 2 == 1 and i < 128:
                mod_col(i // 4, i // 2 % 2)
            if i == NI - 1:
                raw_extra = bt_free[6] + bt_free[7]
        raw_gate.extend(raw_extra)
        w_gate.extend([t_mods[-1], t_cbs])
        for _ in range(3):
            load_slab()
        t = dve.op(tensor_tensor(mv[:, M_MOD + 16:M_MOD + 48], mv[:, M_RAW + 16:M_RAW + 48],
                   vec[:, V_BMOD + 16:V_BMOD + 48], ALU.add), t_mods[-1])
        t_mod = dve.op(scalar_tensor_tensor(mv[:, M_G2:M_G2 + 8], mv[:, M_MOD + 32:M_MOD + 40], 1.0,
                       vec[:, V_N2:V_N2 + 8], ALU.add, ALU.mult), t)

        xt = at("xt", U, [128, 8, 1024], F)
        x2 = at("x2", U + 32 * KB, [128, 1024], F)
        sqt = at("sqt", U + 36 * KB, [128, 2, 1024], F)
        rs2 = at("rs2", U + 44 * KB, [128, 1024], F)
        tt_ = at("tt_", U + 48 * KB, [128, 3, 1024], F)
        s_xt = [sem(f"s_xt{i}") for i in range(8)]
        att_done = (it["b", "o"], (pe.sem, pe.n))
        t_xt = [(load(s_xt[k], 1, xt[:, k, :], T["xT"][k][:, 0:1024], *att_done),) for k in range(8)]
        osq = at("osq", U + 32 * KB, [128, 512], F)
        slots.readers = [srd.readers[0], srd.readers[1], ptr.readers[0] + ptr.readers[1]]
        mslot.readers = [o_free[0], o_free[1]]

        for n, buf in enumerate((oa, ob)):
            for b in range(8):
                c = 8 * n + b
                t = act.op(activation(osq[:, :], buf[:, b, :], ACT.Square,
                           accum_out=oss[:, c:c + 1]), it["ab"[n], "o"], *att_done, (act.sem, act.n))
        t = act.op(activation(ors[:, :], oss[:, :], ACT.Ln, bias=EPS, scale=1.0 / 512), t)
        t_or = act.op(activation(ors[:, :], ors[:, :], ACT.Exp, scale=-0.5), t)
        t_on = []
        for n, buf in enumerate((oa, ob)):
            for b in range(8):
                eng = dve if b % 2 else pool
                t_on.append(eng.op(tensor_scalar(buf[:, b, :], buf[:, b, :],
                            ors[:, 8 * n + b:8 * n + b + 1], None, ALU.mult), t_or))
        t_h = [[] for _ in range(8)]
        for n, buf in enumerate((oa, ob)):
            for f_ in range(4):
                j, free = slots.take()
                pe.wait(*free)
                for b in range(8):
                    pe.wait(t_on[8 * n + b])
                    f = transpose(S[j][:, 128 * b:128 * b + 128],
                                                                        buf[:, b, 128 * f_:128 * f_ + 128], ID)
                    if b == 7:
                        t = pe.op(f)
                    else:
                        pe.run(f)
                k = 4 * n + f_
                g = vec[:, V_ONA + k:V_ONA + k + 1]
                ta = act.op(activation(hh[:, k, :], S[j][:, :], ACT.Copy, scale=g), t, *att_done)
                tb = dve.op(scalar_tensor_tensor(hl[:, k, :], S[j][:, :], g,
                            hh[:, k, :].bitcast(F), ALU.mult, ALU.subtract), ta, *att_done)
                slots.readers[j] = (ta, tb)
                t_h[k] = (ta, tb)

        sqr = Ring(2)
        x2s = {"tok": (), "free": ()}

        def square(k, tok, X):
            a, free = sqr.take()
            t = act.op(activation(sqt[:, a, :], X[:, k, :], ACT.Square), *tok, *free, *x2s.get("ovl", ()))
            if k == 0:
                t = pool.op(tensor_copy(x2[:, :], sqt[:, a, :]), t, *x2s["free"])
            else:
                t = pool.op(tensor_tensor(x2[:, :], x2[:, :], sqt[:, a, :], ALU.add), t, *x2s["tok"])
            sqr.readers[a] = (t,)
            x2s["tok"] = (t,)

        def rstd():
            j, free = slots.take()
            pe.wait(*free, *x2s["tok"])
            one = cst[:, C_ONE:C_ONE + 128]
            pe.run(matmul(S[j][:, 0:512], one, x2[:, 0:512], start=True, stop=True))
            t = pe.op(matmul(S[j][:, 512:1024], one, x2[:, 512:1024], start=True, stop=True))
            x2s["free"] = (t,)
            t = act.op(activation(rs2[:, :], S[j][:, :], ACT.Ln, bias=EPS), t)
            slots.readers[j] = (t,)
            return act.op(activation(rs2[:, :], rs2[:, :], ACT.Exp, scale=-0.5), t)

        ttr = Ring(3)

        def normed(G, SH, toks):
            t_rs = rstd()
            out_ = []
            for k in range(8):
                a, free = ttr.take()
                y = tt_[:, a, :]
                g = G[:, k:k + 1]
                t = pool.op(tensor_tensor(y, xt[:, k, :], rs2[:, :], ALU.mult), t_rs, *toks[k], *free)
                if SH is None:
                    t = act.op(activation(y, y, ACT.Copy, scale=g), t)
                else:
                    s = SH[:, k:k + 1]
                    t = act.op(activation(y, y, ACT.Identity, scale=g, bias=s), t)
                ta = dve.op(tensor_copy(hh[:, k, :], y), t)
                tb = dve.op(tensor_tensor(hl[:, k, :], y, hh[:, k, :].bitcast(F), ALU.subtract), ta)
                ttr.readers[a] = (tb,)
                out_.append((ta, tb))
            return out_

        def residual(k, j, t, gate, sq_last):
            f = (scalar_tensor_tensor(xt[:, k, :], S[j][:, :], gate, xt[:, k, :], ALU.mult, ALU.add)) \
                if gate is not None else (tensor_tensor(xt[:, k, :], S[j][:, :], xt[:, k, :], ALU.add))
            t = dve.op(f, t, t_mod, *t_xt[k])
            slots.readers[j] = (t,)
            t_xt[k] = (t,)
            if sq_last:
                square(k, (t,), xt)

        x2s["ovl"] = tuple(t_on)
        sqr.readers = [(t_or,)] * 2
        for m in range(8):
            j, t = gemm("out", 8, 128, hh, hl, t_h)
            residual(m, j, t, mv[:, M_MOD + 16 + m:M_MOD + 17 + m], True)

        fh = at("fh", U + 60 * KB, [128, 6, 1024], R)
        fl = at("fl", U + 84 * KB, [128, 6, 1024], R)
        sg = at("sg", U + 44 * KB, [128, 2, 1024], F)
        pr = at("pr", U + 52 * KB, [128, 2, 1024], F)
        hid_free = {}
        hid = {}

        def emit_hidden(j_, y, ty, r, ring_k):
            q = j_ % 6
            ta = dve.op(tensor_copy(fh[:, q, :], y), ty, *hid_free.get(j_ - 6, ()))
            tb = pool.op(tensor_tensor(fl[:, q, :], y, fh[:, q, :].bitcast(F), ALU.subtract), ty, ta)
            hid[j_] = (ta, tb)
            return tb

        def down(kind, g, gate, final):
            k0, n = sum(DNG[:g]), DNG[g]
            for m in range(8):
                k_, w_i, wt = next_slab(kind)
                j, free = slots.take()
                pe.wait(*wt, *free)
                for k in range(n):
                    q = (k0 + k) % 6
                    pe.wait(*hid[k0 + k])
                    for i_, (w, x) in enumerate(((wh, fh), (wh, fl), (wl, fh))):
                        stt, en = k == 0 and i_ == 0, k == n - 1 and i_ == 2
                        for c in (0, 512):
                            f = (matmul(
                                S[j][:, c:c + 512], w[:, k_, k, :], x[:, q, c:c + 512], start=stt, stop=en))
                            if en and c:
                                t = pe.op(f)
                            else:
                                pe.run(f)
                w_free[w_i] = (t,)
                gt = gate[:, m:m + 1] if gate is not None else None
                residual(m, j, t, gt, final)
            for k in range(n):
                hid_free[k0 + k] = (t,)

        t_h = normed(mv[:, M_G2:M_G2 + 8], mv[:, M_MOD + 24:M_MOD + 32], t_xt)
        sgr, prr = Ring(2), Ring(2)
        sgr.readers = prr.readers = None
        sgr.readers, prr.readers = [t_h[-1]] * 2, [t_h[-1]] * 2
        x2s["ovl"] = ()
        for kind, a in ffn_order():
            if kind == "gu":
                jg, tg = gemm("f1g", 8, 128, hh, hl, t_h)
                s_, free = sgr.take()
                p_, pfree = prr.take()
                t = act.op(activation(sg[:, s_, :], S[jg][:, :], ACT.Silu), tg, *free)
                slots.readers[jg] = (t,)
                ju, tu = gemm("f1u", 8, 128, hh, hl, t_h)
                t = dve.op(tensor_tensor(pr[:, p_, :], sg[:, s_, :], S[ju][:, :], ALU.mult), t, tu, *pfree)
                slots.readers[ju] = (t,)
                sgr.readers[s_] = (t,)
                tb = emit_hidden(a, pr[:, p_, :], t, None, None)
                prr.readers[p_] = (tb,)
            else:
                down("d1", a, mv[:, M_MOD + 40:M_MOD + 48], a == len(DNG) - 1)

        ttr.readers = [prr.readers[0] + prr.readers[1] + sgr.readers[0] + sgr.readers[1]] * 3
        s_sp = sem("s_spill")
        for k in range(8):
            t_sp = load(s_sp, k + 1, T["spill"][k], xt[:, k, :], *t_xt[k])
        act.wait(*ttr.readers[0])
        t_h = normed(vec[:, V_MIX:V_MIX + 8], None, t_xt)
        vo = at("vo", U, [128, 4, 8, 256], F)
        gq = at("gq", U + 32 * KB, [128, 4, 1024], F)
        gd = at("gd", U + 48 * KB, [128, 8, 512], F)
        gst = at("gst", U + 64 * KB, [128, 8, 256], F)
        gt2 = at("gt2", U + 72 * KB, [128, 2, 1024], F)
        gsq = at("gsq", U + 80 * KB, [128, 1024], F)
        grs = at("grs", U + 84 * KB, [128, 1024], F)
        gz = at("gz", U + 88 * KB, [128, 2, 512], F)
        ge = at("ge", U + 92 * KB, [128, 2, 512], F)
        glr = at("glr", U + 96 * KB, [32, 1024], F)
        wg2 = at("wg2", U + 100 * KB, [32, 512], F)
        ffn_done = tuple(hid_free[21])
        t_w2 = load(sem("s_w2"), 1, wg2[0:17, :], T["w_gate2"], *ffn_done)
        t_gl1 = dve.op(memset(glr[:, :], 1.0), *ffn_done)
        j, t = gemm("gl", 8, 16, hh, hl, t_h)
        t_glr = dve.op(tensor_copy(glr[0:16, :], S[j][0:16, :]), t, t_gl1)
        slots.readers[j] = (t_glr,)
        jg, free = mslot.take()
        gring = Ring(2)
        t_dec = []
        ge_free = mslot.readers[jg]
        jd, dfree = slots.take()
        dring = Ring(2)
        dring.readers = [dfree, dfree]
        jz, zfree = slots.take()
        zring = Ring(2)
        zring.readers = [zfree, zfree]
        pe.wait(*free)
        for i in range(8):
            z, zf = zring.take()
            Z = S[jz][:, 512 * z:512 * z + 512]
            t = pe.op(matmul(Z, glr[0:17, 128 * i:128 * i + 128], wg2[0:17, :], start=True, stop=True),
                      t_glr, t_w2, *zf)
            a, gf = gring.take()
            ta = act.op(activation(ge[:, a, :], Z, ACT.Abs), t, *gf, *ffn_done)
            ta = act.op(activation(ge[:, a, :], ge[:, a, :], ACT.Exp, scale=-1.0), ta)
            ta = act.op(activation(ge[:, a, :], ge[:, a, :], ACT.Ln, bias=1.0), ta)
            tb = dve.op(scalar_tensor_tensor(gz[:, a, :], Z, 0.0, ge[:, a, :], ALU.min, ALU.subtract),
                        ta, t, *ffn_done)
            zring.readers[z] = (tb,)
            d, df = dring.take()
            Dm = S[jd][:, 512 * d:512 * d + 512]
            t = pe.op(matmul(Dm, cst[:, C_SUF:C_SUF + 128], gz[:, a, :], start=True, stop=True), tb, *df)
            for h in range(4):
                f = (matmul(M[jg][:, 16 * h + 2 * i:16 * h + 2 * i + 2], gz[:, a, 128 * h:128 * h + 128],
                     cst[:, C_IND:C_IND + 2], start=True, stop=True))
                if h == 3:
                    tg = pe.op(f)
                else:
                    pe.run(f)
            gring.readers[a] = (tg,)
            td = act.op(activation(gd[:, i, :], Dm, ACT.Exp), t, *t_h[-1])
            dring.readers[d] = (td,)
            t_dec.append(td)
        t_ege = act.op(activation(ege[:, :, :].rearrange("p a b -> p (a b)"), M[jg][:, 0:64], ACT.Exp), tg)
        mslot.readers[jg] = (t_ege,)
        slots.readers[jd] = dring.readers[0] + dring.readers[1]
        slots.readers[jz] = zring.readers[0] + zring.readers[1]

        g2r = Ring(2)
        pend = []
        t_kd, t_v = {}, {}

        def g_fin(u):
            kind, m, a, t = u
            j, free = slots.take()
            pe.wait(t, *free)
            for i in range(8):
                f = transpose(S[j][:, 128 * i:128 * i + 128], gt2[:, a, 128 * i:128 * i + 128], ID)
                if i == 7:
                    t = pe.op(f)
                else:
                    pe.run(f)
            g2r.readers[a] = (t,)
            P3 = S[j][:, :].rearrange("p (a b) -> p a b", b=128)
            if kind == "gk":
                d = gd[:, :, 128 * m:128 * m + 128]
                t = dve.op(tensor_tensor(d, P3, d, ALU.mult), t, t_dec[-1])
                t_kd[m] = t
            else:
                h, c = m // 2, 128 * (m % 2)
                t = act.op(activation(vo[:, h, :, c:c + 128], P3, ACT.Copy), t, t_sp, *t_h[-1])
                t_v[m] = t
            slots.readers[j] = (t,)

        for n in range(12):
            kind, m = ("gk", n) if n < 4 else ("gv", n - 4)
            j, t = gemm(kind, 8, 128, hh, hl, t_h)
            a, free = g2r.take()
            t = dve.op(tensor_copy(gt2[:, a, :], S[j][:, :]), t, *free, *ffn_done)
            slots.readers[j] = (t,)
            pend.append((kind, m, a, t))
            if len(pend) > 1:
                g_fin(pend.pop(0))
        t_q = []
        for m in range(4):
            j, t = gemm("gq", 8, 128, hh, hl, t_h)
            t = act.op(activation(gq[:, m, :], S[j][:, :], ACT.Copy, scale=float(128 ** -0.5)), t, *t_h[-1])
            slots.readers[j] = (t,)
            t_q.append(t)
            if pend:
                g_fin(pend.pop(0))

        kvb = [S[2][:, 0:256], S[2][:, 512:768], M[0][:, 0:256], M[1][:, 0:256]]
        kvr = Ring(4)
        kvr.readers = [slots.readers[2], slots.readers[2], mslot.readers[0], mslot.readers[1]]
        o_rd = [slots.readers[0], slots.readers[1]]
        stv = Ring(8)
        prev = None
        t_gn = {}
        norms = []
        free_gsq = [()]
        free_grs = [()]

        def kv(h, c):
            b, free = kvr.take()
            pe.wait(*free, t_kd[h], t_v[2 * h], t_v[2 * h + 1])
            p0, i = 64 * (c % 2), c // 2
            t = pe.op(matmul(kvb[b], gd[p0:p0 + 64, i, 128 * h:128 * h + 128], vo[p0:p0 + 64, h, i, :],
                                         start=True, stop=True))
            s, sfree = stv.take()
            if c == 0:
                t = dve.op(tensor_copy(gst[:, s, :], kvb[b]), t, *sfree, *ffn_done)
            else:
                q = (s - 1) % 8
                t = dve.op(scalar_tensor_tensor(gst[:, s, :], gst[:, q, :], ege[:, h, c:c + 1], kvb[b],
                           ALU.mult, ALU.add), t, t_ege, *sfree, st["gs"])
            st["gs"] = t
            kvr.readers[b] = (t,)
            return s, t

        def oo(h, c, s, t):
            pe.wait(t, t_q[h], *o_rd[0], *o_rd[1])
            for d in range(2):
                f = (matmul(S[d][:, 64 * c:64 * c + 64], gst[:, s, 128 * d:128 * d + 128],
                     gq[:, h, 64 * c:64 * c + 64], start=True, stop=True))
                if d:
                    t = pe.op(f)
                else:
                    pe.run(f)
            stv.readers[s] = (t,)
            return t

        def head_out(h, t):
            O = vo[:, h, :, :].rearrange("p a b -> p (a b)")
            ta = act.op(activation(O[:, 0:1024], S[0][:, :], ACT.Copy), t)
            tb = dve.op(tensor_copy(O[:, 1024:2048], S[1][:, :]), t)
            o_rd[0], o_rd[1] = (ta,), (tb,)
            t_gn[h] = (ta, tb)

        lag = []
        for h in range(4):
            for c in range(16):
                s, t = kv(h, c)
                lag.append((h, c, s, t))
                if len(lag) > 2:
                    x = lag.pop(0)
                    t = oo(*x)
                    if x[1] == 15:
                        head_out(x[0], t)
        while lag:
            x = lag.pop(0)
            t = oo(*x)
        head_out(3, t)
        slots.readers = [o_rd[0], o_rd[1], kvr.readers[0] + kvr.readers[1]]
        mslot.readers = [kvr.readers[2], kvr.readers[3]]

        def head_norm(h):
            O = vo[:, h, :, :].rearrange("p a b -> p (a b)")
            j, free = slots.take()
            pe.wait(*free)
            for d in range(2):
                t = act.op(activation(gsq[:, :], O[:, 1024 * d:1024 * d + 1024], ACT.Square),
                           *t_gn[h], *free_gsq[0], *ffn_done)
                pe.wait(t)
                for c in (0, 512):
                    f = (matmul(S[j][:, c:c + 512], cst[:, C_DV:C_DV + 128], gsq[:, c:c + 512],
                         start=d == 0, stop=d == 1))
                    if c:
                        t = pe.op(f)
                    else:
                        pe.run(f)
                free_gsq[0] = (t,)
            t = act.op(activation(grs[:, :], S[j][:, :], ACT.Ln, bias=EPS), t, *free_grs[0])
            slots.readers[j] = (t,)
            t = act.op(activation(grs[:, :], grs[:, :], ACT.Exp, scale=-0.5), t)
            for d in range(2):
                Od = O[:, 1024 * d:1024 * d + 1024]
                g = vec[:, V_GLN + 2 * h + d:V_GLN + 2 * h + d + 1]
                tn = dve.op(scalar_tensor_tensor(Od, Od, g, grs[:, :], ALU.mult, ALU.mult), t, *t_gn[h])
                st["gn", 2 * h + d] = tn
            free_grs[0] = (tn,)

        t_o = []
        for m in range(8):
            j, t = gemm("gr", 8, 128, hh, hl, t_h)
            a, free = g2r.take()
            t = act.op(activation(gt2[:, a, :], S[j][:, :], ACT.Silu), t, *free)
            slots.readers[j] = (t,)
            if m % 2 == 0:
                head_norm(m // 2)
            Od = vo[:, m // 2, :, :].rearrange("p a b -> p (a b)")[:, 1024 * (m % 2):1024 * (m % 2) + 1024]
            t = dve.op(tensor_tensor(Od, Od, gt2[:, a, :], ALU.mult), t, st["gn", m])
            g2r.readers[a] = (t,)
            t_o.append((Od, t))
        r_done = (pe.sem, pe.n)
        t_h = []
        for m in range(8):
            Od, t = t_o[m]
            ta = dve.op(tensor_copy(hh[:, m, :], Od), t, r_done)
            tb = pool.op(tensor_tensor(hl[:, m, :], Od, hh[:, m, :].bitcast(F), ALU.subtract), t, ta, r_done)
            t_h.append((ta, tb))
        t_xt = []
        for k in range(8):
            t_xt.append((load(s_xt[k], 2, xt[:, k, :], T["spill"][k], *t_h[k], *t_h[-1], t_sp),))
        x2s["ovl"] = t_h[-1]
        x2s["free"] += t_h[-1]
        for m in range(8):
            j, t = gemm("go", 8, 128, hh, hl, t_h)
            residual(m, j, t, None, True)
        ttr.readers = [t_h[-1]] * 3
        t_h = normed(vec[:, V_FFN:V_FFN + 8], None, t_xt)

        ub = at("ub", U + 40 * KB, [128, 2, 1026], F)
        tg_ = at("tg_", U + 49 * KB, [128, 1, 1024], F)
        tv_ = at("tv_", U + 53 * KB, [128, 1, 1024], F)
        t = tuple(x2s["free"]) + t_h[-1]
        sqr = Ring(1)
        sqr.readers = [x2s["tok"]]
        t_z = [dve.op(memset(ub[:, i, 0:2], 0.0), *t, *x2s["tok"]) for i in range(2)]
        ubr = Ring(2)
        ubr.readers = [(t_z[1],), (t_z[1],)]
        tring = {0: t_h[-1], 1: t_h[-1]}
        hid_free = {}

        def conv(j, t, buf, which, n):
            a, free = ubr.take()
            x = buf[:, 0, :]
            t0 = act.op(activation(ub[:, a, 2:1026], S[j][:, :], ACT.Copy), t, *free)
            w = [vec[:, V_CW + 44 * i + n:V_CW + 44 * i + n + 1] for i in range(3)]
            t1 = act.op(activation(x, S[j][:, :], ACT.Identity, scale=w[2], bias=vec[:, V_CB + n:V_CB + n + 1]),
                        *tring[which])
            slots.readers[j] = (t1,)
            t2 = dve.op(scalar_tensor_tensor(x, ub[:, a, 1:1025], w[1], x, ALU.mult, ALU.add), t0, t1)
            t3 = dve.op(scalar_tensor_tensor(x, ub[:, a, 0:1024], w[0], x, ALU.mult, ALU.add), t2)
            ubr.readers[a] = (t3,)
            return t3

        for kind, a in ffn_order():
            if kind == "gu":
                jg, tg = gemm("f2g", 8, 128, hh, hl, t_h)
                t = conv(jg, tg, tg_, 0, a)
                ts = act.op(activation(tg_[:, 0, :], tg_[:, 0, :], ACT.Silu), t)
                ju, tu = gemm("f2u", 8, 128, hh, hl, t_h)
                t = conv(ju, tu, tv_, 1, 22 + a)
                t = dve.op(tensor_tensor(tv_[:, 0, :], tv_[:, 0, :], tg_[:, 0, :], ALU.mult), t, ts)
                tring[0] = (t,)
                tb = emit_hidden(a, tv_[:, 0, :], t, None, None)
                tring[1] = (tb,)
            else:
                down("d2", a, None, a == len(DNG) - 1)

        fo = at("fo", U + 60 * KB, [128, 8, 1024], F)
        rs3 = at("rs3", U + 92 * KB, [128, 1024], F)
        j, free = slots.take()
        pe.wait(*free, *x2s["tok"])
        one = cst[:, C_ONE:C_ONE + 128]
        pe.run(matmul(S[j][:, 0:512], one, x2[:, 0:512], start=True, stop=True))
        t = pe.op(matmul(S[j][:, 512:1024], one, x2[:, 512:1024], start=True, stop=True))
        t = act.op(activation(rs3[:, :], S[j][:, :], ACT.Ln, bias=EPS), t)
        t = act.op(activation(rs3[:, :], rs3[:, :], ACT.Exp, scale=-0.5), t)
        s_out = sem("s_out")
        for k in range(8):
            ta = dve.op(scalar_tensor_tensor(fo[:, k, :], xt[:, k, :], vec[:, V_FIN + k:V_FIN + k + 1],
                        rs3[:, :], ALU.mult, ALU.mult), t, *t_xt[k])
            t_out = load(s_out, k + 1, out[k], fo[:, k, :], ta)
        sp.wait(t_out)
        assert at_slab["i"] == len(plan), (at_slab, len(plan))

        block = ctx.enter_context(nc.Block())

        @block.tensor
        def _(e):
            for f in pe.items:
                f(e)

        @block.scalar
        def _(e):
            for f in act.items:
                f(e)

        @block.vector
        def _(e):
            for f in dve.items:
                f(e)

        @block.gpsimd
        def _(e):
            for f in pool.items:
                f(e)

        @block.sync
        def _(e):
            for f in sp.items:
                f(e)


def constants():
    f = np.float32
    c = np.zeros((128, C_N), f)
    i = np.arange(128)
    c[:, C_ID:C_ID + 128] = np.eye(128, dtype=f)
    c[:, C_ONE:C_ONE + 128] = 1.0 / 1024
    c[:, C_BLK:C_BLK + 128] = (i[:, None] // 64 == i[None] // 64) / 64.0
    c[:, C_PERM:C_PERM + 128] = i[:, None] == (i[None] ^ 16)
    c[:, C_SUF:C_SUF + 128] = ((i[:, None] > i[None]) & (i[:, None] // 64 == i[None] // 64)) / 16.0
    c[:, C_DV:C_DV + 128] = 1.0 / 256
    c[:, C_ML:C_ML + 128] = np.where(i[None] < i[:, None], BIG, 0)
    c[:, C_MR:C_MR + 128] = np.where(i[None] > i[:, None], BIG, 0)
    c[:, C_IND:C_IND + 2] = (i[:, None] // 64 == np.arange(2)[None]) / 16.0
    c[:, C_EPS] = 1e-6
    inv = (f(1.0) / (f(10000.0) ** (np.arange(16, dtype=f) / f(16)))).astype(f)
    t = np.arange(1024)
    d = i % 64
    pos = np.where((d < 32)[:, None], t[None] // 64, t[None] % 64).astype(f)
    ang = (pos * inv[d % 16][:, None]).astype(f)
    sign = np.where(d % 32 < 16, -1.0, 1.0).astype(f)
    cs = np.stack([np.cos(ang), np.sin(ang) * sign[:, None]], 1).astype(f)
    return c, np.ascontiguousarray(cs)


def bias_index():
    dr = np.zeros((128, 23, 64), int)
    dc = np.zeros((128, 23, 64), int)
    ok = np.zeros((128, 23, 64), bool)
    q = np.arange(128)
    qr, qc = q // 64, q % 64
    kc = np.arange(64)
    c0 = np.clip(qc - 8, 0, 48)
    col_ok = (kc[None] >= c0[:, None]) & (kc[None] < c0[:, None] + 16)
    es = list(range(1, 15)) + list(range(3, 12))
    for s, e in enumerate(es):
        dr[:, s, :] = np.clip(e - qr, 0, 14)[:, None]
        dc[:, s, :] = np.clip(kc[None] - qc[:, None] + 15, 0, 30)
        row = np.ones(128, bool)
        if s >= 14 and e == 3:
            row = qr == 0
        if s >= 14 and e == 11:
            row = qr == 1
        ok[:, s, :] = col_ok & row[:, None]
    return dr.reshape(128, -1), dc.reshape(128, -1), ok.reshape(128, -1)


def cols(v):
    return np.ascontiguousarray(v).reshape(-1, 128).T


def slabs(w):
    k, m = w.shape
    return np.ascontiguousarray(w.reshape(k // 128, 128, m // 128, 128).transpose(2, 1, 0, 3)).reshape(m // 128, 128, k)


def layout(i):
    f = np.float32
    A = {}
    cst, cs = constants()
    A["cst"], A["cs"] = cst, cs
    v = np.zeros((128, V_N), f)
    v[:, V_BMOD:V_BMOD + 48] = cols(i["b_mod"][0])
    v[:, V_N1:V_N1 + 8] = cols(i["norm1_g"][0])
    for c, n in ((V_QA, "qn_a"), (V_KA, "kn_a"), (V_QB, "qn_b"), (V_KB, "kn_b")):
        v[:, c] = np.concatenate([i[n][0], i[n][0]])
    v[:, V_ONA:V_ONA + 4] = cols(i["on_a"][0])
    v[:, V_ONB:V_ONB + 4] = cols(i["on_b"][0])
    v[:, V_N2:V_N2 + 8] = cols(i["norm2_g"][0])
    v[:, V_MIX:V_MIX + 8] = cols(i["mix_norm_w_2"][0])
    v[:, V_FFN:V_FFN + 8] = cols(i["ffn_norm_w_2"][0])
    v[:, V_FIN:V_FIN + 8] = cols(i["final_norm_w_2"])
    v[:, V_GLN:V_GLN + 8] = cols(i["gla_norm_w_2"][0])
    for t in range(3):
        v[:, V_CW + 44 * t:V_CW + 44 * t + 44] = cols(i["ffn_conv_w_2"][0, t])
    v[:, V_CB:V_CB + 44] = cols(i["ffn_conv_b_2"][0])
    A["vec"] = v
    cc = np.stack([cols(i["c"][0]), cols(i["c_ctx"])], 2)
    A["cc"] = np.ascontiguousarray(cc).reshape(128, 16)
    A["c_row"] = np.ascontiguousarray(i["c"])
    A["sink"] = np.ascontiguousarray(i["sink_a"])
    x = np.concatenate([i["x"][0], i["ctx"][0]], 0)
    A["xT"] = np.ascontiguousarray(x.T).reshape(8, 128, 1280)
    w = i["w_mod"][0]
    A["w_mod0"] = slabs(w[:, :2048])
    A["w_modT"] = np.ascontiguousarray(w[:, 2048:].T).reshape(32, 128, 1024)
    w = i["w_in"][0]
    qa, ka, va, qb, kb, vb = np.split(w, np.cumsum([512, 128, 128, 512, 512]), axis=1)
    order = np.concatenate([np.concatenate([np.arange(64) + 64 * j, np.arange(64) + 64 * (j + 4)]) for j in range(4)])
    A["w_in"] = slabs(np.concatenate([ka, kb, va, vb, qa[:, order], qb], 1))
    A["w_out"] = slabs(i["w_out"][0])
    A["w_f1g"] = slabs(i["w_gate"][0])
    A["w_f1u"] = slabs(i["w_up"][0])
    A["w_d1"] = slabs(i["w_down"][0])
    dr, dc, ok = bias_index()
    A["bias"] = np.where(ok[None], i["rpb_b"][0][:, dr, dc], f(-BIG)).astype(f)
    g = i["gla_w_in_2"][0]
    q, k, vv, r, gl = np.split(g, np.cumsum([512, 512, 1024, 1024]), axis=1)
    A["w_gq"], A["w_gk"], A["w_gv"], A["w_gr"] = slabs(q), slabs(k), slabs(vv), slabs(r)
    glp = np.zeros((1024, 128), f)
    glp[:, :16] = gl
    A["w_gl"] = slabs(glp)
    A["w_gate2"] = np.concatenate([i["gla_w_gate2_2"][0], i["gla_b_gate_2"]], 0)
    A["w_go"] = slabs(i["gla_w_out_2"][0])
    u = i["ffn_w_up_2"][0]
    A["w_f2g"], A["w_f2u"] = slabs(u[:, :2816]), slabs(u[:, 2816:])
    A["w_d2"] = slabs(i["ffn_w_down_2"][0])
    return A


def kernel(**inputs):
    import concourse.bacc as _bacc
    from concourse.bass_utils import run_bass_kernel_spmd as _run

    arrays = layout({k: np.asarray(v) for k, v in inputs.items()})
    nc = _bacc.Bacc("TRN2", target_bir_lowering=False, num_devices=1)
    T = {}
    for name, a in arrays.items():
        T[name] = nc.dram_tensor(f"in_{name}", a.shape, mybir.dt.from_np(a.dtype), kind="ExternalInput").ap()
    T["spill"] = nc.dram_tensor("spill", (8, 128, 1024), F).ap()
    out = nc.dram_tensor("out_0", (8, 128, 1024), F, kind="ExternalOutput").ap()
    build(nc, T, out)
    r = _run(nc, [{f"in_{n}": a for n, a in arrays.items()}], core_ids=[0])
    got = r.results[0]["out_0"]
    return np.ascontiguousarray(got.reshape(1024, 1024).T).reshape(1, 1024, 1024)
```

```python
from contextlib import ExitStack

import numpy as np

import concourse.bass as bass
from concourse import mybir

F = mybir.dt.float32
R = mybir.dt.float32r
BF = mybir.dt.bfloat16
ALU = mybir.AluOpType
ACT = mybir.ActivationFunctionType
AX = mybir.AxisListType.X
KB = 1024
BIG = 1.0e30

C_ID, C_ONE, C_BLK, C_PERM, C_SUF, C_DV, C_ML, C_MR = [128 * i for i in range(8)]
C_IND = 1024
C_EPS = 1026
C_N = 1032
V_BMOD, V_N1, V_QA, V_KA, V_QB, V_KB, V_ONA, V_ONB = 0, 48, 56, 57, 58, 59, 60, 64
V_N2, V_MIX, V_FFN, V_FIN, V_GLN, V_CW, V_CB = 68, 76, 84, 92, 100, 108, 240
V_N = 288
M_MOD, M_CMOD, M_G1, M_GC, M_QA, M_QB, M_G2, M_RAW = 0, 48, 64, 72, 80, 81, 82, 96
M_N = 144

DNG = [5, 5, 4, 4, 4]
NPM = 6
NH = 22


def slab_plan():
    plan = [("mod", m) for m in range(NPM)]
    plan += [("in", m) for m in range(18)]
    plan += [("out", m) for m in range(8)]

    def ffn(gu, dn):
        out, h = [], 0
        order = ffn_order()
        for kind, a in order:
            if kind == "gu":
                out += [(gu + "g", a), (gu + "u", a)]
            else:
                out += [(dn, a * 8 + m) for m in range(8)]
        return out

    plan += ffn("f1", "d1")
    plan += [("gl", 0)] + [("gv", m) for m in range(8)] + [("gk", m) for m in range(4)]
    plan += [("gq", m) for m in range(4)] + [("gr", m) for m in range(8)]
    plan += [("go", m) for m in range(8)]
    plan += ffn("f2", "d2")
    return plan


def ffn_order():
    order, done, start = [], 0, 0
    for g, n in enumerate(DNG):
        while done < min(start + n + 1, NH):
            order.append(("gu", done))
            done += 1
        order.append(("dn", g))
        start += n
    return order


def ln_table():
    return lambda e: e.preload_act_table_set("natural_log")

def activation(*a, **k):
    return lambda e: e.activation(*a, **k)

def matmul(*a, **k):
    return lambda e: e.matmul(*a, **k)

def memset(*a, **k):
    return lambda e: e.memset(*a, **k)

def reciprocal(*a, **k):
    return lambda e: e.reciprocal(*a, **k)

def scalar_tensor_tensor(*a, **k):
    return lambda e: e.scalar_tensor_tensor(*a, **k)

def tensor_copy(*a, **k):
    return lambda e: e.tensor_copy(*a, **k)

def tensor_reduce(*a, **k):
    return lambda e: e.tensor_reduce(*a, **k)

def tensor_scalar(*a, **k):
    return lambda e: e.tensor_scalar(*a, **k)

def tensor_tensor(*a, **k):
    return lambda e: e.tensor_tensor(*a, **k)

def tensor_tensor_reduce(*a, **k):
    return lambda e: e.tensor_tensor_reduce(*a, **k)

def transpose(*a, **k):
    return lambda e: e.transpose(*a, **k)


def build(nc, T, out):
    B0 = 16512
    names = {}

    def at(name, off, shape, dt):
        return nc.alloc_sbuf_tensor_at(name, shape, dt, offset=off)

    o = B0
    cst = at("cst", o, [128, C_N], F); o += C_N * 4
    vec = at("vec", o, [128, V_N], F); o += V_N * 4
    mv = at("mv", o, [128, M_N], F); o += M_N * 4
    idb = at("idb", o, [128, 128], BF); o += 256
    mlb = at("mlb", o, [128, 128], BF); o += 256
    mrb = at("mrb", o, [128, 128], BF); o += 256
    snk = at("snk", o, [128, 16], F); o += 64
    csl = at("csl", o, [128, 16], F); o += 64
    nmx = at("nmx", o, [128, 32], F); o += 128
    den = at("den", o, [128, 32], F); o += 128
    rdn = at("rdn", o, [128, 32], F); o += 128
    oss = at("oss", o, [128, 16], F); o += 64
    ors = at("ors", o, [128, 16], F); o += 64
    ege = at("ege", o, [128, 4, 16], F); o += 256
    dsn = at("dsn", o, [128, 32], F); o += 128
    o = (o + 31) // 32 * 32
    A_RAW, A_W = o, o + 12 * KB
    raw = at("raw", o, [128, 3, 1024], F); o += 12 * KB
    wh = at("wh", o, [128, 2, 8, 128], R); o += 8 * KB
    wl = at("wl", o, [128, 2, 8, 128], R); o += 8 * KB
    AH = o
    hh = at("hh", o, [128, 8, 1024], R); o += 32 * KB
    hl = at("hl", o, [128, 8, 1024], R); o += 32 * KB
    U = o

    with ExitStack() as ctx:
        sem = lambda n: ctx.enter_context(nc.semaphore(n))
        S = [ctx.enter_context(nc.psum_tensor(f"S{i}", [128, 1024], F)) for i in range(3)]
        M = [ctx.enter_context(nc.psum_tensor(f"M{i}", [128, 512], F)) for i in range(2)]

        class Queue:

            def __init__(self, name):
                self.name, self.sem, self.n, self.items, self.seen = name, sem("s_" + name), 0, [], {}

            def wait(self, *toks):
                for s, v in toks:
                    if self.seen.get(s.name, 0) < v:
                        self.seen[s.name] = v
                        self.items.append(lambda e, s=s, v=v: e.wait_ge(s, v))

            def run(self, f, *toks):
                self.wait(*toks)
                self.items.append(f)

            def op(self, f, *toks):
                self.wait(*toks)
                self.n += 1
                self.items.append(lambda e: f(e).then_inc(self.sem, 1))
                return (self.sem, self.n)

        pe, act, dve, pool, sp = (Queue(n) for n in ("pe", "act", "dve", "pool", "sp"))

        def load(s, n, dst, src, *toks):
            sp.run(lambda e: e.dma_start(dst, src).then_inc(s, 16), *toks)
            return (s, 16 * n)

        class Ring:

            def __init__(self, n):
                self.n, self.i, self.readers, self.held = n, 0, [()] * n, None

            def take(self):
                if self.i % self.n == self.held:
                    self.i += 1
                k = self.i % self.n
                self.i += 1
                return k, self.readers[k]

        slots = Ring(3)
        mslot = Ring(2)

        plan = slab_plan()
        s_raw = [sem(f"s_raw{i}") for i in range(3)]
        raw_free, w_free = {}, {}
        loaded, split = {}, {}
        cur = {"load": 0, "split": 0, "w": 0}
        raw_gate, w_gate = [], []

        def src_of(kind, m):
            if kind == "mod":
                return T["w_mod0"][m], 1024
            if kind in ("d1", "d2"):
                g = m // 8
                k0, k = sum(DNG[:g]), DNG[g]
                return T["w_" + kind][m % 8][:, 128 * k0:128 * (k0 + k)], 128 * k
            return T["w_" + kind][m], 1024

        def load_slab():
            i = cur["load"]
            if i >= (len(plan) if raw_gate else NPM + 18):
                return
            cur["load"] += 1
            src, n = src_of(*plan[i])
            j = i % 3
            loaded[i] = load(s_raw[j], i // 3 + 1, raw[:, j, 0:n], src, *(raw_free[i - 3] if i >= 3 else ()), *raw_gate)

        def split_slab():
            i = cur["split"]
            if i >= len(plan):
                return
            cur["split"] += 1
            if plan[i][0] == "mod":
                return
            n, j, k = src_of(*plan[i])[1], i % 3, cur["w"] % 2
            free = w_free.get(cur["w"] - 2, ()) + tuple(w_gate)
            cur["w"] += 1
            h = wh[:, k, :, :].rearrange("p a b -> p (a b)")[:, 0:n]
            l = wl[:, k, :, :].rearrange("p a b -> p (a b)")[:, 0:n]
            r = raw[:, j, 0:n]
            a = act.op(activation(h, r, ACT.Copy), loaded[i], *free)
            b = pool.op(tensor_tensor(l, r, h.bitcast(F), ALU.subtract), a, loaded[i], *free)
            raw_free[i] = (a, b)
            split[i] = (k, cur["w"] - 1, (a, b))
            load_slab()

        at_slab = {"i": 0, "done": 0, "hold": NPM + 18, "late": False}

        def split_ahead():
            while not at_slab["late"] and cur["split"] < min(at_slab["done"] + 2, at_slab["hold"]):
                split_slab()

        def next_slab(kind):
            i = at_slab["i"]
            at_slab["i"] += 1
            assert plan[i][0] == kind, (plan[i], kind)
            return split[i]

        def slab_done(w_i, tok):
            w_free[w_i] = (tok,)
            at_slab["done"] += 1
            split_ahead()

        class Product:

            def __init__(self, kind, kt, mm, hi, lo, toks, ctx_act=None):
                self.k_, self.w_i, wt = next_slab(kind)
                self.kt, self.mm, self.hi, self.lo, self.toks, self.cx = kt, mm, hi, lo, toks, ctx_act
                self.j, free = slots.take()
                pe.wait(*wt, *free)
                if ctx_act is not None:
                    self.jc, cfree = mslot.take()
                    pe.wait(*cfree)

            def step(self, k, count=False):
                kt, mm, j = self.kt, self.mm, self.j
                pe.wait(*self.toks[k][:-1])
                wk, vk = wh[:, self.k_, k, 0:mm], wl[:, self.k_, k, 0:mm]
                for n, (w, x) in enumerate(((wk, self.hi), (vk, self.hi), (wk, self.lo))):
                    if n == 2:
                        pe.wait(self.toks[k][-1])
                    st_, en = k == 0 and n == 0, k == kt - 1 and n == 2
                    fs = [matmul(S[j][0:mm, c:c + 512], w, x[:, k, c:c + 512], start=st_, stop=en) for c in (0, 512)]
                    if self.cx is not None:
                        fs.append(matmul(M[self.jc][0:mm, 0:256], w, self.cx[n // 2][:, k, :], start=st_, stop=en))
                    for f in fs[:-1]:
                        pe.run(f)
                    if en or (count and n == 2):
                        self.tok = pe.op(fs[-1])
                    else:
                        pe.run(fs[-1])
                if k == kt - 1:
                    slab_done(self.w_i, self.tok)
                return (pe.sem, pe.n)

        def gemm(kind, kt, mm, hi, lo, toks, fill=(), done=None, ctx_act=None):
            p = Product(kind, kt, mm, hi, lo, toks, ctx_act)
            fill = list(fill)
            for k in range(kt):
                t = p.step(k, done is not None)
                if done is not None:
                    done.append(t)
                if fill:
                    f = fill.pop(0)
                    if f is not None:
                        f()
            return (p.j, p.tok) if ctx_act is None else (p.j, p.jc, p.tok)

        def gemm_pair(kinds, mms, hi, lo, toks, ctx_act=None, fill=()):
            a = Product(kinds[0], 8, mms[0], hi, lo, toks, ctx_act)
            fill = list(fill)

            def step_a(k):
                a.step(k)
                if fill:
                    fill.pop(0)()

            step_a(0)
            step_a(1)
            b = Product(kinds[1], 8, mms[1], hi, lo, toks, ctx_act)
            b.step(0)
            b.step(1)
            for k in range(2, 8):
                step_a(k)
                if k < 4:
                    b.step(k)
            for k in range(4, 8):
                b.step(k)
            if ctx_act is not None:
                return (a.j, a.jc, a.tok), (b.j, b.jc, b.tok)
            return (a.j, a.tok), (b.j, b.tok)

        def all_of(toks):
            return tuple(x for t in toks for x in t)

        s_c = sem("s_c")
        load(s_c, 1, cst[:, :], T["cst"])
        load(s_c, 2, vec[:, :], T["vec"])
        t_c = load(s_c, 3, csl[:, :], T["cc"])
        ID = cst[:, C_ID:C_ID + 128]
        EPS = cst[:, C_EPS:C_EPS + 1]

        hch = at("hch", U, [128, 8, 256], R)
        hcl = at("hcl", U + 8 * KB, [128, 8, 256], R)
        P_QB, P_KA, P_KB, P_V = U, U + 16 * KB, U + 21 * KB, U + 41 * KB
        P_QA, P_CS = U + 66 * KB, U + 82 * KB
        P_SQ, P_RS, P_RP, P_VT = U + 90 * KB, U + 95 * KB, U + 100 * KB, U + 100 * KB
        qb = at("qb", P_QB, [128, 4, 1024], F)
        ka = at("ka", P_KA, [128, 1280], F)
        kb = at("kb", P_KB, [128, 4, 1280], F)
        vv = at("vv", P_V, [128, 10, 640], F)
        qa = at("qa", P_QA, [128, 4, 1024], F)
        cs = at("cs", P_CS, [128, 2, 1024], F)
        sq = at("sq", P_SQ, [128, 1280], F)
        rs = at("rs", P_RS, [128, 1280], F)
        rp = at("rp", P_RP, [128, 1024], F)
        vt = at("vt", P_VT, [128, 1280], F)
        xw = at("xw", P_V, [128, 8, 1280], F)
        xq = at("xq", P_KA, [128, 3, 1280], F)

        crow = at("crow", AH, [128, 2, 1024], F)
        mtl = at("mtl", AH + 8 * KB, [128, 4, 1024], F)
        mjk = at("mjk", AH + 24 * KB, [128, 1024], F)
        s_cr, s_mt = sem("s_cr"), [sem(f"s_mt{i}") for i in range(4)]
        s_xw = [sem(f"s_xw{i}") for i in range(8)]
        t_xw, t_mt, mt_done = [], {}, {}

        def mt_load(n):
            t_mt[n] = load(s_mt[n % 4], n // 4 + 1, mtl[:, n % 4, :], T["w_modT"][n], *mt_done.get(n - 4, ()))

        for k in range(8):
            t_xw.append(load(s_xw[k], 1, xw[:, k, :], T["xT"][k]))
            if k == 0:
                load(s_cr, 1, crow[:, 0, :], T["c_row"].to_broadcast([128, 1024]))
                t_cr = load(s_cr, 2, crow[:, 1, :], T["cx_row"].to_broadcast([128, 1024]))
            if k in (3, 6, 7):
                load_slab()
            if k in (0, 4, 7):
                mt_load(len(t_mt))
        mt_load(3)

        t_sil = act.op(activation(csl[:, :], csl[:, :], ACT.Silu), t_c)
        t_idb = act.op(activation(idb[:, :], ID, ACT.Copy))
        act.op(activation(mlb[:, :], cst[:, C_ML:C_ML + 128], ACT.Copy))
        t_msk = act.op(activation(mrb[:, :], cst[:, C_MR:C_MR + 128], ACT.Copy))
        dve.op(tensor_scalar(mv[:, M_QA:M_QA + 1], vec[:, V_QA:V_QA + 1], -0.125, None, ALU.mult), t_c)
        t_qg = dve.op(tensor_scalar(mv[:, M_QB:M_QB + 1], vec[:, V_QB:V_QB + 1], -0.125, None, ALU.mult))

        t_crs = act.op(activation(crow[:, :, :].rearrange("p a b -> p (a b)"),
                                  crow[:, :, :].rearrange("p a b -> p (a b)"), ACT.Silu), t_cr)

        def mt_sum(n):
            for i in range(2):
                c = (M_RAW, M_CMOD)[i] + NPM + n
                t = dve.op(tensor_tensor_reduce(mjk[:, :], mtl[:, n % 4, :], crow[:, i, :], 1.0, 0.0,
                           ALU.mult, ALU.add, mv[:, c:c + 1]), t_mt[n], t_crs, (dve.sem, dve.n))
            mt_done[n] = (t,)

        for n in range(4):
            mt_sum(n)
        for n in (4, 5):
            mt_load(n)
            mt_sum(n)

        xqr = Ring(3)
        j, _ = slots.take()
        jc, _ = mslot.take()
        for k in range(8):
            a, free = xqr.take()
            t = act.op(activation(xq[:, a, :], xw[:, k, :], ACT.Square), t_xw[k], *free)
            pe.wait(t, t_c)
            for c, d in ((0, S[j][:, 0:512]), (512, S[j][:, 512:1024]), (1024, M[jc][:, 0:256])):
                f = (matmul(
                    d, cst[:, C_ONE:C_ONE + 128], xq[:, a, c:c + min(512, 1280 - c)], start=k == 0, stop=k == 7))
                if c == 1024:
                    t_ms = pe.op(f)
                else:
                    pe.run(f)
            xqr.readers[a] = (t_ms,)
        act.op(activation(rs[:, 0:1024], S[j][:, :], ACT.Ln, bias=EPS), t_ms)
        t = act.op(activation(rs[:, 1024:1280], M[jc][:, 0:256], ACT.Ln, bias=EPS))
        slots.readers[j] = mslot.readers[jc] = (t,)
        t_rs = act.op(activation(rs[:, :], rs[:, :], ACT.Exp, scale=-0.5), t)
        jm, mfree = mslot.take()
        pe.wait(t_sil, *mfree)
        for m in range(NPM):
            while cur["split"] <= m:
                split_slab()
            for k in range(8):
                f = (matmul(
                    M[jm][:, 2 * m:2 * m + 2], raw[:, m % 3, 128 * k:128 * k + 128], csl[:, 2 * k:2 * k + 2],
                    start=k == 0, stop=k == 7))
                pe.wait(loaded[m])
                if k == 7:
                    t = pe.op(f)
                else:
                    pe.run(f)
            raw_free[m] = (t,)
            load_slab()
            if m < 4:
                mt_load(6 + m)
        t_xr = {}

        def xr(k, eng):
            t_xr[k] = eng.op(tensor_tensor(xw[:, k, :], xw[:, k, :], rs[:, :], ALU.mult), t_rs, t_xw[k])

        for k in (0, 1, 2, 4, 5, 6):
            xr(k, pool)
        for n in range(6, 16 - NPM):
            mt_sum(n)
            if n < 8:
                xr((3, 7)[n - 6], dve)
        t_md = mt_done[15 - NPM][0]
        t_cs = load(sem("s_cs"), 1, cs[:, :, :], T["cs"])
        at_slab["i"] = at_slab["done"] = NPM
        split_ahead()
        mp = M[jm][:, 0:2 * NPM].rearrange("p (m c) -> p c m", c=2)
        dve.op(tensor_tensor(mv[:, M_MOD + NPM:M_MOD + 16], mv[:, M_RAW + NPM:M_RAW + 16],
                             vec[:, V_BMOD + NPM:V_BMOD + 16], ALU.add), t_md)
        dve.op(tensor_tensor(mv[:, M_CMOD + NPM:M_CMOD + 16], mv[:, M_CMOD + NPM:M_CMOD + 16],
                             vec[:, V_BMOD + NPM:V_BMOD + 16], ALU.add), t_md)
        t1 = dve.op(tensor_tensor(mv[:, M_MOD:M_MOD + NPM], mp[:, 0, :], vec[:, V_BMOD:V_BMOD + NPM], ALU.add), t)
        t2 = dve.op(tensor_tensor(mv[:, M_CMOD:M_CMOD + NPM], mp[:, 1, :], vec[:, V_BMOD:V_BMOD + NPM], ALU.add))
        mslot.readers[jm] = (t1, t2)
        t1 = dve.op(scalar_tensor_tensor(mv[:, M_G1:M_G1 + 8], mv[:, M_MOD + 8:M_MOD + 16], 1.0,
                                                     vec[:, V_N1:V_N1 + 8], ALU.add, ALU.mult), t2)
        t_g = dve.op(scalar_tensor_tensor(mv[:, M_GC:M_GC + 8], mv[:, M_CMOD + 8:M_CMOD + 16], 1.0,
                                                      vec[:, V_N1:V_N1 + 8], ALU.add, ALU.mult), t1)
        t_h = []
        for k in range(8):
            xk = xw[:, k, :]
            ta = act.op(activation(xk[:, 0:1024], xk[:, 0:1024], ACT.Identity,
                        bias=mv[:, M_MOD + k:M_MOD + k + 1], scale=mv[:, M_G1 + k:M_G1 + k + 1]), t_g, t_xr[k])
            tb = act.op(activation(xk[:, 1024:1280], xk[:, 1024:1280], ACT.Identity,
                        bias=mv[:, M_CMOD + k:M_CMOD + k + 1], scale=mv[:, M_GC + k:M_GC + k + 1]))
            tc_ = dve.op(tensor_copy(hh[:, k, :], xk[:, 0:1024]), ta)
            td = (pool if k % 2 else dve).op(tensor_tensor(hl[:, k, :], xk[:, 0:1024], hh[:, k, :].bitcast(F), ALU.subtract), tc_, ta)
            tc_ = dve.op(tensor_copy(hch[:, k, :], xk[:, 1024:1280]), tb)
            te = dve.op(tensor_tensor(hcl[:, k, :], xk[:, 1024:1280], hch[:, k, :].bitcast(F), ALU.subtract), tc_)
            t_h.append((te, td))

        units = [("k", ka[:, :], vec[:, V_KA:V_KA + 1], True)]
        units += [("k", kb[:, m, :], vec[:, V_KB:V_KB + 1], False) for m in range(4)]
        units += [("v", m, None, False) for m in range(5)]
        units += [("q", qa[:, m, :], mv[:, M_QA:M_QA + 1], True) for m in range(4)]
        units += [("q", qb[:, m, :], mv[:, M_QB:M_QB + 1], False) for m in range(4)]
        t_ready = {}
        free_sq, free_vt, free_rp = [()], [()], [()]
        st = {}

        def stage0(u, fill):
            kind, dst, g, rope = units[u]
            cx = kind != "q"
            if u == 0:
                st["pair"] = gemm_pair(("in", "in"), (128, 128), hh, hl, t_h, ctx_act=(hch, hcl))
            if u < 2:
                j, jc, t = st["pair"][u]
            elif cx:
                j, jc, t = gemm("in", 8, 128, hh, hl, t_h, fill, ctx_act=(hch, hcl))
            else:
                j, t = gemm("in", 8, 128, hh, hl, t_h, fill)
                jc = None
            w = 1280 if cx else 1024
            if kind == "v":
                d = (sq if dst % 2 else vt)[:, :]
                dve.wait(*free_vt[0], *free_rp[0], *free_sq[0])
            else:
                d = dst
            if u == len(units) - 4:
                st["ctx_done"] = t
            if cx:
                tt = dve.op(tensor_copy(d[:, 1024:1280], M[jc][:, 0:256]), t)
                mslot.readers[jc] = (tt,)
            tt = dve.op(tensor_copy(d[:, 0:1024], S[j][:, :]), t)
            slots.readers[j] = (tt,)
            st[u] = tt

        def stage1(u):
            kind, dst, g, rope = units[u]
            j, free = slots.take()
            cx = kind != "q"
            if cx:
                jc, cfree = mslot.take()
                pe.wait(*cfree)
            pe.wait(*free)
            if kind == "v":
                pe.wait(st[u])
                src = sq if dst % 2 else vt
                for i in range(10):
                    d = S[j][:, 128 * i:128 * i + 128] if i < 8 else M[jc][:, 128 * (i - 8):128 * (i - 7)]
                    f = transpose(d, src[:, 128 * i:128 * i + 128], ID)
                    if i == 9:
                        t = pe.op(f)
                    else:
                        pe.run(f)
                if dst % 2:
                    free_sq[0] = (t,)
                else:
                    free_vt[0] = (t,)
                c = 128 * dst
                act.op(activation(vv[:, 0:8, c:c + 128], S[j][:, :].rearrange("p (a b) -> p a b", b=128), ACT.Copy), t)
                tt = act.op(activation(vv[:, 8:10, c:c + 128], M[jc][:, 0:256].rearrange("p (a b) -> p a b", b=128), ACT.Copy))
                slots.readers[j] = mslot.readers[jc] = (tt,)
                t_ready[u] = (tt,)
                return
            w = 1280 if cx else 1024
            t = act.op(activation(sq[:, 0:w], dst[:, 0:w], ACT.Square), st[u], *free_sq[0])
            pe.wait(t)
            blk = cst[:, C_BLK:C_BLK + 128]
            pe.run(matmul(S[j][:, 0:512], blk, sq[:, 0:512], start=True, stop=True))
            f = matmul(S[j][:, 512:1024], blk, sq[:, 512:1024], start=True, stop=True)
            if cx:
                pe.run(f)
                t = pe.op(matmul(M[jc][:, 0:256], blk, sq[:, 1024:1280], start=True, stop=True))
            else:
                t = pe.op(f)
            free_sq[0] = (t,)
            w = 1280 if cx else 1024
            tt = act.op(activation(rs[:, 0:1024], S[j][:, :], ACT.Ln, bias=EPS), t, *st.get("rs_free", ()))
            slots.readers[j] = (tt,)
            if cx:
                tt = act.op(activation(rs[:, 1024:1280], M[jc][:, 0:256], ACT.Ln, bias=EPS))
                mslot.readers[jc] = (tt,)
            tt = act.op(activation(rs[:, 0:w], rs[:, 0:w], ACT.Exp, scale=-0.5), tt)
            tt = dve.op(scalar_tensor_tensor(dst[:, 0:w], dst[:, 0:w], g, rs[:, 0:w], ALU.mult, ALU.mult), tt, t_qg, st[u])
            st["rs_free"] = (tt,)
            st[u, "n"] = tt
            t_ready[u] = (tt,)

        def stage2(u):
            kind, dst, g, rope = units[u]
            if not rope:
                return
            j, free = slots.take()
            pe.wait(st[u, "n"], *free)
            pm = cst[:, C_PERM:C_PERM + 128]
            pe.run(matmul(S[j][:, 0:512], pm, dst[:, 0:512], start=True, stop=True))
            t = pe.op(matmul(S[j][:, 512:1024], pm, dst[:, 512:1024], start=True, stop=True))
            ta = dve.op(tensor_tensor(rp[:, :], S[j][:, :], cs[:, 1, :], ALU.mult), t, t_cs, *free_rp[0], *free_vt[0])
            slots.readers[j] = (ta,)
            tb = pool.op(tensor_tensor(dst[:, 0:1024], dst[:, 0:1024], cs[:, 0, :], ALU.mult), t, t_cs, st[u, "n"])
            tb = pool.op(tensor_tensor(dst[:, 0:1024], dst[:, 0:1024], rp[:, :], ALU.add), ta, tb)
            free_rp[0] = (tb,)
            t_ready[u] = (tb,)

        nu = len(units)
        for s in range(nu):
            fill = [None] * 8
            if s >= 3:
                fill[0] = lambda: stage2(s - 3)
                if units[s - 3][3]:
                    slots.i += 1
            if s >= 2:
                fill[3] = lambda: stage1(s - 1)
            if s == 2:
                stage1(0)
            stage0(s, fill)
        stage2(nu - 3)
        stage1(nu - 1)
        stage2(nu - 2)
        stage2(nu - 1)

        pp = at("pp", AH, [128, 3, 896], F)
        pt = at("pt", AH + 11 * KB, [128, 2, 2, 7, 128], R)
        qs = at("qs", AH + 25 * KB, [128, 2, 1024], R)
        qx = at("qx", AH + 33 * KB, [128, 1024], R)
        kh = at("kh", AH + 41 * KB, [128, 2, 1280], R)
        kl = at("kl", AH + 51 * KB, [128, 2, 1280], R)
        osq = at("osq", AH + 37 * KB, [128, 512], F)
        ii = at("ii", AH + 39 * KB, [128, 64], F)
        ot = at("ot", AH + 61 * KB, [128, 2, 256], F)
        vh = at("vh", U + 98 * KB, [128, 2, 10, 128], R)
        bt = at("bt", A_RAW, [128, 2, 1472], F)
        cb = at("cb", A_W, [128, 1024], F)
        mr = at("mr", A_W + 4 * KB, [128, 3, 1024], F)
        oa = at("oa", P_CS, [128, 8, 512], F)
        ob = at("ob", P_QA, [128, 8, 512], F)
        p1 = (st[nu - 1], *st["rs_free"], *free_sq[0], *free_vt[0], *free_rp[0])
        t_cb = load(sem("s_cb"), 1, cb[:, :], T["c_row"].to_broadcast([128, 1024]), *p1)
        t_sk = load(sem("s_sk"), 1, snk[:, 0:8], T["sink"].to_broadcast([128, 8]))
        t_cbs = act.op(activation(cb[:, :], cb[:, :], ACT.Silu), t_cb)
        t_snk = act.op(activation(snk[:, 8:16], snk[:, 0:8], ACT.Copy, scale=-1.0), t_sk)
        s_mr = [sem(f"s_mr{i}") for i in range(3)]
        mr_free, t_mods = {}, []

        def mod_load(n):
            if n < 32:
                st["mr", n] = load(s_mr[n % 3], n // 3 + 1, mr[:, n % 3, :], T["w_modT"][16 - NPM + n], *p1,
                                   *mr_free.get(n - 3, ()))

        def mod_col(n):
            r = mr[:, n % 3, :]
            t = pool.op(tensor_tensor(r, r, cb[:, :], ALU.mult), st["mr", n], t_cbs)
            return t

        def mod_half(n, half):
            r, c = slice(512 * half, 512 * half + 512), mv[:, M_RAW + 16 + n:M_RAW + 17 + n]
            t = dve.op(tensor_tensor_reduce(mr[:, n % 3, r], mr[:, n % 3, r], cb[:, r], 1.0, c if half else 0.0,
                       ALU.mult, ALU.add, c), st["mr", n], t_cbs, *st.get("mh", ()))
            st["mh"] = (t,)
            if half:
                mr_free[n] = (t,)
                t_mods.append(t)
                mod_load(n + 3)

        def mod_sum(n, t):
            r = mr[:, n % 3, :]
            t = act.op(activation(r, r, ACT.Copy, accum_out=mv[:, M_RAW + 16 + n:M_RAW + 17 + n]), t)
            mr_free[n] = (t,)
            t_mods.append(t)
            mod_load(n + 3)

        s_bt = [sem("s_bt0"), sem("s_bt1")]
        bt_free, t_bt = {}, {}

        def bias_table(h):
            t_bt[h] = load(s_bt[h % 2], h // 2 + 1, bt[:, h % 2, :], T["bias"][h], *p1, *bt_free.get(h - 2, ()))

        def bias_neg(h):
            t_bt[h] = act.op(activation(bt[:, h % 2, :], bt[:, h % 2, :], ACT.Copy, scale=-1.0), t_bt[h])

        heads = []
        for p in range(4):
            heads += [("a", p, p), ("a", p + 4, p)]
        for p in range(4):
            heads += [("b", 2 * p, p + 4), ("b", 2 * p + 1, p + 4)]
        start = [0, 0, 0, 128, 256, 384, 512, 512]
        size = [512, 512, 576, 576, 576, 576, 512, 512]
        bcol = [6 * 64, 4 * 64, 896, 896, 896, 896, 2 * 64, 0]
        items = []
        for n, (kind, h, p) in enumerate(heads):
            for b in range(8):
                if kind == "a":
                    b0, b1 = max(b - 1, 0), min(b + 1, 7)
                    items.append((n, kind, h, p, b, 128 * b0, 128 * (b1 - b0 + 1)))
                else:
                    items.append((n, kind, h, p, b, start[b], size[b]))

        srd, ptr, pring, ptring = Ring(2), Ring(2), Ring(3), Ring(2)
        srd.readers = [slots.readers[0], slots.readers[1]]
        banks = [S[2][:, 0:512], S[2][:, 512:1024]]
        ptr.readers = [slots.readers[2], slots.readers[2]]
        oring, otr = Ring(2), Ring(2)
        oring.readers = [mslot.readers[0], mslot.readers[1]]
        it = {}
        q_rd, v_rd, t_qk, t_vh = {}, {}, {}, {}

        s_hd = [sem("s_hd0"), sem("s_hd1")]
        n_hd = [0, 0]

        def halves(n):
            return slice(64 * (n % 2), 64 * (n % 2) + 64), slice(64 - 64 * (n % 2), 128 - 64 * (n % 2))

        def prep_head(n):
            kind, h, p = heads[n]
            z = n % 2
            own, other = halves(n)
            src, u = (qa[:, p, :], 10 + p) if p < 4 else (qb[:, p - 4, :], 10 + p)
            free = q_rd.get(z, ())
            first = n < 2
            lo = dve if first else pool

            def hi(dst, src):
                if first:
                    return act.op(activation(dst, src, ACT.Copy), *t_ready[u], *p1, *free)
                return pool.op(tensor_copy(dst, src), *t_ready[u], *p1, *free, (pool.sem, pool.n))

            ta = hi(qs[own, z, :], src[own, :])
            tb = lo.op(tensor_tensor(qx[own, :], src[own, :], qs[own, z, :].bitcast(F), ALU.subtract),
                       ta, *t_ready[u], *p1, *free, (pool.sem, pool.n))
            n_hd[z] += 1
            t = load(s_hd[z], n_hd[z], qs[other, z, :].bitcast(F), qx[own, :].bitcast(F), tb)
            if n < 2 or kind == "b":
                k, u = (ka[:, :], 0) if kind == "a" else (kb[:, p - 4, :], p - 3)
                ta = hi(kh[own, z, :], k[own, :])
                tb = lo.op(tensor_tensor(kl[own, z, :], k[own, :], kh[own, z, :].bitcast(F), ALU.subtract),
                           ta, *t_ready[u], *p1, *free, (pool.sem, pool.n))
                load(s_hd[z], n_hd[z] + 1, kh[other, z, :].bitcast(F), kh[own, z, :].bitcast(F), ta)
                n_hd[z] += 2
                t = load(s_hd[z], n_hd[z], kl[other, z, :].bitcast(F), kl[own, z, :].bitcast(F), tb)
            t_qk[n] = (t, tb)
            if not first:
                pool.wait(tb)

        def keep_warm(n):
            bk, free = ptr.take()
            pe.wait(t_msk, *free)
            for _ in range(n):
                t = pe.op(matmul(banks[bk], idb[:, :], mlb[:, :].unsqueeze(1).to_broadcast([128, 4, 128]), start=True, stop=True))
            ptr.readers[bk] = (t,)

        def prep_v(n):
            z = n % 2
            c = 64 * n if n < 2 else 128 + 64 * (n - 8)
            u = 5 if n < 2 else 6 + (n - 8) // 2
            free = v_rd.get(z, ())
            v = vv[:, :, c:c + 64]
            h_, l_ = vh[:, z, :, 0:64], vh[:, z, :, 64:128]
            if n < 2:
                ta = act.op(activation(h_, v, ACT.Copy), *t_ready[u], *p1, *free)
            else:
                ta = pool.op(tensor_copy(h_, v), *t_ready[u], *p1, *free)
            tb = pool.op(tensor_tensor(l_, v, h_.bitcast(F), ALU.subtract), ta, *t_ready[u], *p1, *free)
            t_vh[z, n >= 8] = (ta, tb)

        def qk(i):
            n, kind, h, p, b, k0, L = items[i]
            s_, free = srd.take()
            D = S[s_]
            z = n % 2
            Q = qs[:, z, 128 * b:128 * b + 128]
            pe.wait(*free)
            if i >= 4:
                join(i - 4, s_)
            pe.wait(*t_qk[n], t_msk)
            w = 256 + L
            parts = [(0, 256, 1024, None)]
            n1 = min(256, L)
            if kind == "a":
                m = (256, mlb) if b > 0 else (384, mrb)
                parts.append((256, 256 + n1, k0, m))
                if L > 256:
                    parts.append((512, w, k0 + 256, (512, mrb)))
            else:
                parts += [(256, 512, k0, None), (512, w, k0 + 256, None)]
            for c0, c1, kc, m in parts:
                for x, K in enumerate((kh, kl)):
                    f = matmul(D[:, c0:c1], Q, K[:, z, kc:kc + c1 - c0], start=x == 0, stop=x == 1 and m is None)
                    if c1 == w and x == 1 and m is None:
                        t = pe.op(f)
                    else:
                        pe.run(f)
                if m is not None:
                    f = matmul(D[:, m[0]:m[0] + 128], idb[:, :], m[1][:, :], start=False, stop=True)
                    if c1 == w:
                        t = pe.op(f)
                    else:
                        pe.run(f)
            q_rd[z] = (t,)
            col = b + 8 * (n % 4)
            nm = nmx[:, col:col + 1]
            old = it.get(("col", col), ())
            it[i, "j"] = (take_out(i - 4, s_, t),) if i >= 4 else ()
            if kind == "a":
                t = dve.op(tensor_reduce(nm, D[:, 0:w], AX, ALU.min), t, *old)
                t = dve.op(tensor_scalar(nm, nm, snk[:, 8 + h:9 + h], None, ALU.min), t, t_snk)
            else:
                bc = bcol[b]
                t = dve.op(tensor_reduce(nm, D[:, 0:256], AX, ALU.min), t, *old)
                t = dve.op(tensor_tensor_reduce(D[:, 256:w], D[:, 256:w], bt[:, h % 2, bc:bc + L], 1.0, nm,
                           ALU.add, ALU.min, nm), t, t_bt[h])
                bt_free[h] = (t,)
            it[i] = (s_, w, t, col, old)

        def ex(i):
            s_, w, t, col, old = it[i]
            D, nm = S[s_], nmx[:, col:col + 1]
            pk, pfree = pring.take()
            t = act.op(activation(pp[:, pk, 0:w], D[:, 0:w], ACT.Exp, bias=nm, scale=-1.0,
                       accum_out=den[:, col:col + 1]), t, *pfree, *old)
            srd.readers[s_] = (t, *it[i, "j"])
            it[i] = (pk, t)

        def tr(i):
            n, kind, h, p, b, k0, L = items[i]
            pk, t = it[i]
            pe.wait(t)
            nt = (256 + L + 127) // 128
            tk, tfree = ptring.take()
            toks = []
            for half in range(2):
                tiles = list(range(4 * half, min(4 * half + 4, nt)))
                if not tiles:
                    continue
                bk, free = ptr.take()
                pe.wait(*free)
                for x in tiles:
                    f = transpose(banks[bk][:, 128 * (x - 4 * half):128 * (x - 4 * half) + 128],
                                  pp[:, pk, 128 * x:128 * x + 128], ID)
                    if x == tiles[-1]:
                        tp = pe.op(f)
                    else:
                        pe.run(f)
                pring.readers[pk] = (tp,)
                src = banks[bk][:, 0:128 * len(tiles)]
                H, Lo = (pt[:, tk, y, 4 * half:4 * half + len(tiles), :].rearrange("p a b -> p (a b)") for y in (0, 1))
                ta = act.op(activation(H, src, ACT.Copy), tp, *tfree)
                tb = dve.op(tensor_tensor(Lo, src, H.bitcast(F), ALU.subtract), tp, ta, *tfree)
                toks += [ta, tb]
                ptr.readers[bk] = (ta, tb)
            it[i, "t"] = (tk, toks, nt)

        def av(i):
            n, kind, h, p, b, k0, L = items[i]
            tk, toks, nt = it[i, "t"]
            ok, free = oring.take()
            pe.wait(*toks, *free, *t_vh[n % 2, kind == "b"])
            tiles = [8, 9] + [k0 // 128 + x for x in range(nt - 2)]
            for x, v in enumerate(tiles):
                f = matmul(M[ok][:, 0:256], vh[:, n % 2, v, :], pt[:, tk, :, x, :], start=x == 0, stop=x == nt - 1)
                if x == nt - 1:
                    t = pe.op(f)
                else:
                    pe.run(f)
            ptring.readers[tk] = (t,)
            v_rd[n % 2] = (t,)
            o_, ofree = otr.take()
            t = act.op(activation(ot[:, o_, :], M[ok][:, 0:256], ACT.Copy), t, *ofree, *p1)
            oring.readers[ok] = (t,)
            it[i, "o"] = (o_, t)

        def join(i, s_):
            o_, t = it[i, "o"]
            pe.wait(t, t_ii)
            pe.run(matmul(S[s_][:, 960:1024], ot[:, o_, 0:128], ii[:, :], start=True, stop=False))
            t = pe.op(matmul(S[s_][:, 960:1024], ot[:, o_, 128:256], ii[:, :], start=False, stop=True))
            otr.readers[o_] = (t,)
            return t

        def take_out(i, s_, t):
            n, kind, h, p, b, k0, L = items[i]
            buf = oa if kind == "a" else ob
            t = dve.op(tensor_copy(buf[:, b, 64 * h:64 * h + 64], S[s_][:, 960:1024]), t, *p1)
            if b % 4 == 3:
                c = 8 * (n % 4) + b - 3
                dst, dc, te = buf[:, b - 3:b + 1, 64 * h:64 * h + 64], den[:, c:c + 4], it[i][1]
                if kind == "a":
                    te = act.op(activation(dsn[:, c:c + 4], nmx[:, c:c + 4], ACT.Exp, bias=snk[:, h:h + 1]), te, t_sk)
                    te = dve.op(tensor_tensor(dc, dc, dsn[:, c:c + 4], ALU.add), te)
                r = dve.op(reciprocal(rdn[:, c:c + 4], dc), te, *it.get(("rdn", c), ()))
                R4 = rdn[:, c:c + 4].unsqueeze(2).to_broadcast([128, 4, 64])
                to = pool.op(tensor_tensor(dst, dst, R4, ALU.mult), t, r)
                it["rdn", c] = (to,)
                for x in range(4):
                    it["col", c + x] = (r,)
                it[kind, "o"] = to
            return t

        def out_square(n, b):
            c = 8 * n + b
            st["osq"] = act.op(activation(osq[:, :], (oa, ob)[n][:, b, :], ACT.Square, accum_out=oss[:, c:c + 1]),
                               it["ab"[n], "o"], *st.get("osq_t", ()), *p1)
            st["osq_t"] = (st["osq"],)

        def out_scale(n, b, eng):
            buf, c = (oa, ob)[n][:, b, :], 8 * n + b
            t_on[n, b] = eng.op(tensor_scalar(buf, buf, ors[:, c:c + 1], None, ALU.mult), st["or", n])

        def out_ln(n):
            o8 = slice(8 * n, 8 * n + 8)
            st["ln", n] = act.op(activation(ors[:, o8], oss[:, o8], ACT.Ln, bias=EPS, scale=1.0 / 512), st["osq"])

        def out_exp(n):
            o8 = slice(8 * n, 8 * n + 8)
            st["or", n] = act.op(activation(ors[:, o8], ors[:, o8], ACT.Exp, scale=-0.5), st["ln", n])

        t_on = {}

        t_ii = dve.op(tensor_tensor(ii[:, :], cst[:, C_ID:C_ID + 64], cst[:, C_ID + 64:C_ID + 128], ALU.add), *p1)
        t_pz = dve.op(memset(pp[:, :, 832:896], 0.0), *p1)
        pe.wait(t_pz)
        bias_table(0)
        bias_table(1)
        for n in range(3):
            mod_load(n)
        prep_head(0)
        prep_head(1)
        prep_v(0)
        prep_v(1)
        NI = len(items)
        keep_warm(60)
        for i in range(NI + 4):
            if i < NI:
                n, kind, h, p, b = items[i][:5]
                if kind == "b" and b == 0:
                    bias_neg(h)
                qk(i)
                if b == 7 and kind == "b" and h + 2 < 8:
                    bias_table(h + 2)
                if b == 1 and 1 <= n < 15:
                    prep_head(n + 1)
                if b == 2 and 7 <= n < 15:
                    prep_v(n + 1)
            if i >= NI:
                z, free = srd.take()
                pe.wait(*free)
                srd.readers[z] = (take_out(i - 4, z, join(i - 4, z)),)
            if 1 <= i < 4:
                keep_warm(8)
            if 1 <= i <= NI:
                tr(i - 1)
            if i < NI:
                ex(i)
            if 2 <= i < NI + 2:
                av(i - 2)
            if i >= 56 and i % 2 and i < 128:
                mod_half(i // 4, i // 2 % 2)
            elif i % 4 == 1 and i < 56:
                t_mc = mod_col(i // 4)
            elif i % 4 == 3 and i < 56:
                mod_sum(i // 4, t_mc)
            if 68 <= i < 76:
                out_square(0, i - 68)
            if i == 76:
                out_ln(0)
                out_exp(0)
            if i % 4 == 3 and 79 <= i < 111:
                out_scale(0, (i - 79) // 4, pool)
            if i == NI - 1:
                raw_gate.extend(bt_free[6] + bt_free[7])
                for _ in range(3):
                    load_slab()
            if i == NI:
                for b in range(4):
                    out_square(1, b)
        for b in range(4, 8):
            out_square(1, b)
        out_ln(1)
        w_gate.extend([t_mods[-1], t_cbs])
        at_slab["hold"] = len(plan)
        split_ahead()
        t = dve.op(tensor_tensor(mv[:, M_MOD + 16:M_MOD + 48], mv[:, M_RAW + 16:M_RAW + 48],
                   vec[:, V_BMOD + 16:V_BMOD + 48], ALU.add), t_mods[-1])
        t_mod = dve.op(scalar_tensor_tensor(mv[:, M_G2:M_G2 + 8], mv[:, M_MOD + 32:M_MOD + 40], 1.0,
                       vec[:, V_N2:V_N2 + 8], ALU.add, ALU.mult), t)

        xt = at("xt", U, [128, 8, 1024], F)
        x2 = at("x2", U + 32 * KB, [128, 1024], F)
        sqt = at("sqt", U + 36 * KB, [128, 2, 1024], F)
        rs2 = at("rs2", U + 44 * KB, [128, 1024], F)
        tt_ = at("tt_", U + 48 * KB, [128, 3, 1024], F)
        s_xt = [sem(f"s_xt{i}") for i in range(8)]
        att_done = (it["b", "o"], (pe.sem, pe.n))
        t_xt = [(load(s_xt[k], 1, xt[:, k, :], T["xT"][k][:, 0:1024], *att_done),) for k in range(8)]
        slots.readers = [srd.readers[0], srd.readers[1], ptr.readers[0] + ptr.readers[1]]
        mslot.readers = [oring.readers[0], oring.readers[1]]

        t_h = [()] * 8

        def turn(k):
            n, f_ = k // 4, k % 4
            buf, g = (oa, ob)[n], vec[:, V_ONA + k:V_ONA + k + 1]
            for half in range(2):
                j, free = mslot.take()
                pe.wait(*free)
                for b in range(4):
                    pe.wait(t_on[n, 4 * half + b])
                    f = transpose(M[j][:, 128 * b:128 * b + 128], buf[:, 4 * half + b, 128 * f_:128 * f_ + 128], ID)
                    if b == 3:
                        t = pe.op(f)
                    else:
                        pe.run(f)
                r = slice(512 * half, 512 * half + 512)
                ta = act.op(activation(hh[:, k, r], M[j][:, :], ACT.Copy, scale=g), t, *att_done, st["osq"])
                tb = dve.op(scalar_tensor_tensor(hl[:, k, r], M[j][:, :], g, hh[:, k, r].bitcast(F),
                            ALU.mult, ALU.subtract), ta, *att_done)
                mslot.readers[j] = (ta, tb)
                t_h[k] += (ta, tb)

        turn(0)
        out_exp(1)
        for b in range(8):
            out_scale(1, b, pool if b % 2 else dve)
        turn(1)
        turn(2)

        sqr = Ring(2)
        x2s = {"tok": (), "free": ()}

        def square(k, tok, X):
            a, free = sqr.take()
            if k == 6:
                act.run(ln_table())
            if k == 7:
                x2s["last"] = a, [act.op(activation(sqt[:, a, r], X[:, k, r], ACT.Square), t, *free,
                                         *x2s.get("ovl", ()))
                                  for r, t in zip((slice(0, 512), slice(512, 1024)), tok)]
                sqr.readers[a] = (x2s["last"][1][1],)
                return
            t = act.op(activation(sqt[:, a, :], X[:, k, :], ACT.Square), *tok, *free, *x2s.get("ovl", ()))
            if k == 0:
                t = pool.op(tensor_copy(x2[:, :], sqt[:, a, :]), t, *x2s["free"])
            else:
                t = pool.op(tensor_tensor(x2[:, :], x2[:, :], sqt[:, a, :], ALU.add), t, *x2s["tok"])
            sqr.readers[a] = (t,)
            x2s["tok"] = (t,)

        def rstd(dst, free_dst=()):
            j, free = slots.take()
            one = cst[:, C_ONE:C_ONE + 128]
            a, t7 = x2s["last"]
            pe.wait(*free, *x2s["tok"])
            for c in (0, 512):
                pe.run(matmul(S[j][:, c:c + 512], one, x2[:, c:c + 512], start=True, stop=False))
            t = [pe.op(matmul(S[j][:, c:c + 512], one, sqt[:, a, c:c + 512], start=False, stop=True), t7[c // 512])
                 for c in (0, 512)]
            x2s["free"] = sqr.readers[a] = (t[1],)
            for i, c in enumerate((0, 512)):
                t[i] = act.op(activation(dst[:, c:c + 512], S[j][:, c:c + 512], ACT.Ln, bias=EPS), t[i], *free_dst)
            slots.readers[j] = (t[1],)
            return act.op(activation(dst[:, :], dst[:, :], ACT.Exp, scale=-0.5), t[1])

        ttr = Ring(3)

        def normed(G, SH, toks):
            t_rs = rstd(rs2)
            out_, ys = [], {}

            def first(k):
                a, free = ttr.take()
                y = tt_[:, a, :]
                t = dve.op(scalar_tensor_tensor(y, xt[:, k, :], G[:, k:k + 1], rs2[:, :], ALU.mult, ALU.mult),
                           t_rs, *toks[k], *free)
                s = None if SH is None else SH[:, k:k + 1]
                if s is not None and k % 2:
                    t = act.op(activation(y, y, ACT.Identity, bias=s), t)
                if s is None or k % 2:
                    ta = act.op(activation(hh[:, k, :], y, ACT.Copy), t)
                else:
                    ta = act.op(activation(hh[:, k, :], y, ACT.Identity, bias=s), t)
                ys[k] = (a, y, s, ta)

            first(0)
            for k in range(8):
                if k < 7:
                    first(k + 1)
                a, y, s, ta = ys[k]
                h = hh[:, k, :].bitcast(F)
                if s is None or k % 2:
                    tb = (pool if k % 2 else dve).op(tensor_tensor(hl[:, k, :], y, h, ALU.subtract), ta)
                else:
                    tb = dve.op(scalar_tensor_tensor(hl[:, k, :], y, s, h, ALU.add, ALU.subtract), ta)
                ttr.readers[a] = (tb,)
                out_.append((ta, tb))
            return out_

        fin = None

        def residual(k, j, t, gate, sq_last):
            ts = []
            for r in ((slice(0, 512), slice(512, 1024)) if sq_last and k == 7 else (slice(0, 1024),)):
                x = xt[:, k, r]
                f = (scalar_tensor_tensor(x, S[j][:, r], gate, x, ALU.mult, ALU.add)) \
                    if gate is not None else (tensor_tensor(x, S[j][:, r], x, ALU.add))
                ts.append(dve.op(f, t, t_mod, *t_xt[k]))
            t = ts[-1]
            slots.readers[j] = (t,)
            t_xt[k] = (t,)
            if sq_last:
                square(k, ts, xt)
                at_slab["late"] = False
                split_ahead()
                if fin is not None and k < 7:
                    t_xt[k] = (act.op(activation(xt[:, k, :], xt[:, k, :], ACT.Copy,
                                                 scale=vec[:, V_FIN + k:V_FIN + k + 1]), (act.sem, act.n), t),)

        x2s["ovl"] = att_done
        x2s["free"] = att_done
        pair = gemm_pair(("out", "out"), (128, 128), hh, hl, t_h,
                         fill=[lambda k=k: turn(k) for k in range(3, 8)] + [lambda: None] * 3)
        for m in range(8):
            at_slab["late"] = m == 7
            j, t = pair[m] if m < 2 else gemm("out", 8, 128, hh, hl, t_h)
            residual(m, j, t, mv[:, M_MOD + 16 + m:M_MOD + 17 + m], True)

        fh = at("fh", U + 60 * KB, [128, 6, 1024], R)
        fl = at("fl", U + 84 * KB, [128, 6, 1024], R)
        sg = at("sg", U + 44 * KB, [128, 2, 1024], F)
        pr = at("pr", U + 52 * KB, [128, 2, 1024], F)
        hid_free = {}
        hid = {}

        def emit_hidden(j_, y, ty, r, ring_k):
            q = j_ % 6
            ta = dve.op(tensor_copy(fh[:, q, :], y), ty, *hid_free.get(j_ - 6, ()))
            tb = pool.op(tensor_tensor(fl[:, q, :], y, fh[:, q, :].bitcast(F), ALU.subtract), ty, ta)
            hid[j_] = (ta, tb)
            return tb

        def down(kind, g, gate, final):
            k0, n = sum(DNG[:g]), DNG[g]
            for m in range(8):
                k_, w_i, wt = next_slab(kind)
                j, free = slots.take()
                pe.wait(*wt, *free)
                for k in range(n):
                    q = (k0 + k) % 6
                    pe.wait(hid[k0 + k][0])
                    for i_, (w, x) in enumerate(((wh, fh), (wl, fh), (wh, fl))):
                        if i_ == 2:
                            pe.wait(hid[k0 + k][1])
                        stt, en = k == 0 and i_ == 0, k == n - 1 and i_ == 2
                        for c in (0, 512):
                            f = (matmul(
                                S[j][:, c:c + 512], w[:, k_, k, :], x[:, q, c:c + 512], start=stt, stop=en))
                            if en and c:
                                t = pe.op(f)
                            else:
                                pe.run(f)
                at_slab["late"] = final and m == 7
                slab_done(w_i, t)
                gt = gate[:, m:m + 1] if gate is not None else None
                residual(m, j, t, gt, final)
            for k in range(n):
                hid_free[k0 + k] = (t,)

        t_h = normed(mv[:, M_G2:M_G2 + 8], mv[:, M_MOD + 24:M_MOD + 32], t_xt)
        sgr, prr = Ring(2), Ring(2)
        sgr.readers = prr.readers = None
        sgr.readers, prr.readers = [all_of(t_h)] * 2, [all_of(t_h)] * 2
        x2s["ovl"] = ()
        for kind, a in ffn_order():
            if kind == "gu":
                if a == 0:
                    (jg, tg), up = gemm_pair(("f1g", "f1u"), (128, 128), hh, hl, t_h)
                else:
                    jg, tg = gemm("f1g", 8, 128, hh, hl, t_h)
                s_, free = sgr.take()
                p_, pfree = prr.take()
                t = act.op(activation(sg[:, s_, :], S[jg][:, :], ACT.Silu), tg, *free)
                slots.readers[jg] = (t,)
                ju, tu = up if a == 0 else gemm("f1u", 8, 128, hh, hl, t_h)
                t = dve.op(tensor_tensor(pr[:, p_, :], sg[:, s_, :], S[ju][:, :], ALU.mult), t, tu, *pfree)
                slots.readers[ju] = (t,)
                sgr.readers[s_] = (t,)
                tb = emit_hidden(a, pr[:, p_, :], t, None, None)
                prr.readers[p_] = (tb,)
            else:
                down("d1", a, mv[:, M_MOD + 40:M_MOD + 48], a == len(DNG) - 1)

        ttr.readers = [prr.readers[0] + prr.readers[1] + sgr.readers[0] + sgr.readers[1]] * 3
        s_sp = sem("s_spill")
        for k in range(8):
            t_sp = load(s_sp, k + 1, T["spill"][k], xt[:, k, :], *t_xt[k])
        act.wait(*ttr.readers[0])
        t_h = normed(vec[:, V_MIX:V_MIX + 8], None, t_xt)
        nd = all_of(t_h)
        vo = at("vo", U, [128, 4, 8, 256], F)
        gq = at("gq", U + 32 * KB, [128, 4, 1024], F)
        gd = at("gd", U + 48 * KB, [128, 8, 512], F)
        gst = at("gst", U + 64 * KB, [128, 8, 256], F)
        gt2 = at("gt2", U + 72 * KB, [128, 2, 1024], F)
        gsq = at("gsq", U + 80 * KB, [128, 2, 1024], F)
        gz = at("gz", U + 88 * KB, [128, 1, 512], F)
        ge = at("ge", U + 90 * KB, [128, 1, 512], F)
        glr = at("glr", U + 92 * KB, [32, 1024], F)
        wg2 = at("wg2", U + 96 * KB, [32, 512], F)
        grs = at("grs", U + 104 * KB, [128, 1024], F)
        go_ = at("go_", U + 88 * KB, [128, 2, 2, 1024], F)
        ffn_done = tuple(hid_free[21])
        t_w2 = load(sem("s_w2"), 1, wg2[0:17, :], T["w_gate2"], *ffn_done)
        t_gl1 = dve.op(memset(glr[:, :], 1.0), *ffn_done)
        (j, t), gv0 = gemm_pair(("gl", "gv"), (16, 128), hh, hl, t_h)
        t_glr = dve.op(tensor_copy(glr[0:16, :], S[j][0:16, :]), t, t_gl1)
        slots.readers[j] = (t_glr,)
        jg, gfree = mslot.take()
        jd, dfree = slots.take()
        slots.held = jd
        Z, Dm = S[jd][:, 0:512], S[jd][:, 512:1024]
        dec = {"z": dfree, "d": dfree, "g": ffn_done, "gd": []}

        def decay_a(i):
            t = pe.op(matmul(Z, glr[0:17, 128 * i:128 * i + 128], wg2[0:17, :], start=True, stop=True),
                      t_glr, t_w2, *dec["z"])
            g = ge[:, 0, :]
            ta = act.op(activation(g, Z, ACT.Abs), t, *dec["g"])
            ta = act.op(activation(g, g, ACT.Exp, scale=-1.0), ta)
            ta = act.op(activation(g, g, ACT.Ln, bias=1.0), ta)
            tb = dve.op(scalar_tensor_tensor(gz[:, 0, :], Z, 0.0, g, ALU.min, ALU.subtract), ta, t, *dec["g"])
            dec["z"] = dec["t"] = (tb,)

        def decay_b(i):
            t = pe.op(matmul(Dm, cst[:, C_SUF:C_SUF + 128], gz[:, 0, :], start=True, stop=True),
                      *dec["t"], *dec["d"], *gfree)
            for h in range(4):
                f = (matmul(M[jg][:, 16 * h + 2 * i:16 * h + 2 * i + 2], gz[:, 0, 128 * h:128 * h + 128],
                     cst[:, C_IND:C_IND + 2], start=True, stop=True))
                if h == 3:
                    tg = pe.op(f)
                else:
                    pe.run(f)
            dec["g"] = (tg,)
            td = act.op(activation(gd[:, i, :], Dm, ACT.Exp), t, *nd)
            dec["d"] = (td,)
            dec["gd"].append(td)

        def decay(i):
            return [None, lambda: decay_a(i), None, None, None, None, lambda: decay_b(i)]

        g2r = Ring(2)
        pend = []
        t_kd, t_v = {}, {}

        def g_fin(u):
            kind, m, a, t = u
            j, free = slots.take()
            pe.wait(t, *free)
            for i in range(8):
                f = transpose(S[j][:, 128 * i:128 * i + 128], gt2[:, a, 128 * i:128 * i + 128], ID)
                if i == 7:
                    t = pe.op(f)
                else:
                    pe.run(f)
            g2r.readers[a] = (t,)
            P3 = S[j][:, :].rearrange("p (a b) -> p a b", b=128)
            if kind == "gk":
                d = gd[:, :, 128 * m:128 * m + 128]
                t = dve.op(tensor_tensor(d, P3, d, ALU.mult), t, dec["gd"][-1])
                t_kd[m] = t
            else:
                h, c = m // 2, 128 * (m % 2)
                t = act.op(activation(vo[:, h, :, c:c + 128], P3, ACT.Copy), t, t_sp, *nd)
                t_v[m] = t
            slots.readers[j] = (t,)

        for n in range(12):
            kind, m = ("gv", n) if n < 8 else ("gk", n - 8)
            j, t = gv0 if n == 0 else gemm(kind, 8, 128, hh, hl, t_h, fill=decay(n - 1) if n < 9 else ())
            a, free = g2r.take()
            t = dve.op(tensor_copy(gt2[:, a, :], S[j][:, :]), t, *free, *ffn_done)
            slots.readers[j] = (t,)
            pend.append((kind, m, a, t))
            if n == 8:
                t_ege = act.op(activation(ege[:, :, :].rearrange("p a b -> p (a b)"), M[jg][:, 0:64], ACT.Exp), *dec["g"])
                mslot.readers[jg] = (t_ege,)
                slots.readers[jd] = (*dec["z"], *dec["d"])
                slots.held = None
            if len(pend) > 1:
                g_fin(pend.pop(0))

        kvr = Ring(2)
        kvr.readers = [mslot.readers[0], mslot.readers[1]]
        stv = Ring(8)
        free_go, free_gsq, free_grs = [dec["g"] + dec["z"]] * 2, [ffn_done], [ffn_done]
        lag, t_q, t_half, t_gn = [], {}, {}, {}

        def kv(h, c):
            b, free = kvr.take()
            pe.wait(*free, t_kd[h], t_v[2 * h], t_v[2 * h + 1])
            p0, i = 64 * (c % 2), c // 2
            t = pe.op(matmul(M[b][:, 0:256], gd[p0:p0 + 64, i, 128 * h:128 * h + 128], vo[p0:p0 + 64, h, i, :],
                      start=True, stop=True))
            s, sfree = stv.take()
            if c == 0:
                t = dve.op(tensor_copy(gst[:, s, :], M[b][:, 0:256]), t, *sfree, *ffn_done)
            else:
                q = (s - 1) % 8
                t = dve.op(scalar_tensor_tensor(gst[:, s, :], gst[:, q, :], ege[:, h, c:c + 1], M[b][:, 0:256],
                           ALU.mult, ALU.add), t, t_ege, *sfree, st["gs"])
            st["gs"] = t
            kvr.readers[b] = (t,)
            lag.append((h, c, s, t))

        def oo():
            h, c, s, t = lag.pop(0)
            if c % 8 == 0:
                st["o"], free = slots.take()
                pe.wait(*free)
            j = st["o"]
            pe.wait(t, t_q[h])
            for d in range(2):
                x = 512 * d + 64 * (c % 8)
                f = (matmul(S[j][:, x:x + 64], gst[:, s, 128 * d:128 * d + 128],
                     gq[:, h, 64 * c:64 * c + 64], start=True, stop=True))
                if d:
                    t = pe.op(f)
                else:
                    pe.run(f)
            stv.readers[s] = (t,)
            if c % 8 == 7:
                x = c // 8
                t = act.op(activation(go_[:, h % 2, :, 512 * x:512 * x + 512], S[j][:, :].rearrange("p (a b) -> p a b", b=512),
                           ACT.Copy), t, *free_go[h % 2])
                slots.readers[j] = (t,)
                if c == 15:
                    head_squares(h, t)

        def scan_step(h, c):
            kv(h, c)
            if len(lag) > 2:
                oo()

        def head_squares(h, t):
            for d in range(2):
                ta = act.op(activation(gsq[:, d, :], go_[:, h % 2, d, :], ACT.Square), t, *free_gsq[0])
            st["hs"] = pool.op(tensor_tensor(gsq[:, 0, :], gsq[:, 0, :], gsq[:, 1, :], ALU.add), ta)

        def head_norm(h):
            j, free = slots.take()
            pe.wait(*free, st["hs"])
            pe.run(matmul(S[j][:, 0:512], cst[:, C_DV:C_DV + 128], gsq[:, 0, 0:512], start=True, stop=True))
            t = pe.op(matmul(S[j][:, 512:1024], cst[:, C_DV:C_DV + 128], gsq[:, 0, 512:1024], start=True, stop=True))
            free_gsq[0] = (t,)
            t = act.op(activation(grs[:, :], S[j][:, :], ACT.Ln, bias=EPS), t, *free_grs[0])
            slots.readers[j] = (t,)
            t = act.op(activation(grs[:, :], grs[:, :], ACT.Exp, scale=-0.5), t)
            O = vo[:, h, :, :].rearrange("p a b -> p (a b)")
            for d in range(2):
                g = vec[:, V_GLN + 2 * h + d:V_GLN + 2 * h + d + 1]
                tn = dve.op(scalar_tensor_tensor(O[:, 1024 * d:1024 * d + 1024], go_[:, h % 2, d, :], g, grs[:, :],
                            ALU.mult, ALU.mult), t)
                t_gn[2 * h + d] = tn
            free_grs[0] = free_go[h % 2] = (tn,)

        def scan_fill(x):
            if not 0 <= x <= 9:
                return ()
            h, half = x // 2, x % 2
            steps = [lambda c=c: scan_step(h, 8 * half + c) for c in range(8)] if x < 8 else \
                [lambda: (oo() if lag else None)] * 3 + [None] * 5
            if half == 1 and h > 0:
                inner = steps[3]
                steps[3] = lambda: ((inner() if inner else None), head_norm(h - 1))
            return steps

        for m in range(4):
            j, t = gemm("gq", 8, 128, hh, hl, t_h, fill=scan_fill(m - 1))
            t = act.op(activation(gq[:, m, :], S[j][:, :], ACT.Copy, scale=float(128 ** -0.5)), t, *nd)
            slots.readers[j] = (t,)
            t_q[m] = t
            if pend:
                g_fin(pend.pop(0))

        t_o, read, t_go = [], [], []

        def form(m):
            Od, t = t_o[m]
            ta = act.op(activation(hh[:, m, :], Od, ACT.Copy), t, read[m])
            tb = (pool if m % 2 else dve).op(tensor_tensor(hl[:, m, :], Od, hh[:, m, :].bitcast(F), ALU.subtract),
                                             t, ta, read[m])
            t_go.append((ta, tb))

        for m in range(8):
            fill = scan_fill(m + 3) if m < 7 else [lambda k=k: form(k) for k in range(7)]
            at_slab["late"] = True
            j, t = gemm("gr", 8, 128, hh, hl, t_h, fill=fill, done=read if m == 7 else None)
            a, free = g2r.take()
            t = act.op(activation(gt2[:, a, :], S[j][:, :], ACT.Silu), t, *free)
            slots.readers[j] = (t,)
            at_slab["late"] = False
            split_ahead()
            Od = vo[:, m // 2, :, :].rearrange("p a b -> p (a b)")[:, 1024 * (m % 2):1024 * (m % 2) + 1024]
            t = dve.op(tensor_tensor(Od, Od, gt2[:, a, :], ALU.mult), t, t_gn[m])
            g2r.readers[a] = (t,)
            t_o.append((Od, t))
        form(7)
        t_h = t_go
        t_xt = []
        for k in range(8):
            t_xt.append((load(s_xt[k], 2, xt[:, k, :], T["spill"][k], *t_h[k], t_sp),))
        x2s["ovl"] = ((pe.sem, pe.n),)
        x2s["free"] += x2s["ovl"]
        pair = gemm_pair(("go", "go"), (128, 128), hh, hl, t_h)
        for m in range(8):
            at_slab["late"] = m == 7
            j, t = pair[m] if m < 2 else gemm("go", 8, 128, hh, hl, t_h)
            residual(m, j, t, None, True)
        ttr.readers = [all_of(t_h)] * 3
        t_h = normed(vec[:, V_FFN:V_FFN + 8], None, t_xt)

        ub = at("ub", U + 40 * KB, [128, 2, 1026], F)
        tg_ = at("tg_", U + 49 * KB, [128, 1, 1024], F)
        tv_ = at("tv_", U + 53 * KB, [128, 1, 1024], F)
        t = tuple(x2s["free"]) + all_of(t_h)
        sqr = Ring(1)
        sqr.readers = [x2s["tok"] + x2s["free"]]
        t_z = [dve.op(memset(ub[:, i, 0:2], 0.0), *t, *x2s["tok"]) for i in range(2)]
        ubr = Ring(2)
        ubr.readers = [(t_z[1],), (t_z[1],)]
        tring = {0: all_of(t_h), 1: all_of(t_h)}
        hid_free = {}

        def conv(j, t, buf, which, n):
            a, free = ubr.take()
            x = buf[:, 0, :]
            t0 = act.op(activation(ub[:, a, 2:1026], S[j][:, :], ACT.Copy), t, *free)
            w = [vec[:, V_CW + 44 * i + n:V_CW + 44 * i + n + 1] for i in range(3)]
            t1 = act.op(activation(x, S[j][:, :], ACT.Identity, scale=w[2], bias=vec[:, V_CB + n:V_CB + n + 1]),
                        *tring[which])
            slots.readers[j] = (t1,)
            t2 = dve.op(scalar_tensor_tensor(x, ub[:, a, 1:1025], w[1], x, ALU.mult, ALU.add), t0, t1)
            t3 = dve.op(scalar_tensor_tensor(x, ub[:, a, 0:1024], w[0], x, ALU.mult, ALU.add), t2)
            ubr.readers[a] = (t3,)
            return t3

        fin = []
        for kind, a in ffn_order():
            if kind == "gu":
                if a == 0:
                    (jg, tg), up = gemm_pair(("f2g", "f2u"), (128, 128), hh, hl, t_h)
                else:
                    jg, tg = gemm("f2g", 8, 128, hh, hl, t_h)
                t = conv(jg, tg, tg_, 0, a)
                ts = act.op(activation(tg_[:, 0, :], tg_[:, 0, :], ACT.Silu), t)
                ju, tu = up if a == 0 else gemm("f2u", 8, 128, hh, hl, t_h)
                t = conv(ju, tu, tv_, 1, 22 + a)
                t = dve.op(tensor_tensor(tv_[:, 0, :], tv_[:, 0, :], tg_[:, 0, :], ALU.mult), t, ts)
                tring[0] = (t,)
                tb = emit_hidden(a, tv_[:, 0, :], t, None, None)
                tring[1] = (tb,)
            else:
                down("d2", a, None, a == len(DNG) - 1)

        rs3 = at("rs3", U + 92 * KB, [128, 1024], F)
        t = rstd(rs3)
        s_out = sem("s_out")
        for k in (7, 2, 0, 5, 1, 3, 6, 4):
            x = xt[:, k, :]
            if k == 7:
                ta = dve.op(scalar_tensor_tensor(x, x, vec[:, V_FIN + 7:V_FIN + 8], rs3[:, :], ALU.mult, ALU.mult),
                            t, *t_xt[k])
            else:
                ta = (pool if k in (2, 5, 6) else dve).op(tensor_tensor(x, x, rs3[:, :], ALU.mult), t, *t_xt[k])
            fin.append((k, ta))
        for k, ta in fin:
            t_out = load(s_out, fin.index((k, ta)) + 1, out[k], xt[:, k, :], ta)
        sp.wait(t_out)
        assert at_slab["i"] == len(plan), (at_slab, len(plan))

        block = ctx.enter_context(nc.Block())

        @block.tensor
        def _(e):
            for f in pe.items:
                f(e)

        @block.scalar
        def _(e):
            for f in act.items:
                f(e)

        @block.vector
        def _(e):
            for f in dve.items:
                f(e)

        @block.gpsimd
        def _(e):
            for f in pool.items:
                f(e)

        @block.sync
        def _(e):
            for f in sp.items:
                f(e)


def constants():
    f = np.float32
    c = np.zeros((128, C_N), f)
    i = np.arange(128)
    c[:, C_ID:C_ID + 128] = np.eye(128, dtype=f)
    c[:, C_ONE:C_ONE + 128] = 1.0 / 1024
    c[:, C_BLK:C_BLK + 128] = (i[:, None] // 64 == i[None] // 64) / 64.0
    c[:, C_PERM:C_PERM + 128] = i[:, None] == (i[None] ^ 16)
    c[:, C_SUF:C_SUF + 128] = ((i[:, None] > i[None]) & (i[:, None] // 64 == i[None] // 64)) / 16.0
    c[:, C_DV:C_DV + 128] = 1.0 / 256
    c[:, C_ML:C_ML + 128] = np.where(i[None] < i[:, None], BIG, 0)
    c[:, C_MR:C_MR + 128] = np.where(i[None] > i[:, None], BIG, 0)
    c[:, C_IND:C_IND + 2] = (i[:, None] // 64 == np.arange(2)[None]) / 16.0
    c[:, C_EPS] = 1e-6
    inv = (f(1.0) / (f(10000.0) ** (np.arange(16, dtype=f) / f(16)))).astype(f)
    t = np.arange(1024)
    d = i % 64
    pos = np.where((d < 32)[:, None], t[None] // 64, t[None] % 64).astype(f)
    ang = (pos * inv[d % 16][:, None]).astype(f)
    sign = np.where(d % 32 < 16, -1.0, 1.0).astype(f)
    cs = np.stack([np.cos(ang), np.sin(ang) * sign[:, None]], 1).astype(f)
    return c, np.ascontiguousarray(cs)


def bias_index():
    dr = np.zeros((128, 23, 64), int)
    dc = np.zeros((128, 23, 64), int)
    ok = np.zeros((128, 23, 64), bool)
    q = np.arange(128)
    qr, qc = q // 64, q % 64
    kc = np.arange(64)
    c0 = np.clip(qc - 8, 0, 48)
    col_ok = (kc[None] >= c0[:, None]) & (kc[None] < c0[:, None] + 16)
    es = list(range(1, 15)) + list(range(3, 12))
    for s, e in enumerate(es):
        dr[:, s, :] = np.clip(e - qr, 0, 14)[:, None]
        dc[:, s, :] = np.clip(kc[None] - qc[:, None] + 15, 0, 30)
        row = np.ones(128, bool)
        if s >= 14 and e == 3:
            row = qr == 0
        if s >= 14 and e == 11:
            row = qr == 1
        ok[:, s, :] = col_ok & row[:, None]
    return dr.reshape(128, -1), dc.reshape(128, -1), ok.reshape(128, -1)


def cols(v):
    return np.ascontiguousarray(v).reshape(-1, 128).T


def slabs(w):
    k, m = w.shape
    return np.ascontiguousarray(w.reshape(k // 128, 128, m // 128, 128).transpose(2, 1, 0, 3)).reshape(m // 128, 128, k)


def layout(i):
    f = np.float32
    A = {}
    cst, cs = constants()
    A["cst"], A["cs"] = cst, cs
    v = np.zeros((128, V_N), f)
    v[:, V_BMOD:V_BMOD + 48] = cols(i["b_mod"][0])
    v[:, V_N1:V_N1 + 8] = cols(i["norm1_g"][0])
    for c, n in ((V_QA, "qn_a"), (V_KA, "kn_a"), (V_QB, "qn_b"), (V_KB, "kn_b")):
        v[:, c] = np.concatenate([i[n][0], i[n][0]])
    v[:, V_ONA:V_ONA + 4] = cols(i["on_a"][0])
    v[:, V_ONB:V_ONB + 4] = cols(i["on_b"][0])
    v[:, V_N2:V_N2 + 8] = cols(i["norm2_g"][0])
    v[:, V_MIX:V_MIX + 8] = cols(i["mix_norm_w_2"][0])
    v[:, V_FFN:V_FFN + 8] = cols(i["ffn_norm_w_2"][0])
    v[:, V_FIN:V_FIN + 8] = cols(i["final_norm_w_2"])
    v[:, V_GLN:V_GLN + 8] = cols(i["gla_norm_w_2"][0])
    for t in range(3):
        v[:, V_CW + 44 * t:V_CW + 44 * t + 44] = cols(i["ffn_conv_w_2"][0, t])
    v[:, V_CB:V_CB + 44] = cols(i["ffn_conv_b_2"][0])
    A["vec"] = v
    cc = np.stack([cols(i["c"][0]), cols(i["c_ctx"])], 2)
    A["cc"] = np.ascontiguousarray(cc).reshape(128, 16)
    A["c_row"] = np.ascontiguousarray(i["c"])
    A["cx_row"] = np.ascontiguousarray(i["c_ctx"]).reshape(1, 1024)
    A["sink"] = np.ascontiguousarray(i["sink_a"])
    x = np.concatenate([i["x"][0], i["ctx"][0]], 0)
    A["xT"] = np.ascontiguousarray(x.T).reshape(8, 128, 1280)
    w = i["w_mod"][0]
    A["w_mod0"] = slabs(w[:, :128 * NPM])
    A["w_modT"] = np.ascontiguousarray(w[:, 128 * NPM:].T).reshape(48 - NPM, 128, 1024)
    w = i["w_in"][0]
    qa, ka, va, qb, kb, vb = np.split(w, np.cumsum([512, 128, 128, 512, 512]), axis=1)
    order = np.concatenate([np.concatenate([np.arange(64) + 64 * j, np.arange(64) + 64 * (j + 4)]) for j in range(4)])
    A["w_in"] = slabs(np.concatenate([ka, kb, va, vb, qa[:, order], qb], 1))
    A["w_out"] = slabs(i["w_out"][0])
    A["w_f1g"] = slabs(i["w_gate"][0])
    A["w_f1u"] = slabs(i["w_up"][0])
    A["w_d1"] = slabs(i["w_down"][0])
    dr, dc, ok = bias_index()
    A["bias"] = np.where(ok[None], i["rpb_b"][0][:, dr, dc], f(-BIG)).astype(f)
    g = i["gla_w_in_2"][0]
    q, k, vv, r, gl = np.split(g, np.cumsum([512, 512, 1024, 1024]), axis=1)
    A["w_gq"], A["w_gk"], A["w_gv"], A["w_gr"] = slabs(q), slabs(k), slabs(vv), slabs(r)
    glp = np.zeros((1024, 128), f)
    glp[:, :16] = gl
    A["w_gl"] = slabs(glp)
    A["w_gate2"] = np.concatenate([i["gla_w_gate2_2"][0], i["gla_b_gate_2"]], 0)
    A["w_go"] = slabs(i["gla_w_out_2"][0])
    u = i["ffn_w_up_2"][0]
    A["w_f2g"], A["w_f2u"] = slabs(u[:, :2816]), slabs(u[:, 2816:])
    A["w_d2"] = slabs(i["ffn_w_down_2"][0])
    return A


def kernel(**inputs):
    import concourse.bacc as _bacc
    from concourse.bass_utils import run_bass_kernel_spmd as _run

    arrays = layout({k: np.asarray(v) for k, v in inputs.items()})
    nc = _bacc.Bacc("TRN2", target_bir_lowering=False, num_devices=1)
    T = {}
    for name, a in arrays.items():
        T[name] = nc.dram_tensor(f"in_{name}", a.shape, mybir.dt.from_np(a.dtype), kind="ExternalInput").ap()
    T["spill"] = nc.dram_tensor("spill", (8, 128, 1024), F).ap()
    out = nc.dram_tensor("out_0", (8, 128, 1024), F, kind="ExternalOutput").ap()
    build(nc, T, out)
    r = _run(nc, [{f"in_{n}": a for n, a in arrays.items()}], core_ids=[0])
    got = r.results[0]["out_0"]
    return np.ascontiguousarray(got.reshape(1024, 1024).T).reshape(1, 1024, 1024)
```
